# Optimizing a Trainium2 kernel written in Bass

```python
import jax, jax.numpy as jnp
from jax import lax
import numpy as np

D_MODEL = 2048
BATCH = 1
SEQ = 128
DEPTH = 2
DEC_BATCH = 1
DEC_SEQ = 256
PAST_LEN = 128

GRID_W = 64
HEAD_DIM = 128
A_HEADS = D_MODEL // (2 * HEAD_DIM)
A_KV_HEADS = A_HEADS // 4
A_GROUPS = A_HEADS // A_KV_HEADS
A_WINDOW = 128
A_BLOCK = 128
B_HEADS = D_MODEL // (2 * HEAD_DIM)
NB_KH = 8
NB_KW = 16
A_WIDTH = A_HEADS * HEAD_DIM
A_KV_WIDTH = A_KV_HEADS * HEAD_DIM
B_WIDTH = B_HEADS * HEAD_DIM
ATTN_WIDTH = A_WIDTH + B_WIDTH
ATTN_SPLITS = (A_WIDTH, A_WIDTH + A_KV_WIDTH, A_WIDTH + 2 * A_KV_WIDTH,
               A_WIDTH + 2 * A_KV_WIDTH + B_WIDTH, A_WIDTH + 2 * A_KV_WIDTH + 2 * B_WIDTH,
               A_WIDTH + 2 * A_KV_WIDTH + 3 * B_WIDTH)
ATTN_IN = A_WIDTH + 2 * A_KV_WIDTH + 3 * B_WIDTH + ATTN_WIDTH
CONV_WIDTH = D_MODEL
CONV_K = 31
N_ATTN_LAYERS = (DEPTH + 1) // 2
N_CONV_LAYERS = DEPTH // 2
CTX_QBLOCK = 128
ROPE_BASE = 10000.0
EPS = 1e-6

kernel_name = "hybrid_flow_prefix_trunk_step"

def rms_norm(x, g):
    xf = x.astype(jnp.float32)
    y = xf * lax.rsqrt(jnp.mean(xf * xf, axis=-1, keepdims=True) + EPS)
    return (y * g.astype(jnp.float32)).astype(x.dtype)

def layer_norm(x, g, b):
    xf = x.astype(jnp.float32)
    mu = jnp.mean(xf, axis=-1, keepdims=True)
    xc = xf - mu
    var = jnp.mean(xc * xc, axis=-1, keepdims=True)
    return (xc * lax.rsqrt(var + EPS) * g.astype(jnp.float32) + b.astype(jnp.float32)).astype(x.dtype)

def modulation(cond, w, b):
    m = (jax.nn.silu(cond) @ w + b)[:, None, :]
    return jnp.split(m, 3, axis=-1)

def axial_rope_tables(length, dtype):
    t = jnp.arange(length)
    row = (t // GRID_W).astype(jnp.float32)
    col = (t % GRID_W).astype(jnp.float32)
    n_freq = HEAD_DIM // 4
    inv = ROPE_BASE ** (-jnp.arange(n_freq, dtype=jnp.float32) / n_freq)
    ang_r = row[:, None] * inv[None, :]
    ang_c = col[:, None] * inv[None, :]
    ang = jnp.concatenate([ang_r, ang_r, ang_c, ang_c], axis=-1)
    return jnp.cos(ang).astype(dtype), jnp.sin(ang).astype(dtype)

def apply_rope(x, cos, sin):
    x1r, x2r, x1c, x2c = jnp.split(x, 4, axis=-1)
    rot = jnp.concatenate([-x2r, x1r, -x2c, x1c], axis=-1)
    return x * cos[None, :, None, :] + rot * sin[None, :, None, :]

def softmax_with_sink(s, sink):
    m = jnp.maximum(jnp.max(s, axis=-1, keepdims=True), sink)
    p = jnp.exp(s - m)
    return p / (jnp.sum(p, axis=-1, keepdims=True) + jnp.exp(sink - m))

def context_attention(q, k, v, sink):
    bn, lc, kvh, grp, hd = q.shape
    nq = lc // CTX_QBLOCK
    qb = jnp.moveaxis(q.reshape(bn, nq, CTX_QBLOCK, kvh, grp, hd), 1, 0)
    scale = HEAD_DIM ** -0.5

    def block(qq):
        s = jnp.einsum('bqkgd,bskd->bkgqs', qq, k, preferred_element_type=jnp.float32) * scale
        if sink is None:
            p = jax.nn.softmax(s, axis=-1)
        else:
            p = softmax_with_sink(s, sink.astype(jnp.float32)[None, :, :, None, None])
        return jnp.einsum('bkgqs,bskd->bqkgd', p.astype(v.dtype), v)

    o = lax.map(block, qb)
    return jnp.moveaxis(o, 0, 1).reshape(bn, lc, kvh * grp * hd)

def windowed_gqa_sink(q, k, v, k_ctx, v_ctx, sink):
    bn, length, _, hd = q.shape
    nb = length // A_BLOCK
    scale = HEAD_DIM ** -0.5
    qb = q.reshape(bn, nb, A_BLOCK, A_KV_HEADS, A_GROUPS, hd)

    def band(t):
        tp = jnp.pad(t, ((0, 0), (A_BLOCK, A_BLOCK), (0, 0), (0, 0)))
        tp = tp.reshape(bn, nb + 2, A_BLOCK, A_KV_HEADS, hd)
        return jnp.concatenate([tp[:, :-2], tp[:, 1:-1], tp[:, 2:]], axis=2)

    kw, vw = band(k), band(v)
    blk = jnp.arange(nb)[:, None, None]
    q_pos = blk * A_BLOCK + jnp.arange(A_BLOCK)[None, :, None]
    k_pos = blk * A_BLOCK - A_BLOCK + jnp.arange(3 * A_BLOCK)[None, None, :]
    mask = (jnp.abs(k_pos - q_pos) <= A_WINDOW) & (k_pos >= 0) & (k_pos < length)
    s_loc = jnp.einsum('bnqkgd,bnskd->bnkgqs', qb, kw, preferred_element_type=jnp.float32) * scale
    s_loc = jnp.where(mask[None, :, None, None], s_loc, -jnp.inf)
    s_ctx = jnp.einsum('bnqkgd,bskd->bnkgqs', qb, k_ctx, preferred_element_type=jnp.float32) * scale
    sink_b = sink.astype(jnp.float32).reshape(A_KV_HEADS, A_GROUPS)[None, None, :, :, None, None]
    p = softmax_with_sink(jnp.concatenate([s_loc, s_ctx], axis=-1), sink_b).astype(v.dtype)
    n_loc = 3 * A_BLOCK
    o = (jnp.einsum('bnkgqs,bnskd->bnqkgd', p[..., :n_loc], vw)
         + jnp.einsum('bnkgqs,bskd->bnqkgd', p[..., n_loc:], v_ctx))
    return o.reshape(bn, length, A_WIDTH)

def neighbourhood_attention(q, k, v, k_ctx, v_ctx, rpb):
    bn, length, nh, hd = q.shape
    rows = length // GRID_W
    wr = min(NB_KH, rows)
    scale = HEAD_DIM ** -0.5
    qg = jnp.moveaxis(q.reshape(bn, rows, GRID_W, nh, hd), 1, 0)
    kg = k.reshape(bn, rows, GRID_W, nh, hd)
    vg = v.reshape(bn, rows, GRID_W, nh, hd)
    cols = jnp.arange(GRID_W)
    col_start = jnp.clip(cols - NB_KW // 2, 0, GRID_W - NB_KW)
    col_ok = (cols[None, :] >= col_start[:, None]) & (cols[None, :] < col_start[:, None] + NB_KW)
    col_idx = jnp.clip(cols[None, :] - cols[:, None] + NB_KW - 1, 0, 2 * NB_KW - 2)
    col_mask = jnp.broadcast_to(col_ok[:, None, :], (GRID_W, wr, GRID_W)).reshape(GRID_W, wr * GRID_W)
    n_loc = wr * GRID_W

    def row_block(args):
        r, q_r = args
        r_start = jnp.clip(r - NB_KH // 2, 0, rows - wr)
        k_r = lax.dynamic_slice_in_dim(kg, r_start, wr, axis=1).reshape(bn, n_loc, nh, hd)
        v_r = lax.dynamic_slice_in_dim(vg, r_start, wr, axis=1).reshape(bn, n_loc, nh, hd)
        row_idx = r_start + jnp.arange(wr) - r + NB_KH - 1
        bias = rpb[:, row_idx[None, :, None], col_idx[:, None, :]]
        bias = bias.reshape(nh, GRID_W, n_loc).astype(jnp.float32)
        s_loc = jnp.einsum('bqhd,bshd->bhqs', q_r, k_r, preferred_element_type=jnp.float32) * scale + bias[None]
        s_loc = jnp.where(col_mask[None, None], s_loc, -jnp.inf)
        s_ctx = jnp.einsum('bqhd,bshd->bhqs', q_r, k_ctx, preferred_element_type=jnp.float32) * scale
        p = jax.nn.softmax(jnp.concatenate([s_loc, s_ctx], axis=-1), axis=-1).astype(v.dtype)
        return (jnp.einsum('bhqs,bshd->bqhd', p[..., :n_loc], v_r)
                + jnp.einsum('bhqs,bshd->bqhd', p[..., n_loc:], v_ctx))

    o = lax.map(row_block, (jnp.arange(rows), qg))
    return jnp.moveaxis(o, 0, 1).reshape(bn, length, nh * hd)

def attn_mixer_context(h, w_in, w_out, sink):
    bn, lc, _ = h.shape
    qa, ka, va, qb, kb, vb, z = jnp.split(h @ w_in, ATTN_SPLITS, axis=-1)
    ka = ka.reshape(bn, lc, A_KV_HEADS, HEAD_DIM)
    va = va.reshape(bn, lc, A_KV_HEADS, HEAD_DIM)
    kb = kb.reshape(bn, lc, B_HEADS, HEAD_DIM)
    vb = vb.reshape(bn, lc, B_HEADS, HEAD_DIM)
    oa = context_attention(qa.reshape(bn, lc, A_KV_HEADS, A_GROUPS, HEAD_DIM), ka, va,
                           sink.reshape(A_KV_HEADS, A_GROUPS))
    ob = context_attention(qb.reshape(bn, lc, B_HEADS, 1, HEAD_DIM), kb, vb, None)
    y = jnp.concatenate([oa, ob], axis=-1) * jax.nn.silu(z)
    return y @ w_out, ka, va, kb, vb

def attn_mixer_latent(h, k_ctx_a, v_ctx_a, k_ctx_b, v_ctx_b, w_in, w_out, sink, rpb, cos, sin):
    bn, length, _ = h.shape
    qa, ka, va, qb, kb, vb, z = jnp.split(h @ w_in, ATTN_SPLITS, axis=-1)
    qa = apply_rope(qa.reshape(bn, length, A_HEADS, HEAD_DIM), cos, sin)
    ka = apply_rope(ka.reshape(bn, length, A_KV_HEADS, HEAD_DIM), cos, sin)
    va = va.reshape(bn, length, A_KV_HEADS, HEAD_DIM)
    oa = windowed_gqa_sink(qa, ka, va, k_ctx_a, v_ctx_a, sink)
    ob = neighbourhood_attention(qb.reshape(bn, length, B_HEADS, HEAD_DIM),
                                 kb.reshape(bn, length, B_HEADS, HEAD_DIM),
                                 vb.reshape(bn, length, B_HEADS, HEAD_DIM), k_ctx_b, v_ctx_b, rpb)
    y = jnp.concatenate([oa, ob], axis=-1) * jax.nn.silu(z)
    return y @ w_out

def conv_mixer(h, w_in, dw, dw_b, ln_g, ln_b, w_out):
    a, g, z = jnp.split(h @ w_in, 3, axis=-1)
    u = a * jax.nn.sigmoid(g)
    u = lax.conv_general_dilated(u, dw[:, None, :], window_strides=(1,),
                                 padding=[(CONV_K // 2, CONV_K // 2)],
                                 dimension_numbers=('NWC', 'WIO', 'NWC'),
                                 feature_group_count=CONV_WIDTH) + dw_b
    y = jax.nn.silu(layer_norm(u, ln_g, ln_b)) * jax.nn.silu(z)
    return y @ w_out

def setup_inputs(seed: int = 0) -> dict:
    key = jax.random.key(seed)
    ks = jax.random.split(key, 22)

    def nrm(k, shape, s):
        return jax.random.normal(k, shape, jnp.float32) * s

    return {
        "x_prompt": nrm(ks[0], (BATCH, SEQ, D_MODEL), 1.0),
        "x_sample": nrm(ks[1], (DEC_BATCH, DEC_SEQ, D_MODEL), 1.0),
        "cache_a_k": nrm(ks[2], (DEC_BATCH, N_ATTN_LAYERS, PAST_LEN, A_KV_HEADS, HEAD_DIM), 1.0),
        "cache_a_v": nrm(ks[3], (DEC_BATCH, N_ATTN_LAYERS, PAST_LEN, A_KV_HEADS, HEAD_DIM), 1.0),
        "cache_b_k": nrm(ks[4], (DEC_BATCH, N_ATTN_LAYERS, PAST_LEN, B_HEADS, HEAD_DIM), 1.0),
        "cache_b_v": nrm(ks[5], (DEC_BATCH, N_ATTN_LAYERS, PAST_LEN, B_HEADS, HEAD_DIM), 1.0),
        "c": nrm(ks[6], (DEC_BATCH, D_MODEL), 1.0),
        "c_ctx": nrm(ks[7], (D_MODEL,), 1.0),
        "ada_w": nrm(ks[8], (DEPTH, D_MODEL, 3 * D_MODEL), 0.5 * D_MODEL ** -0.5),
        "ada_b": nrm(ks[9], (DEPTH, 3 * D_MODEL), 0.02),
        "norm_g": 1.0 + nrm(ks[10], (DEPTH, D_MODEL), 0.05),
        "attn_w_in": nrm(ks[11], (N_ATTN_LAYERS, D_MODEL, ATTN_IN), D_MODEL ** -0.5),
        "attn_w_out": nrm(ks[12], (N_ATTN_LAYERS, ATTN_WIDTH, D_MODEL), ATTN_WIDTH ** -0.5),
        "a_sink": nrm(ks[13], (N_ATTN_LAYERS, A_HEADS), 0.5),
        "b_rpb": nrm(ks[14], (N_ATTN_LAYERS, B_HEADS, 2 * NB_KH - 1, 2 * NB_KW - 1), 0.5),
        "conv_w_in": nrm(ks[15], (N_CONV_LAYERS, D_MODEL, 3 * CONV_WIDTH), D_MODEL ** -0.5),
        "conv_dw": nrm(ks[16], (N_CONV_LAYERS, CONV_K, CONV_WIDTH), CONV_K ** -0.5),
        "conv_dw_b": nrm(ks[17], (N_CONV_LAYERS, CONV_WIDTH), 0.02),
        "conv_ln_g": 1.0 + nrm(ks[18], (N_CONV_LAYERS, CONV_WIDTH), 0.05),
        "conv_ln_b": nrm(ks[19], (N_CONV_LAYERS, CONV_WIDTH), 0.02),
        "conv_w_out": nrm(ks[20], (N_CONV_LAYERS, CONV_WIDTH, D_MODEL), CONV_WIDTH ** -0.5),
        "final_g": 1.0 + nrm(ks[21], (D_MODEL,), 0.05),
    }

def reference(x_prompt, x_sample, cache_a_k, cache_a_v, cache_b_k, cache_b_v, c, c_ctx,
              ada_w, ada_b, norm_g, attn_w_in, attn_w_out, a_sink, b_rpb,
              conv_w_in, conv_dw, conv_dw_b, conv_ln_g, conv_ln_b, conv_w_out, final_g):
    x = x_prompt
    ctx_a_k, ctx_a_v, ctx_b_k, ctx_b_v = [], [], [], []
    for layer in range(DEPTH):
        shift, scale, gate = modulation(c_ctx[None, :], ada_w[layer], ada_b[layer])
        h = rms_norm(x, norm_g[layer]) * (1 + scale) + shift
        if layer % 2 == 0:
            ai = layer // 2
            out, ka, va, kb, vb = attn_mixer_context(h, attn_w_in[ai], attn_w_out[ai], a_sink[ai])
            ctx_a_k.append(ka)
            ctx_a_v.append(va)
            ctx_b_k.append(kb)
            ctx_b_v.append(vb)
        else:
            ci = layer // 2
            out = conv_mixer(h, conv_w_in[ci], conv_dw[ci], conv_dw_b[ci], conv_ln_g[ci],
                             conv_ln_b[ci], conv_w_out[ci])
        x = x + gate * out
    y_prompt = rms_norm(x, final_g)
    new_a_k = jnp.stack(ctx_a_k, axis=1)
    new_a_v = jnp.stack(ctx_a_v, axis=1)
    new_b_k = jnp.stack(ctx_b_k, axis=1)
    new_b_v = jnp.stack(ctx_b_v, axis=1)

    x = x_sample
    cos, sin = axial_rope_tables(x_sample.shape[1], x_sample.dtype)
    for layer in range(DEPTH):
        shift, scale, gate = modulation(c, ada_w[layer], ada_b[layer])
        h = rms_norm(x, norm_g[layer]) * (1 + scale) + shift
        if layer % 2 == 0:
            ai = layer // 2
            out = attn_mixer_latent(h, cache_a_k[:, ai], cache_a_v[:, ai], cache_b_k[:, ai], cache_b_v[:, ai],
                                    attn_w_in[ai], attn_w_out[ai], a_sink[ai], b_rpb[ai], cos, sin)
        else:
            ci = layer // 2
            out = conv_mixer(h, conv_w_in[ci], conv_dw[ci], conv_dw_b[ci], conv_ln_g[ci],
                             conv_ln_b[ci], conv_w_out[ci])
        x = x + gate * out
    y_sample = rms_norm(x, final_g)
    return (y_prompt, y_sample, new_a_k, new_a_v, new_b_k, new_b_v)


_drawn_inputs = setup_inputs


def setup_inputs(seed=0):
    import zlib

    import numpy as np

    out = dict(_drawn_inputs(seed))
    spreads = {}
    factors = {'cache_a_k': 7.911,
     'cache_a_v': 6.748,
     'cache_b_k': 4.917,
     'cache_b_v': 4.03,
     'a_sink': 52.85,
     'b_rpb': 8.0,
     'conv_dw_b': 8.0,
     'conv_ln_g': 8.0,
     'conv_ln_b': 31.09}
    for name, (base, spread) in spreads.items():
        noise = np.random.default_rng([zlib.crc32(name.encode()), seed]).standard_normal(out[name].shape)
        drawn = base * np.exp(spread * noise) if base else spread * noise
        out[name] = __import__('jax').numpy.asarray(drawn.astype(out[name].dtype))
    for name, factor in factors.items():
        out[name] = (out[name] * factor).astype(out[name].dtype)
    return out
```

```python
from contextlib import ExitStack

import numpy as np

import concourse.bass as bass
from concourse import mybir

F32 = mybir.dt.float32
F32R = mybir.dt.float32r
ALU = mybir.AluOpType
ACT = mybir.ActivationFunctionType
AX = mybir.AxisListType

P = 128
D = 2048
KT = D // P
CTX, LAT = 128, 256
T = CTX + LAT
A_HEADS, A_KV, B_HEADS = 8, 2, 8
A_W, KV_W, B_W = A_HEADS * P, A_KV * P, B_HEADS * P
COL_QA, COL_KA, COL_VA = 0, A_W, A_W + KV_W
COL_QB = A_W + 2 * KV_W
COL_KB, COL_VB, COL_Z = COL_QB + B_W, COL_QB + 2 * B_W, COL_QB + 3 * B_W
GRID_W, NB_KW, RPB_H, RPB_W = 64, 16, 15, 31
ROWS = LAT // GRID_W
TAPS = 31
HALO = TAPS // 2
PAD = HALO + CTX + HALO + LAT + HALO
SPAN = PAD - 2 * HALO
POOL_TAPS = 12
PRODS = 8
CENTRE = [(0, 1, 2), (3, 4, 5), (6, 7, 8), (9, 10, 11), (12, 13), (14, 15)]
EPS = 1e-6
SCALE = float(P) ** -0.5
NEG = -3.0e38
W2 = 256
BK = 4
RAW, SPLIT = 4, 2
ADA_PAIRS = 3 * D // W2
PAIR_WOUT0, PAIR_GLU, PAIR_Z, PAIR_WOUT1 = 26, 34, 50, 58


def hybrid_trunk(nc, x_prompt, x_sample, cache_a_k, cache_a_v, cache_b_k, cache_b_v, c, c_ctx, ada_w,
                 ada_b, norm_g, attn_w_in, attn_w_out, a_sink, b_rpb, conv_w_in, conv_dw, conv_dw_b,
                 conv_ln_g, conv_ln_b, conv_w_out, final_g, const_rot, const_mask,
                 y_prompt, y_sample, new_a_k, new_a_v, new_b_k, new_b_v):
    ctx = ExitStack()
    with ctx:
        def sb(name, shape, dt=F32, where=ctx):
            return where.enter_context(nc.sbuf_tensor(name, shape, dt))

        def sem(name):
            return ctx.enter_context(nc.semaphore(name))

        X = sb("residual", [P, KT * T])
        H_hi = sb("h_hi", [P, KT, T], F32R)
        H_lo = sb("h_lo", [P, KT, T], F32R)
        raw = sb("w_raw", [P, RAW, BK, W2])
        w_hi = sb("w_hi", [P, SPLIT, BK, W2], F32R)
        w_lo = sb("w_lo", [P, SPLIT, BK, W2], F32R)
        ident = sb("ident", [P, P])
        ones = sb("ones", [P, P])
        pvec = sb("pvec", [P, 224])
        taps = sb("taps", [P, TAPS * KT])
        mod_in = sb("mod_in", [P, 2 * 3 * KT, 2])
        mod = sb("mod", [P, 2 * 3 * KT, 2])
        gain = sb("gain", [P, KT, 2])
        ssum = sb("ssum", [P, T])
        rstd = sb("rstd", [P, T])
        small = sb("small", [P, 32])
        y_area = ExitStack()
        Y_hi = sb("y_hi", [P, KT * T], F32R, y_area)
        Y_lo = sb("y_lo", [P, KT * T], F32R, y_area)
        y_area.close()
        in_area = ExitStack()
        x_tok = sb("x_tok", [P, 3, D], F32, in_area)
        rows1 = sb("rows1", [P, P], F32, in_area)
        rows2 = sb("rows2", [P, P], F32, in_area)
        rows_dw = sb("rows_dw", [P, 4, P], F32, in_area)
        c_tanh = sb("c_tanh", [P, 32], F32, in_area)
        sq0 = sb("sq0", [P, 2, T], F32, in_area)
        in_area.close()
        glu_area = ExitStack()
        th_g = sb("tanh_g", [P, 2, T], F32, glu_area)
        u_pad = sb("u_pad", [P, 2, PAD], F32, glu_area)
        conv_v = sb("conv_v", [P, 2, SPAN], F32, glu_area)
        conv_p = sb("conv_p", [P, 2, SPAN], F32, glu_area)
        tap_prod = sb("tap_products", [P, PRODS, SPAN], F32, glu_area)
        glu_area.close()
        y_hold = sb("y_area", [P, 2 * KT * T])
        att = ExitStack()
        ada_raw = sb("ada_raw", [P, RAW, BK, W2], F32, att)
        cc = sb("cond", [P, KT, 32], F32, att)
        ada_row = sb("ada_row", [P, W2], F32, att)
        rot = sb("rot", [P, P], F32, att)
        cos = sb("cos", [P, LAT], F32, att)
        sin = sb("sin", [P, LAT], F32, att)
        sink = sb("sink", [P, A_HEADS + B_HEADS], F32, att)
        zero = sb("zero", [P, P], F32, att)
        q = sb("q", [P, 2, T], F32, att)
        k = sb("k", [P, 2, T], F32, att)
        v = sb("v", [P, 3, 2 * P], F32, att)
        ck_rows = sb("ck_rows", [P, 2 * P], F32, att)
        ck = sb("ck", [P, 2 * P], F32, att)
        cv = sb("cv", [P, 2 * P], F32, att)
        k_out = sb("k_out", [P, 2 * P], F32, att)
        flip = sb("flip", [P, P], F32, att)
        mask = sb("mask", [P, 2, T], F32, att)
        rpb = sb("rpb", [P, 2, 2, LAT], F32, att)
        s = sb("scores", [P, 2 * T + CTX], F32, att)
        pT = sb("probs_t", [P, 3 * LAT + CTX], F32, att)
        zs = sb("z_silu", [P, 2, T], F32, att)
        yf = sb("y_full", [P, T], F32, att)
        st = sb("softmax_stats", [P, 6, 4], F32, att)
        att.close()
        cnv = ExitStack()
        C = sb("conv_out", [P, KT * T], F32, cnv)
        SZ = sb("silu_z", [P, KT * T], F32, cnv)
        zt = sb("tanh_z", [P, 2, T], F32, cnv)
        lsum = sb("conv_sum", [P, T], F32, cnv)
        cnv.close()
        fin = ExitStack()
        out_tok = sb("out_tok", [P, 3, D], F32, fin)
        fin_g = sb("x_gained", [P, 2, T], F32, fin)
        fin.close()
        l_hold = sb("layer_area", [P, 2 * KT * T + 1248])
        h_t = sb("h_t", [P, 2, T])
        h_f = sb("h_f", [P, 2, T])

        acc = ctx.enter_context(nc.psum_tensor("acc", [P, 4, 512], F32))
        p_ada = ctx.enter_context(nc.psum_tensor("p_ada", [P, 512], F32))
        p_s = ctx.enter_context(nc.psum_tensor("p_s", [P, 2, 512], F32))
        p_m = ctx.enter_context(nc.psum_tensor("p_m", [P, 512], F32))

        PV_ADA_B, PV_C, PV_CCTX = 0, 96, 112
        PV_NORM, PV_FINAL, PV_DWB, PV_LNG, PV_LNB = 128, 160, 176, 192, 208

        const_in = sem("const_in"); x_in = sem("x_in")
        raw_in = [sem(f"raw_in{i}") for i in range(RAW)]
        ada_in = [sem(f"ada_in{i}") for i in range(RAW)]
        hi_ready = sem("hi_ready"); lo_ready = sem("lo_ready")
        w_used = sem("w_used")
        acc_free = [sem("acc_even_free"), sem("acc_odd_free")]
        ada_used = sem("ada_used"); ada_out = sem("ada_out")
        m_ready = sem("m_ready"); m_free = sem("m_free")
        par_t = sem("params_turned"); par_ready = sem("params_ready"); c_th = sem("cond_tanh")
        cc_ready = sem("cond_ready"); zeroed = sem("zeroed")
        xt_ready = sem("x_turned"); x_done = sem("x_stored")
        ss_ready = sem("squares_summed"); rt_ready = sem("root_ready"); rs_ready = sem("rstd_ready")
        t_ready = sem("normed"); hf_ready = sem("h_full"); hh_ready = sem("h_hi_ready")
        h_ready = sem("h_ready")
        rope_ready = sem("roped"); s_ready = sem("scores_ready"); negm_ready = sem("negmax_ready")
        exp_done = sem("exp_done"); rcp_ready = sem("rcp_ready"); probs_ready = sem("probs_ready")
        pt_ready = sem("probs_turned"); pt_out = sem("probs_t_stored")
        z_tanh = sem("z_tanh"); yh_ready = sem("y_hi_ready"); y_ready = sem("y_ready")
        ck_in = sem("ck_in"); cv_in = sem("cv_in"); rpb_in = sem("rpb_in")
        ko_sent = sem("k_out_sent"); v_sent = sem("v_sent")
        th_ready = sem("tanh_g_ready"); u_ready = sem("u_ready"); pc_ready = sem("pool_taps_ready")
        prod_ready = sem("tap_products_ready"); prod_added = sem("tap_products_added")
        c_ready = sem("conv_ready"); pc_summed = sem("conv_summed")
        ln_sum = sem("ln_summed"); cen_ready = sem("centred"); sq_ready = sem("squared")
        cn_ready = sem("ln_normed"); v_ready = sem("ln_affine"); y2_full = sem("y2_full")
        y2h_ready = sem("y2_hi"); y2_done = sem("y2_ready"); lsq_ready = sem("ln_squares")
        sq_summed = sem("ln_squares_summed")
        xs_ready = sem("x_updated"); fg_ready = sem("final_gained"); ft_ready = sem("final_turned")
        ft_out = sem("final_stored"); fs_ready = sem("final_scaled"); y_sent = sem("y_sent")

        w_in0 = attn_w_in[0].rearrange("(k p) n -> p k n", p=P)
        w_out0 = attn_w_out[0].rearrange("(k p) n -> p k n", p=P)
        w_in1 = conv_w_in[0].rearrange("(k p) n -> p k n", p=P)
        w_out1 = conv_w_out[0].rearrange("(k p) n -> p k n", p=P)
        w_ada = [ada_w[i].rearrange("(k p) n -> p k n", p=P) for i in range(2)]

        M_START = 0
        M_FIRST = M_START + 16 + 1
        M_A = M_FIRST + 5
        M_B = M_A + 3 * 7
        M_BLOOP = M_B + 9
        M_LAST = M_BLOOP + 3 * 8
        M_NORM1 = M_LAST + 4
        M_LN = M_NORM1 + 1
        M_FIN = M_LN + 2

        def at(e, sm, n):
            if not isinstance(n, int) or n > 0:
                e.wait_ge(sm, n)

        def evacuated(e, par, half):
            e.wait_ge(acc_free[par], half + 1)

        block = ctx.enter_context(nc.Block())

        @block.sync
        def _(sp):
            consts = [(ident[:], const_rot[0, :, 0:P]), (rot[:], const_rot[1, :, 0:P]),
                      (flip[:], const_rot[0, :, P:]),
                      (cos[:], const_rot[2]), (sin[:], const_rot[3]),
                      (rows1[0:96], ada_b.rearrange("l (r f) -> (l r) f", f=P)),
                      (rows1[96:112], c.rearrange("b (r f) -> (b r) f", f=P)),
                      (rows1[112:128], c_ctx.rearrange("(r f) -> r f", f=P)),
                      (rows2[0:32], norm_g.rearrange("l (r f) -> (l r) f", f=P)),
                      (rows2[32:48], final_g.rearrange("(r f) -> r f", f=P)),
                      (rows2[48:64], conv_dw_b.rearrange("l (r f) -> (l r) f", f=P)),
                      (rows2[64:80], conv_ln_g.rearrange("l (r f) -> (l r) f", f=P)),
                      (rows2[80:96], conv_ln_b.rearrange("l (r f) -> (l r) f", f=P)),
                      (rows_dw[0:124], conv_dw[0].rearrange("k (r f) -> (k r) f", f=P)
                       .rearrange("(a b) f -> b a f", b=124)),
                      (sink[:, 0:A_HEADS], a_sink.broadcast_to([P, A_HEADS])),
                      (mask[:], const_mask[0])]
            assert len(consts) == 16
            for dst, src in consts:
                sp.dma_start(dst, src).then_inc(const_in, 16)
            sp.dma_start(x_tok[:, 0], x_prompt[0]).then_inc(x_in, 16)
            for j in range(2):
                sp.dma_start(x_tok[:, 1 + j], x_sample[0, j * P:(j + 1) * P]).then_inc(x_in, 16)

            def ada(a, src, col, first=False):
                for s_ in range(BK):
                    ada_block(a, s_, src, col, first)

            def ada_block(a, s_, src, col, first=False):
                if not first:
                    sp.wait_ge(ada_used, 4 * a + s_ - 3)
                sp.dma_start(ada_raw[:, s_], src[:, BK * s_:BK * s_ + BK, bass.ds(col, W2)])\
                    .then_inc(ada_in[s_], 16)

            def w_block(m, s_, src, col, first=False):
                if not first:
                    sp.wait_ge(lo_ready, 4 * m + s_ - 3)
                sp.dma_start(raw[:, s_], src[:, BK * s_:BK * s_ + BK, bass.ds(col, W2)])\
                    .then_inc(raw_in[s_], 16)

            for s_ in range(BK):
                w_block(0, s_, w_in0, COL_KA, first=True)
            ada(0, w_ada[0], 0, first=True)
            with sp.Fori(1, 16) as a:
                ada(a, w_ada[0], a * W2)

            def pairs(m, cols, src, ada_of=lambda t: [], small_of=lambda t: None, ready=0):
                for t in range(4 * len(cols)):
                    if t >= ready:
                        w_block(m + t // 4, t % 4, src, cols[t // 4])
                    for a in ada_of(t):
                        ada_block(*a)
                    small_of(t)

            sp.dma_start(ck_rows[:], cache_a_k[0, 0].rearrange("s h d -> s (h d)")).then_inc(ck_in, 16)
            sp.dma_start(cv[:], cache_a_v[0, 0].rearrange("s h d -> s (h d)")).then_inc(cv_in, 16)
            g0 = 2 * D
            pairs(0, [COL_KA, COL_VA, COL_QA], w_in0,
                  lambda t: [(16 + t // 4, t % 4, w_ada[0], g0 + W2 * (t // 4))], ready=4)

            def kv_out(m_free_n, half, k_to, v_to):
                sp.wait_ge(m_free, m_free_n)
                sp.dma_start(k_to, k_out[:]).then_inc(ko_sent, 16)
                sp.wait_ge(acc_free[1], half + 1)
                sp.dma_start(v_to, v[:, 0]).then_inc(v_sent, 16)

            kv_out(M_FIRST + 3, 0, new_a_k[0, 0].rearrange("s h d -> s (h d)"),
                   new_a_v[0, 0].rearrange("s h d -> s (h d)"))

            def a_step(n):
                pairs(3 + 2 * n, [COL_Z + W2 * n, COL_QA + W2 * (n + 1)], w_in0,
                      lambda t: [(19 + 4 * n + t // 2, 2 * (t % 2) + j, w_ada[1], (4 * n + t // 2) * W2)
                                 for j in range(2)])

            with sp.Fori(0, 3) as n:
                a_step(n)

            def heads(x, i):
                return x[0, 0, :, bass.ds(2 * i, 2)].rearrange("s h d -> s (h d)")

            rpb_flat = b_rpb.rearrange("l h r c -> (l h r c)")

            def small_loads(i):
                def at_tick(t):
                    if t == 8:
                        sp.wait_ge(m_free, M_FIRST + 4 if isinstance(i, int) else M_BLOOP + 8 * (i - 2) + 7)
                        sp.dma_start(ck_rows[:], heads(cache_b_k, i)).then_inc(ck_in, 16)
                    if t == 12:
                        sp.wait_ge(s_ready, 2 * (i + 3) + 2)
                        for j in range(2):
                            for qt in range(2):
                                for half in range(2):
                                    r = 2 * qt + half
                                    off = ((2 * i + j) * RPB_H + 7 - r) * RPB_W + NB_KW - GRID_W
                                    first = rpb_flat[bass.ds(off, 1)]
                                    src = bass.AP(first.tensor, first.offset,
                                                  [[1, GRID_W], [RPB_W, ROWS], [1, GRID_W]])
                                    dst = rpb[64 * half:64 * half + 64, j, qt]\
                                        .rearrange("p (r c) -> p r c", c=GRID_W)
                                    sp.dma_start(dst, src).then_inc(rpb_in, 16)
                        if isinstance(i, int) and i == 0:
                            sp.wait_ge(negm_ready, 2 * 4)
                            sp.dma_start(mask[:], const_mask[1]).then_inc(const_in, 16)
                    if t == 13:
                        sp.wait_ge(y_ready, 2 * (i + 3) + 2)
                        sp.dma_start(cv[:], heads(cache_b_v, i)).then_inc(cv_in, 16)
                return at_tick

            def b_loads(i, src, first_col):
                pairs(9 + 4 * i, [COL_Z + W2 * (i + 3), COL_KB + W2 * i, COL_VB + W2 * i,
                                  COL_QB + W2 * i], w_in0,
                      lambda t: [(31 + 4 * i + t // 4, t % 4, src, first_col + (t // 4) * W2)],
                      small_loads(i))
                kv_out(M_B + 7 if isinstance(i, int) else M_BLOOP + 8 * (i - 1) + 6, 5 + 2 * i,
                       heads(new_b_k, i), heads(new_b_v, i))

            b_loads(0, w_ada[0], g0 + W2 * 3)
            with sp.Fori(1, 4) as i:
                b_loads(i, w_ada[1], (8 + 4 * i) * W2)
            pairs(25, [COL_Z + 7 * W2], w_in0,
                  lambda t: [(47, t % 4, w_ada[0], g0 + 7 * W2)])
            with sp.Fori(0, 8) as j:
                pairs(PAIR_WOUT0 + j, [j * W2], w_out0)
            with sp.Fori(1, 9) as j:
                pairs(PAIR_GLU - 2 + 2 * j, [W2 * j + (D - W2), W2 * j - W2], w_in1)
            with sp.Fori(0, 8) as j:
                pairs(PAIR_Z + j, [2 * D + j * W2], w_in1)
            with sp.Fori(0, 8) as j:
                pairs(PAIR_WOUT1 + j, [j * W2], w_out1)
            outs = [y_prompt[0], y_sample[0, 0:P], y_sample[0, P:2 * P]]
            for i in range(3):
                sp.wait_ge(fs_ready, i + 1)
                sp.dma_start(outs[i], out_tok[:, i]).then_inc(y_sent, 16)
            sp.wait_ge(y_sent, 48)
            sp.wait_ge(ko_sent, 16 * 5)
            sp.wait_ge(v_sent, 16 * 5)

        @block.tensor
        def _(pe):
            def m_use(n):
                at(pe, m_free, n)

            def mm3(out, wh, wl, xh, xl, start, stop):
                pe.matmul(out, wh, xh, start=start, stop=False)
                pe.matmul(out, wh, xl, start=False, stop=False)
                return pe.matmul(out, wl, xh, start=False, stop=stop)

            def w_block(m, half, par, s_, kind="h", x_wait=None):
                if s_ == 0:
                    at(pe, acc_free[par], half)
                pe.wait_ge(lo_ready, 4 * m + s_ + 1)
                b = s_ % SPLIT
                for kk in range(BK):
                    kt = BK * s_ + kk
                    if x_wait is not None:
                        pe.wait_ge(x_wait[0], x_wait[1] + kt + 1)
                    if kind == "v":
                        for t in range(3):
                            out = acc[:, 2 * par + t // 2, (t % 2) * W2:(t % 2) * W2 + W2]
                            xh, xl = (z[:, kt, t * P:(t + 1) * P] for z in (H_hi, H_lo))
                            pe.matmul(out, xh, w_hi[:, b, kk], start=(kt == 0 and t != 1), stop=False,
                                      skip_group_check=True)
                            pe.matmul(out, xh, w_lo[:, b, kk], start=False, stop=False,
                                      skip_group_check=True)
                            last = pe.matmul(out, xl, w_hi[:, b, kk], start=False, stop=(kt == KT - 1),
                                             skip_group_check=True)
                        continue
                    if kind == "h":
                        xh, xl = H_hi[:, kt], H_lo[:, kt]
                    else:
                        xh, xl = Y_hi[:, kt * T:(kt + 1) * T], Y_lo[:, kt * T:(kt + 1) * T]
                    for j in range(2):
                        cols = slice(j * P, (j + 1) * P)
                        last = mm3(acc[:, 2 * par + j, 0:T], w_hi[:, b, kk, cols], w_lo[:, b, kk, cols],
                                   xh, xl, kt == 0, kt == KT - 1)
                last.then_inc(w_used, 1)

            def ada_block(a, s_):
                pe.wait_ge(ada_in[s_], 16 * (a + 1))
                if s_ == 0:
                    at(pe, ada_out, a)
                for g in range(4):
                    last = pe.matmul(p_ada[32 * g:32 * g + 32, 0:W2], cc[:, BK * s_ + g],
                                     ada_raw[:, s_, g], start=(s_ == 0), stop=(s_ == 3),
                                     tile_position=(0, 32 * g))
                last.then_inc(ada_used, 1)

            def ada_turn(a, use):
                pe.wait_ge(ada_out, a + 1)
                m_use(use)
                for j in range(2):
                    last = pe.transpose(p_m[:, j * P:(j + 1) * P], ada_row[:, j * P:(j + 1) * P], ident[:])
                last.then_inc(m_ready, 1)

            pe.wait_ge(const_in, 256)
            pe.transpose(p_s[:, 0, 0:P], rows1[:], ident[:])
            pe.transpose(p_s[:, 0, P:P + 96], rows2[0:96], ident[0:96, 0:96])
            for i in range(4):
                last = pe.transpose(p_s[:, 1, 124 * i:124 * i + 124], rows_dw[0:124, i],
                                    ident[0:124, 0:124])
            last.then_inc(par_t, 1)
            pe.wait_ge(x_in, 48)
            for f in range(KT):
                at(pe, x_done, f - 3)
                for t in range(3):
                    last = pe.transpose(acc[:, f % 4, t * P:(t + 1) * P],
                                        x_tok[:, t, f * P:(f + 1) * P], ident[:])
                last.then_inc(xt_ready, 1)
            pe.wait_ge(cc_ready, 1)

            def ada_pair(a):
                for s_ in range(BK):
                    ada_block(a, s_)
                ada_turn(a, M_START + a)

            ada_pair(0)
            with pe.Fori(1, 16) as a:
                ada_pair(a)

            def norm_mean(n, use):
                pe.wait_ge(ss_ready, n + 1)
                m_use(use)
                pe.matmul(p_m[:, 0:T], ones[:], ssum[:], start=True, stop=True).then_inc(m_ready, 1)

            norm_mean(0, M_START + 16)

            def rotate(x, use):
                m_use(use)
                pe.matmul(p_m[:].rearrange("p (a b) -> p a b", a=2), rot[:], x[:, :, CTX:T],
                          start=True, stop=True).then_inc(m_ready, 1)

            def scores(n, j, kv, is_a=True):
                at(pe, pt_out, 2 * n + j)
                pe.matmul(p_s[:, 0, T:T + CTX], q[:, j, 0:CTX], k[:, kv, 0:CTX], start=True, stop=True)
                for t in range(2):
                    lhs = q[:, j, CTX + t * P:CTX + (t + 1) * P]
                    pe.matmul(p_s[:, t, 0:LAT], lhs, k[:, kv, CTX:T], start=True, stop=is_a)
                    if not is_a:
                        pe.matmul(p_s[:, t, 0:LAT], flip[:], rpb[:, j, t], start=False, stop=True)
                    last = pe.matmul(p_s[:, t, LAT:LAT + P], lhs, ck[:, kv * P:(kv + 1) * P],
                                     start=True, stop=True)
                last.then_inc(s_ready, 1)

            def turn_probs(n, j):
                pe.wait_ge(probs_ready, 2 * n + j + 1)
                for t in range(2):
                    for kt in range(3):
                        pe.transpose(p_s[:, kt // 2, (kt % 2) * LAT + t * P:(kt % 2) * LAT + (t + 1) * P],
                                     s[:, t * T + kt * P:t * T + (kt + 1) * P], ident[:])
                pe.transpose(p_s[:, 1, LAT:LAT + P], s[:, 2 * T:2 * T + CTX], ident[:])\
                    .then_inc(pt_ready, 1)

            def attend(n, j, kv, use):
                pe.wait_ge(pt_out, 2 * n + j + 1)
                m_use(use)
                vs = slice(kv * P, (kv + 1) * P)
                pe.matmul(p_m[:, 0:CTX], v[:, 0, vs], pT[:, 3 * LAT:3 * LAT + CTX], start=True, stop=True)
                pe.matmul(p_m[:, CTX:T], v[:, 1, vs], pT[:, 0:LAT], start=True, stop=False)
                pe.matmul(p_m[:, CTX:T], v[:, 2, vs], pT[:, LAT:2 * LAT], start=False, stop=False)
                pe.matmul(p_m[:, CTX:T], cv[:, vs], pT[:, 2 * LAT:3 * LAT], start=False, stop=True)\
                    .then_inc(m_ready, 1)

            def turn_k(use):
                m_use(use)
                for j in range(2):
                    last = pe.transpose(p_m[:, j * P:(j + 1) * P], k[:, j, 0:CTX], ident[:])
                last.then_inc(m_ready, 1)

            def turn_ck(i, use):
                pe.wait_ge(ck_in, 16 * (i + 1))
                m_use(use)
                for j in range(2):
                    last = pe.transpose(p_m[:, j * P:(j + 1) * P], ck_rows[:, j * P:(j + 1) * P], ident[:])
                last.then_inc(m_ready, 1)

            for t in range(12):
                m, s_ = t // 4, t % 4
                w_block(m, m // 2, m % 2, s_, "v" if m == 1 else "h", (h_ready, 0) if m == 0 else None)
                ada_block(16 + m, s_)
                if t == 4:
                    evacuated(pe, 0, 0)
                    rotate(k, M_FIRST)
                if t == 5:
                    ada_turn(16, M_FIRST + 1)
                if t == 6:
                    turn_k(M_FIRST + 2)
                if t == 8:
                    turn_ck(0, M_FIRST + 3)
                if t == 9:
                    ada_turn(17, M_FIRST + 4)

            def a_step(n, kv):
                use = M_A + 7 * n
                for t in range(8):
                    i, s_ = t // 4, t % 4
                    m = 3 + 2 * n + i
                    w_block(m, 1 + n + i, 1 - i, s_)
                    for j in range(2):
                        ada_block(19 + 4 * n + t // 2, 2 * (t % 2) + j)
                    if t == 0:
                        evacuated(pe, 0, 1 + n)
                        rotate(q, use)
                    if t == 1:
                        pe.wait_ge(rope_ready, n + 2)
                        scores(n, 0, kv)
                        ada_turn(18 + 4 * n, use + 1)
                    if t == 2:
                        ada_turn(19 + 4 * n, use + 2)
                    if t == 3:
                        turn_probs(n, 0)
                    if t == 4:
                        pe.wait_ge(cv_in, 16)
                        attend(n, 0, kv, use + 3)
                        scores(n, 1, kv)
                    if t == 5:
                        ada_turn(20 + 4 * n, use + 4)
                    if t == 6:
                        turn_probs(n, 1)
                        ada_turn(21 + 4 * n, use + 5)
                    if t == 7:
                        attend(n, 1, kv, use + 6)

            a_step(0, 0)
            a_step(1, 0)
            a_step(2, 1)

            def b_step(n, is_a, last=False):
                i = n - 3
                use = (M_B if is_a else M_BLOOP + 8 * (n - 4)) + (1 if is_a else 0)
                ab = 31 + 4 * i
                kvs = (1, 1) if is_a else (0, 1)
                for t in range(12 if last else 16):
                    pi, s_ = t // 4, t % 4
                    m, half, par = 9 + 4 * i + pi, 4 + 2 * i + (pi + 1) // 2, 1 - pi % 2
                    if last and pi > 0:
                        w_block(m, half, par, s_, "y", (y_ready, 0) if pi == 1 else None)
                    else:
                        w_block(m, half, par, s_, "v" if pi == 2 else "h")
                    if not (last and pi > 0):
                        ada_block(ab + pi, s_)
                    if t == 0 and is_a:
                        evacuated(pe, 0, 1 + n)
                        rotate(q, M_B)
                    if t == 1:
                        if is_a:
                            pe.wait_ge(rope_ready, n + 2)
                        else:
                            evacuated(pe, 0, 4 + 2 * i)
                            pe.wait_ge(rpb_in, 128 * i)
                        scores(n, 0, kvs[0], is_a)
                        ada_turn(ab - 1, use)
                    if t == 3:
                        turn_probs(n, 0)
                    if t == 4:
                        if not is_a:
                            pe.wait_ge(cv_in, 16 * (i + 1))
                        attend(n, 0, kvs[0], use + 1)
                        scores(n, 1, kvs[1], is_a)
                    if t == 5:
                        ada_turn(ab, use + 2)
                    if t == 6:
                        turn_probs(n, 1)
                        if last:
                            attend(n, 1, kvs[1], use + 3)
                    if last:
                        continue
                    if t == 7:
                        attend(n, 1, kvs[1], use + 3)
                    if t == 9:
                        ada_turn(ab + 1, use + 4)
                    if t == 10:
                        evacuated(pe, 0, 5 + 2 * i)
                        turn_k(use + 5)
                    if t == 11:
                        turn_ck(i + 1, use + 6)
                    if t == 13:
                        ada_turn(ab + 2, use + 7)

            b_step(3, True)
            with pe.Fori(4, 7) as n:
                b_step(n, False)
            b_step(7, False, last=True)

            with pe.Fori(1, 4) as p:
                for t in range(8):
                    i, s_ = t // 4, t % 4
                    w_block(PAIR_WOUT0 + 2 * p + i, PAIR_WOUT0 // 2 + p, i, s_, "y")

            norm_mean(1, M_NORM1)

            def two_pairs(p, x_wait=None):
                for t in range(8):
                    i, s_ = t // 4, t % 4
                    w_block(PAIR_GLU + 2 * p + i, PAIR_GLU // 2 + p, i, s_, "h", x_wait if i == 0 else None)
                    if isinstance(p, int) and p == 9 and t == 1:
                        pe.wait_ge(ln_sum, 1)
                        m_use(M_LN)
                        pe.matmul(p_m[:, 0:T], ones[:], lsum[:], start=True, stop=True).then_inc(m_ready, 1)
                    if isinstance(p, int) and p == 10 and t == 1:
                        norm_mean(2, M_LN + 1)

            two_pairs(0, (h_ready, KT))
            with pe.Fori(1, 9) as p:
                two_pairs(p)
            two_pairs(9)
            two_pairs(10)
            two_pairs(11)

            def turn_final(f, b):
                pe.wait_ge(fg_ready, f + 1)
                at(pe, ft_out, f - 1 if isinstance(f, int) else f - 1)
                for t in range(3):
                    last = pe.transpose(p_s[:, b, t * P:(t + 1) * P], fin_g[:, b, t * P:(t + 1) * P],
                                        ident[:])
                last.then_inc(ft_ready, 1)

            def out_pairs(p, first=False):
                for t in range(8):
                    i, s_ = t // 4, t % 4
                    w_block(PAIR_WOUT1 + 2 * p + i, PAIR_WOUT1 // 2 + p, i, s_, "y",
                            (y2_done, 0) if first and i == 0 else None)
                    if t in (1, 2) and not first:
                        turn_final(4 * p - 2 + t - 1, t - 1)
                    if t in (5, 6):
                        turn_final(4 * p + t - 5, t - 5)

            out_pairs(0, first=True)
            with pe.Fori(1, 4) as p:
                out_pairs(p)
            turn_final(14, 0)
            turn_final(15, 1)
            pe.wait_ge(ss_ready, 4)
            m_use(M_FIN)
            for t in range(3):
                last = pe.matmul(p_m[:, 2 * t:2 * t + 2], ssum[:, t * P:(t + 1) * P], ones[:, 0:2],
                                 start=True, stop=True)
            last.then_inc(m_ready, 1)

        @block.scalar
        def _(act):
            def split(mb, k_):
                m, s_ = mb + k_ // 4, k_ % 4
                act.wait_ge(raw_in[s_], 16 * (m + 1))
                at(act, w_used, 4 * m + s_ - 1)
                act.activation(w_hi[:, s_ % SPLIT], raw[:, s_], ACT.Copy).then_inc(hi_ready, 1)

            def root(n, use, x):
                act.wait_ge(m_free, use + 1)
                act.activation(x, x, ACT.Sqrt).then_inc(rt_ready, 1)

            def h_tiles(layer, mb):
                def two(i):
                    for j in range(2):
                        act.wait_ge(hf_ready, layer * KT + 2 * i + j + 1)
                        act.activation(H_hi[:].rearrange("p k t -> p (k t)")[:, bass.ds((2 * i + j) * T, T)],
                                       h_f[:, j], ACT.Copy).then_inc(hh_ready, 1)
                with act.Fori(0, 4) as i:
                    two(i)
                split(mb, 2)
                with act.Fori(4, 6) as i:
                    two(i)
                split(mb, 3)
                with act.Fori(6, 8) as i:
                    two(i)

            act.wait_ge(par_ready, 1)
            act.activation(c_tanh[:], pvec[:, PV_C:PV_C + 32], ACT.Tanh, scale=0.5).then_inc(c_th, 1)
            for f in range(KT):
                act.wait_ge(xt_ready, f + 1)
                act.activation(X[:, f * T:(f + 1) * T], acc[:, f % 4, 0:T], ACT.Copy).then_inc(x_done, 1)
            split(0, 0)
            split(0, 1)
            root(0, M_START + 16, rstd[:])
            h_tiles(0, 0)

            def take(par, mb_done, out, scale=1.0):
                act.wait_ge(w_used, 4 * mb_done + 4)
                act.activation(out, acc[:, 2 * par:2 * par + 2, 0:T], ACT.Copy, scale=scale)\
                    .then_inc(acc_free[par], 1)

            def take_v(mb_done, n_sent):
                act.wait_ge(w_used, 4 * mb_done + 4)
                at(act, v_sent, n_sent)
                act.activation(v[:, 0:2].rearrange("p a b -> p (a b)"), acc[:, 2], ACT.Copy)
                act.activation(v[:, 2], acc[:, 3, 0:W2], ACT.Copy).then_inc(acc_free[1], 1)

            def exps(n, j):
                act.wait_ge(negm_ready, 2 * n + j + 1)
                for r in range(3):
                    cols = slice(r * T, r * T + (T if r < 2 else CTX))
                    act.activation(s[:, cols], s[:, cols], ACT.Exp, bias=st[:, 1, r:r + 1],
                                   accum_out=st[:, 2, r:r + 1])
                act.activation(st[:, 3, 0:3], st[:, 1, 0:3], ACT.Exp, bias=sink[:, bass.ds(2 * n + j, 1)])\
                    .then_inc(exp_done, 1)

            def store_pt(n, j):
                act.wait_ge(pt_ready, 2 * n + j + 1)
                act.activation(pT[:, 0:512], p_s[:, 0], ACT.Copy)
                act.activation(pT[:, 512:3 * LAT + CTX], p_s[:, 1, 0:T], ACT.Copy).then_inc(pt_out, 1)

            def y_hi(n, j, use):
                act.wait_ge(m_free, use + 1)
                act.activation(Y_hi[:, bass.ds((2 * n + j) * T, T)], yf[:], ACT.Copy).then_inc(yh_ready, 1)

            def z_gate(n, mb_done, par):
                act.wait_ge(w_used, 4 * mb_done + 4)
                act.activation(zs[:], acc[:, 2 * par:2 * par + 2, 0:T], ACT.Tanh, scale=0.5)\
                    .then_inc(z_tanh, 1)

            for k_ in range(4, 14):
                split(0, k_)
                if k_ == 5:
                    take(0, 0, k[:])
                if k_ == 9:
                    take_v(1, 0)
                if k_ == 13:
                    take(0, 2, q[:], SCALE)

            def a_step(n):
                mb, use = 3 + 2 * n, M_A + 7 * n
                for k_ in range(2, 10):
                    split(mb, k_)
                    if k_ == 3:
                        exps(n, 0)
                    if k_ == 5:
                        z_gate(n, mb, 1)
                        store_pt(n, 0)
                    if k_ == 6:
                        y_hi(n, 0, use + 3)
                        exps(n, 1)
                    if k_ == 8:
                        store_pt(n, 1)
                    if k_ == 9:
                        y_hi(n, 1, use + 6)
                        take(0, mb + 1, q[:], SCALE)

            with act.Fori(0, 3) as n:
                a_step(n)

            def b_step(n, is_a, last=False):
                i = n - 3
                mb, use = 9 + 4 * i, (M_B + 1 if is_a else M_BLOOP + 8 * (n - 4))
                for k_ in range(2, 14 if last else 18):
                    split(mb, k_)
                    if k_ == 3:
                        exps(n, 0)
                    if k_ == 5:
                        z_gate(n, mb, 1)
                        store_pt(n, 0)
                    if k_ == 6:
                        y_hi(n, 0, use + 1)
                        exps(n, 1)
                    if k_ == 8:
                        store_pt(n, 1)
                        if last:
                            y_hi(n, 1, use + 3)
                    if last:
                        if k_ in (9, 13):
                            squares((k_ - 9) // 4, (PAIR_WOUT0 + (k_ - 9) // 4) // 2, (k_ - 9) // 4)
                        continue
                    if k_ == 9:
                        y_hi(n, 1, use + 3)
                        take(0, mb + 1, k[:])
                    if k_ == 13:
                        take_v(mb + 2, 16 * (i + 1))
                    if k_ == 17:
                        take(0, mb + 3, q[:], SCALE)

            def squares(pr, half, par):
                act.wait_ge(acc_free[par], half + 1)
                act.activation(h_f[:].rearrange("p a b -> p (a b)"), X[:, bass.ds(2 * pr * T, 2 * T)],
                               ACT.Square).then_inc(sq_ready, 1)

            b_step(3, True)
            with act.Fori(4, 7) as n:
                b_step(n, False)
            b_step(7, False, last=True)
            with act.Fori(1, 4) as p:
                for k_ in range(2, 10):
                    split(PAIR_WOUT0 + 2 * p, k_)
                    if k_ in (5, 9):
                        i = (k_ - 5) // 4
                        squares(2 * p + i, PAIR_WOUT0 // 2 + p, i)

            root(1, M_NORM1, rstd[:])
            h_tiles(1, PAIR_GLU)

            def tanh_g(p):
                act.wait_ge(w_used, 4 * (PAIR_GLU + 2 * p) + 4)
                at(act, acc_free[1], PAIR_GLU // 2 + p)
                act.activation(th_g[:], acc[:, 0:2, 0:T], ACT.Tanh, scale=0.5).then_inc(acc_free[0], 1)

            def tanh_z(j, par):
                act.wait_ge(w_used, 4 * (PAIR_Z + j) + 4)
                at(act, acc_free[1 - par], (PAIR_Z + j + par) // 2)
                act.activation(zt[:], acc[:, 2 * par:2 * par + 2, 0:T], ACT.Tanh, scale=0.5)\
                    .then_inc(z_tanh, 1)

            def tap_products(p, part):
                for i in range(POOL_TAPS * part // 4, POOL_TAPS * (part + 1) // 4):
                    j, tap = i // POOL_TAPS, TAPS - POOL_TAPS + i % POOL_TAPS
                    if i == 0:
                        act.wait_ge(acc_free[1], PAIR_GLU // 2 + p + 1)
                    at(act, prod_added, 2 * POOL_TAPS * p + i + 1 - PRODS)
                    act.activation(tap_prod[:, i % PRODS], u_pad[:, j, tap:tap + SPAN], ACT.Copy,
                                   scale=taps[:, bass.ds(tap * KT + 2 * p + j, 1)]).then_inc(prod_ready, 1)

            for k_ in range(4, 10):
                split(PAIR_GLU, k_)
                if k_ == 5:
                    tanh_g(0)

            def glu_step(p):
                for k_ in range(2, 10):
                    split(PAIR_GLU + 2 * p, k_)
                    tap_products(p - 1, k_ - 2)
                    if k_ == 5:
                        tanh_g(p)

            glu_step(1)
            with act.Fori(2, 8) as p:
                glu_step(p)

            def centred_square(f):
                act.wait_ge(cen_ready, f + 1)
                at(act, sq_summed, f - 1)
                act.activation(h_f[:, f % 2], C[:, f * T:(f + 1) * T], ACT.Square).then_inc(lsq_ready, 1)

            def ln_gate(f):
                tile = C[:, f * T:(f + 1) * T]
                act.wait_ge(cn_ready, f + 1)
                act.activation(tile, tile, ACT.Identity, scale=pvec[:, PV_LNG + f:PV_LNG + f + 1],
                               bias=pvec[:, PV_LNB + f:PV_LNB + f + 1])
                act.drain()
                act.activation(h_t[:, f % 2], tile, ACT.Tanh, scale=0.5).then_inc(v_ready, 1)

            def y2_tile(f):
                act.wait_ge(y2_full, f + 1)
                act.activation(Y_hi[:, f * T:(f + 1) * T], h_f[:, f % 2], ACT.Copy).then_inc(y2h_ready, 1)
                if f + 1 < KT:
                    ln_gate(f + 1)

            for p in range(8, 12):
                for k_ in range(2, 10):
                    split(PAIR_GLU + 2 * p, k_)
                    if p == 8:
                        tap_products(7, k_ - 2)
                    if p == 9 and k_ >= 4:
                        for f in CENTRE[k_ - 4]:
                            centred_square(f)
                    if k_ in (5, 9):
                        tanh_z(2 * (p - 8) + (k_ - 5) // 4, (k_ - 5) // 4)
                    if p == 10 and k_ == 3:
                        root(2, M_LN + 1, rstd[:])
                        ln_gate(0)
                    if p == 10 and k_ >= 4:
                        y2_tile(k_ - 4)
                    if p == 11:
                        y2_tile(k_ + 4)

            def final_pair(pr, half, par):
                squares(pr, half, par)
                for j in range(2):
                    f = 2 * pr + j
                    at(act, ft_ready, f - 1)
                    act.activation(fin_g[:, j], X[:, bass.ds(f * T, T)], ACT.Copy,
                                   scale=pvec[:, bass.ds(PV_FINAL + f, 1)]).then_inc(fg_ready, 1)

            def out_step(p, first=False, last=False):
                for k_ in range(2, 10):
                    if not (last and k_ > 7):
                        split(PAIR_WOUT1 + 2 * p, k_)
                    if first and k_ < 4:
                        y2_tile(12 + k_)
                    if k_ in (5, 9):
                        i = (k_ - 5) // 4
                        final_pair(2 * p + i, PAIR_WOUT1 // 2 + p, i)

            out_step(0, first=True)
            with act.Fori(1, 3) as p:
                out_step(p)
            out_step(3, last=True)
            root(3, M_FIN, small[:, 4:10])

        @block.vector
        def _(dve):
            def split(mb, k_):
                m, s_ = mb + k_ // 4, k_ % 4
                dve.wait_ge(hi_ready, 4 * m + s_ + 1)
                dve.tensor_tensor(w_lo[:, s_ % SPLIT], raw[:, s_], w_hi[:, s_ % SPLIT].bitcast(F32),
                                  ALU.subtract).then_inc(lo_ready, 1)

            def over2(x, n):
                return x.unsqueeze(1).broadcast_to([P, 2, n])

            def ada_store(a):
                dve.wait_ge(ada_used, 4 * a + 4)
                dve.tensor_copy(ada_row[:], p_ada[:, 0:W2]).then_inc(ada_out, 1)

            def ada_sum(a, use):
                dve.wait_ge(m_ready, use + 1)
                dve.tensor_reduce(mod_in[:].rearrange("p f c -> p (f c)")[:, bass.ds(4 * a, 4)]
                                  .rearrange("p (f c) -> p f c", c=2),
                                  p_m[:, 0:2 * P].rearrange("p (f g c) -> p f c g", f=2, g=4)[:, :, 0:2, :],
                                  AX.X, ALU.add).then_inc(m_free, 1)

            def mod_done(pair, a, n):
                for c_ in range(2):
                    dve.tensor_tensor(mod[:, 2 * pair:2 * (pair + n), c_], mod_in[:, 2 * a:2 * (a + n), c_],
                                      pvec[:, PV_ADA_B + 2 * pair:PV_ADA_B + 2 * (pair + n)], ALU.add)

            def norm_rstd(n, use, out, src):
                dve.wait_ge(m_ready, use + 1)
                dve.tensor_scalar(out, src, EPS, None, ALU.add).then_inc(m_free, 1)
                dve.wait_ge(rt_ready, n + 1)
                dve.reciprocal(out, out).then_inc(rs_ready, 1)

            def h_tiles(layer, mb):
                base = 3 * KT * layer
                dve.scalar_tensor_tensor(out=gain[:], in0=mod[:, base + KT:base + 2 * KT, :], scalar=1.0,
                                         in1=pvec[:, PV_NORM + layer * KT:PV_NORM + (layer + 1) * KT]
                                         .unsqueeze(2).broadcast_to([P, KT, 2]), op0=ALU.add, op1=ALU.mult)
                dve.drain()
                gain_f = gain[:].rearrange("p k c -> p (k c)")
                mod_f = mod[:].rearrange("p k c -> p (k c)")

                def two(i):
                    dve.drain()
                    for j in range(2):
                        f = 2 * i + j
                        dve.wait_ge(t_ready, layer * KT + f + 1)
                        for c_, cols in enumerate((slice(0, CTX), slice(CTX, T))):
                            last = dve.tensor_scalar(h_f[:, j, cols], h_t[:, j, cols],
                                                     gain_f[:, bass.ds(2 * f + c_, 1)],
                                                     mod_f[:, bass.ds(2 * (base + f) + c_, 1)],
                                                     ALU.mult, ALU.add)
                        last.then_inc(hf_ready, 1)
                    for j in range(2):
                        f = 2 * i + j
                        dve.wait_ge(hh_ready, layer * KT + f + 1)
                        at_ = bass.ds(f * T, T)
                        dve.tensor_tensor(H_lo[:].rearrange("p k t -> p (k t)")[:, at_], h_f[:, j],
                                          H_hi[:].rearrange("p k t -> p (k t)")[:, at_].bitcast(F32),
                                          ALU.subtract).then_inc(h_ready, 1)
                with dve.Fori(0, 4) as i:
                    two(i)
                split(mb, 2)
                with dve.Fori(4, 6) as i:
                    two(i)
                split(mb, 3)
                with dve.Fori(6, 8) as i:
                    two(i)

            dve.memset(cc[:], 0.0)
            dve.memset(ones[:], 1.0 / D)
            dve.memset(zero[:], 0.0)
            dve.memset(ssum[:], 0.0)
            dve.memset(sink[:, A_HEADS:], NEG)
            dve.wait_ge(par_t, 1)
            dve.tensor_copy(pvec[:], p_s[:, 0, 0:224])
            dve.tensor_scalar(taps[:], p_s[:, 1, 0:TAPS * KT], 0.5, None, ALU.mult)
            dve.drain().then_inc(par_ready, 1)
            dve.wait_ge(c_th, 1)
            dve.scalar_tensor_tensor(out=c_tanh[:], in0=c_tanh[:], scalar=1.0, in1=pvec[:, PV_C:PV_C + 32],
                                     op0=ALU.add, op1=ALU.mult)
            dve.drain()
            for col, src in ((0, 16), (1, 0)):
                last = dve.tensor_scalar(cc[:, :, col:col + 1], c_tanh[:, src:src + 16].unsqueeze(2), 0.5,
                                         None, ALU.mult)
            last.then_inc(cc_ready, 1)
            dve.wait_ge(x_done, KT)
            with dve.Fori(0, 16) as a:
                ada_store(a)
                x_f = X[:, bass.ds(a * T, T)]
                dve.tensor_tensor(h_f[:, 0], x_f, x_f, ALU.mult)
                dve.drain()
                dve.tensor_tensor(ssum[:], ssum[:], h_f[:, 0], ALU.add)
                ada_sum(a, M_START + a)
                dve.drain()
            dve.drain().then_inc(ss_ready, 1)
            mod_done(0, 0, 16)
            dve.drain()
            split(0, 0)
            split(0, 1)
            norm_rstd(0, M_START + 16, rstd[:], p_m[:, 0:T])
            h_tiles(0, 0)

            def rope(x, use):
                dve.wait_ge(m_ready, use + 1)
                lat, tmp = x[:, :, CTX:T], h_t[:, :, 0:LAT]
                dve.tensor_tensor(tmp, p_m[:].rearrange("p (a b) -> p a b", a=2), over2(sin[:], LAT),
                                  ALU.mult).then_inc(m_free, 1)
                dve.tensor_tensor(lat, lat, over2(cos[:], LAT), ALU.mult)
                dve.drain()
                dve.tensor_tensor(lat, lat, tmp, ALU.add).then_inc(rope_ready, 1)

            def maxima(n, j, is_a=True):
                dve.wait_ge(s_ready, 2 * n + j + 1)
                dve.memset(st[:, 0, 3:4], NEG)
                if not is_a:
                    dve.wait_ge(const_in, 16 * 17)
                for t in range(2):
                    dve.tensor_tensor_reduce(out=s[:, t * T:(t + 1) * T], in0=p_s[:, t, 0:T],
                                             in1=mask[:, t], scale=1.0, scalar=NEG, op0=ALU.add,
                                             op1=ALU.max, accum_out=st[:, 0, t:t + 1])
                dve.tensor_tensor_reduce(out=s[:, 2 * T:], in0=p_s[:, 0, T:T + CTX], in1=zero[:], scale=1.0,
                                         scalar=NEG, op0=ALU.add, op1=ALU.max, accum_out=st[:, 0, 2:3])
                dve.drain()
                dve.tensor_scalar(st[:, 1, 0:3], st[:, 0, 0:3], sink[:, bass.ds(2 * n + j, 1)], -1.0,
                                  ALU.max, ALU.mult).then_inc(negm_ready, 1)

            def denominators(n, j):
                dve.wait_ge(exp_done, 2 * n + j + 1)
                dve.tensor_tensor(st[:, 4, 0:3], st[:, 2, 0:3], st[:, 3, 0:3], ALU.add)
                dve.drain()
                dve.reciprocal(st[:, 5, 0:3], st[:, 4, 0:3]).then_inc(rcp_ready, 1)

            def z_gate(n, par):
                dve.wait_ge(z_tanh, n + 1)
                dve.scalar_tensor_tensor(out=zs[:], in0=zs[:], scalar=1.0,
                                         in1=acc[:, 2 * par:2 * par + 2, 0:T], op0=ALU.add, op1=ALU.mult)\
                    .then_inc(acc_free[par], 1)

            def y_mul(n, j, use):
                dve.wait_ge(m_ready, use + 1)
                dve.scalar_tensor_tensor(out=yf[:], in0=p_m[:, 0:T], scalar=0.5, in1=zs[:, j],
                                         op0=ALU.mult, op1=ALU.mult).then_inc(m_free, 1)

            def y_lo(n, j):
                dve.wait_ge(yh_ready, 2 * n + j + 1)
                at_ = bass.ds((2 * n + j) * T, T)
                dve.tensor_tensor(Y_lo[:, at_], yf[:], Y_hi[:, at_].bitcast(F32), ALU.subtract)\
                    .then_inc(y_ready, 1)

            def k_store(use):
                dve.wait_ge(m_ready, use + 1)
                dve.tensor_copy(k_out[:], p_m[:, 0:2 * P]).then_inc(m_free, 1)

            def ck_store(use):
                dve.wait_ge(m_ready, use + 1)
                dve.tensor_copy(ck[:], p_m[:, 0:2 * P]).then_inc(m_free, 1)

            for k_ in range(4, 14):
                split(0, k_)
                if k_ in (5, 9, 13):
                    ada_store(16 + (k_ - 5) // 4)
                if k_ == 6:
                    rope(k, M_FIRST)
                if k_ == 7:
                    ada_sum(16, M_FIRST + 1)
                if k_ == 8:
                    k_store(M_FIRST + 2)
                if k_ == 10:
                    ck_store(M_FIRST + 3)
                if k_ == 11:
                    ada_sum(17, M_FIRST + 4)

            def a_step(n):
                mb, use = 3 + 2 * n, M_A + 7 * n
                for k_ in range(2, 10):
                    split(mb, k_)
                    if k_ == 2:
                        rope(q, use)
                    if k_ == 3:
                        ada_sum(18 + 4 * n, use + 1)
                        ada_store(19 + 4 * n)
                        maxima(n, 0)
                    if k_ == 4:
                        denominators(n, 0)
                        ada_sum(19 + 4 * n, use + 2)
                    if k_ == 5:
                        z_gate(n, 1)
                        ada_store(20 + 4 * n)
                    if k_ == 6:
                        dve.drain()
                        y_mul(n, 0, use + 3)
                        maxima(n, 1)
                    if k_ == 7:
                        y_lo(n, 0)
                        denominators(n, 1)
                        ada_sum(20 + 4 * n, use + 4)
                        ada_store(21 + 4 * n)
                    if k_ == 8:
                        ada_sum(21 + 4 * n, use + 5)
                    if k_ == 9:
                        dve.drain()
                        y_mul(n, 1, use + 6)
                        y_lo(n, 1)
                        ada_store(22 + 4 * n)

            with dve.Fori(0, 3) as n:
                a_step(n)

            def b_step(n, is_a, last=False):
                i = n - 3
                mb, ab = 9 + 4 * i, 31 + 4 * i
                use = M_B + 1 if is_a else M_BLOOP + 8 * (n - 4)
                for k_ in range(2, 14 if last else 18):
                    split(mb, k_)
                    if k_ == 2 and is_a:
                        rope(q, M_B)
                    if k_ == 3:
                        ada_sum(ab - 1, use)
                        maxima(n, 0, is_a)
                    if k_ == 4:
                        denominators(n, 0)
                    if k_ == 5:
                        z_gate(n, 1)
                        ada_store(ab)
                    if k_ == 6:
                        dve.drain()
                        y_mul(n, 0, use + 1)
                        maxima(n, 1, is_a)
                    if k_ == 7:
                        y_lo(n, 0)
                        denominators(n, 1)
                        ada_sum(ab, use + 2)
                    if last:
                        if k_ == 7:
                            dve.memset(ssum[:], 0.0)
                            dve.drain()
                            mod_done(ADA_PAIRS * 2 // 3, 16, 3)
                            mod_done(ADA_PAIRS * 2 // 3 + 3, 31, 4)
                            mod_done(ADA_PAIRS * 2 // 3 + 7, 47, 1)
                            mod_done(ADA_PAIRS, 19, 12)
                            mod_done(ADA_PAIRS + 12, 35, 12)
                            dve.drain()
                        if k_ == 8:
                            y_mul(n, 1, use + 3)
                            y_lo(n, 1)
                        if k_ in (9, 13):
                            update(0, (k_ - 9) // 4, PAIR_WOUT0 + (k_ - 9) // 4, (k_ - 9) // 4, 0)
                        continue
                    if k_ == 9:
                        dve.drain()
                        y_mul(n, 1, use + 3)
                        y_lo(n, 1)
                        ada_store(ab + 1)
                    if k_ == 11:
                        ada_sum(ab + 1, use + 4)
                    if k_ == 12:
                        dve.wait_ge(ko_sent, 16 * (i + 1))
                        k_store(use + 5)
                    if k_ == 13:
                        ck_store(use + 6)
                        ada_store(ab + 2)
                    if k_ == 15:
                        ada_sum(ab + 2, use + 7)
                    if k_ == 17:
                        ada_store(ab + 3)

            mod_flat = mod[:].rearrange("p k c -> p (k c)")

            def update(layer, pr, m, par, sq0_):
                dve.wait_ge(w_used, 4 * m + 4)
                for j in range(2):
                    for c_, (lo, w) in enumerate(((0, CTX), (CTX, LAT))):
                        x_ = X[:, bass.ds((2 * pr + j) * T + lo, w)]
                        last = dve.scalar_tensor_tensor(
                            out=x_, in0=acc[:, 2 * par + j, lo:lo + w],
                            scalar=mod_flat[:, bass.ds(2 * ((3 * layer + 2) * KT + 2 * pr + j) + c_, 1)],
                            in1=x_, op0=ALU.mult, op1=ALU.add)
                last.then_inc(acc_free[par], 1)
                dve.wait_ge(sq_ready, sq0_ + pr + 1)
                for j in range(2):
                    dve.tensor_tensor(ssum[:], ssum[:], h_f[:, j], ALU.add)
                    dve.drain()

            b_step(3, True)
            with dve.Fori(4, 7) as n:
                b_step(n, False)
            b_step(7, False, last=True)
            with dve.Fori(1, 4) as p:
                for k_ in range(2, 10):
                    split(PAIR_WOUT0 + 2 * p, k_)
                    if k_ in (5, 9):
                        i = (k_ - 5) // 4
                        update(0, 2 * p + i, PAIR_WOUT0 + 2 * p + i, i, 0)
            dve.drain().then_inc(ss_ready, 1)

            norm_rstd(1, M_NORM1, rstd[:], p_m[:, 0:T])
            dve.memset(u_pad[:], 0.0)
            h_tiles(1, PAIR_GLU)

            def glu(p):
                dve.wait_ge(w_used, 4 * (PAIR_GLU + 2 * p) + 8)
                dve.wait_ge(acc_free[0], PAIR_GLU // 2 + p + 1)
                for j in range(2):
                    for lo, to, w in ((0, HALO, CTX), (CTX, 2 * HALO + CTX, LAT)):
                        last = dve.scalar_tensor_tensor(out=u_pad[:, j, to:to + w],
                                                        in0=th_g[:, j, lo:lo + w], scalar=1.0,
                                                        in1=acc[:, 2 + j, lo:lo + w], op0=ALU.add,
                                                        op1=ALU.mult)
                last.then_inc(acc_free[1], 1)

            def tap_steps(p):
                for j in range(2):
                    f = 2 * p + j
                    for tap in range(TAPS - POOL_TAPS):
                        w_ = taps[:, bass.ds(tap * KT + f, 1)]
                        if tap == 0:
                            dve.drain()
                            dve.tensor_scalar(conv_v[:, j], u_pad[:, j, 0:SPAN], w_,
                                              pvec[:, bass.ds(PV_DWB + f, 1)], ALU.mult, ALU.add)
                        else:
                            dve.drain()
                            dve.scalar_tensor_tensor(out=conv_v[:, j], in0=u_pad[:, j, tap:tap + SPAN],
                                                     scalar=w_, in1=conv_v[:, j], op0=ALU.mult, op1=ALU.add)
                        yield
                    dve.drain()
                    dve.wait_ge(pc_ready, f + 1)
                    for lo, frm, w in ((0, 0, CTX), (CTX, CTX + HALO, LAT)):
                        last = dve.tensor_tensor(C[:, bass.ds(f * T + lo, w)], conv_v[:, j, frm:frm + w],
                                                 conv_p[:, j, frm:frm + w], ALU.add)
                    last.then_inc(c_ready, 1)
                    yield

            def z_silu(j, par):
                dve.wait_ge(z_tanh, 8 + j + 1)
                dve.scalar_tensor_tensor(out=SZ[:, 2 * j * T:(2 * j + 2) * T].rearrange("p (a b) -> p a b", a=2),
                                         in0=zt[:], scalar=1.0, in1=acc[:, 2 * par:2 * par + 2, 0:T],
                                         op0=ALU.add, op1=ALU.mult).then_inc(acc_free[par], 1)

            for k_ in range(4, 10):
                split(PAIR_GLU, k_)
            glu(0)

            def conv_step(p, last=False):
                steps = tap_steps(p - 1)
                n = 2 * (TAPS - POOL_TAPS + 1)
                for k_ in range(2, 10):
                    split(PAIR_GLU + 2 * p, k_)
                    for _ in range(n * (k_ - 1) // 8 - n * (k_ - 2) // 8):
                        next(steps)
                    if last and k_ in (5, 9):
                        z_silu((k_ - 5) // 4, (k_ - 5) // 4)
                if not last:
                    glu(p)

            with dve.Fori(1, 8) as p:
                conv_step(p)
            dve.memset(ssum[:], 0.0)
            conv_step(8, last=True)

            def normed(f):
                tile = C[:, f * T:(f + 1) * T]
                dve.tensor_tensor(tile, tile, rstd[:], ALU.mult).then_inc(cn_ready, 1)

            def y2_tile(f):
                tile = C[:, f * T:(f + 1) * T]
                dve.wait_ge(v_ready, f + 1)
                dve.scalar_tensor_tensor(out=tile, in0=h_t[:, f % 2], scalar=1.0, in1=tile, op0=ALU.add,
                                         op1=ALU.mult)
                dve.drain()
                dve.scalar_tensor_tensor(out=h_f[:, f % 2], in0=tile, scalar=0.25, in1=SZ[:, f * T:(f + 1) * T],
                                         op0=ALU.mult, op1=ALU.mult).then_inc(y2_full, 1)
                if f + 1 < KT:
                    normed(f + 1)
                dve.wait_ge(y2h_ready, f + 1)
                dve.tensor_tensor(Y_lo[:, f * T:(f + 1) * T], h_f[:, f % 2],
                                  Y_hi[:, f * T:(f + 1) * T].bitcast(F32), ALU.subtract).then_inc(y2_done, 1)

            for p in range(9, 12):
                for k_ in range(2, 10):
                    split(PAIR_GLU + 2 * p, k_)
                    if p == 9 and k_ == 3:
                        dve.wait_ge(m_ready, M_LN + 1)
                        dve.tensor_copy(rstd[:], p_m[:, 0:T]).then_inc(m_free, 1)
                        dve.drain()
                    if p == 9 and k_ >= 4:
                        for f in CENTRE[k_ - 4]:
                            tile = C[:, f * T:(f + 1) * T]
                            dve.tensor_tensor(tile, tile, rstd[:], ALU.subtract).then_inc(cen_ready, 1)
                    if k_ in (5, 9):
                        z_silu(2 * (p - 8) + (k_ - 5) // 4, (k_ - 5) // 4)
                    if p == 10 and k_ == 3:
                        dve.drain()
                        norm_rstd(2, M_LN + 1, rstd[:], p_m[:, 0:T])
                        dve.drain()
                        normed(0)
                    if p == 10 and k_ >= 4:
                        y2_tile(k_ - 4)
                    if p == 11:
                        y2_tile(k_ + 4)

            def final_store(f, b):
                dve.wait_ge(ft_ready, f + 1)
                dve.tensor_copy(out_tok[:, :, bass.ds(f * P, P)],
                                p_s[:, b, 0:T].rearrange("p (a b) -> p a b", a=3)).then_inc(ft_out, 1)

            def out_step(p, first=False, last=False):
                for k_ in range(2, 10):
                    if not (last and k_ > 7):
                        split(PAIR_WOUT1 + 2 * p, k_)
                    if first and k_ < 4:
                        y2_tile(12 + k_)
                    if first and k_ == 4:
                        dve.memset(ssum[:], 0.0)
                        dve.drain()
                    if k_ in (3, 4) and not first:
                        final_store(4 * p - 2 + k_ - 3, k_ - 3)
                    if k_ in (7, 8):
                        final_store(4 * p + k_ - 7, k_ - 7)
                    if k_ in (5, 9):
                        i = (k_ - 5) // 4
                        update(1, 2 * p + i, PAIR_WOUT1 + 2 * p + i, i, 8)

            out_step(0, first=True)
            with dve.Fori(1, 3) as p:
                out_step(p)
            out_step(3, last=True)
            dve.drain().then_inc(ss_ready, 1)
            final_store(14, 0)
            final_store(15, 1)
            norm_rstd(3, M_FIN, small[:, 4:10], p_m[:, 0:6])
            dve.drain()
            for t in range(3):
                dve.tensor_scalar(out_tok[:, t], out_tok[:, t], small[:, 4 + 2 * t:5 + 2 * t], None,
                                  ALU.mult).then_inc(fs_ready, 1)

        @block.gpsimd
        def _(pool):
            def h_tiles(layer):
                pool.wait_ge(rs_ready, layer + 1)

                def two(i, wait=True):
                    for j in range(2):
                        f = 2 * i + j
                        if wait:
                            pool.wait_ge(hf_ready, layer * KT + f - 1)
                        pool.tensor_tensor(h_t[:, j], X[:, bass.ds(f * T, T)], rstd[:], ALU.mult)\
                            .then_inc(t_ready, 1)
                two(0, wait=False)
                with pool.Fori(1, 8) as i:
                    two(i)

            h_tiles(0)
            with pool.Fori(0, 8) as n:
                for j in range(2):
                    pool.wait_ge(rcp_ready, 2 * n + j + 1)
                    pool.tensor_tensor(s[:, 2 * T:], s[:, 2 * T:], st[:, 5, 2:3].broadcast_to([P, CTX]),
                                       ALU.mult)
                    for r in range(2):
                        cols = slice(r * T, (r + 1) * T)
                        last = pool.tensor_scalar(s[:, cols], s[:, cols], st[:, 5, r:r + 1], None, ALU.mult)
                    last.then_inc(probs_ready, 1)

            h_tiles(1)
            pool.memset(lsum[:], 0.0)
            pool.drain()

            def conv_step(p):
                for j in range(2):
                    for tap in range(1, POOL_TAPS):
                        i = j * POOL_TAPS + tap
                        pool.wait_ge(prod_ready, 2 * POOL_TAPS * p + i + 1)
                        if tap == 1:
                            pool.tensor_tensor(conv_p[:, j], tap_prod[:, (i - 1) % PRODS],
                                               tap_prod[:, i % PRODS], ALU.add).then_inc(prod_added, 2)
                        else:
                            pool.tensor_tensor(conv_p[:, j], conv_p[:, j], tap_prod[:, i % PRODS],
                                               ALU.add).then_inc(prod_added, 1)
                        pool.drain()
                    pool.drain().then_inc(pc_ready, 1)
                for j in range(2):
                    f = 2 * p + j
                    pool.wait_ge(c_ready, f + 1)
                    pool.tensor_tensor(lsum[:], lsum[:], C[:, bass.ds(f * T, T)], ALU.add)
                    pool.drain()

            with pool.Fori(0, 8) as p:
                conv_step(p)
            pool.drain().then_inc(ln_sum, 1)
            for f in range(KT):
                pool.wait_ge(lsq_ready, f + 1)
                pool.tensor_tensor(ssum[:], ssum[:], h_f[:, f % 2], ALU.add).then_inc(sq_summed, 1)
                pool.drain()
            pool.drain().then_inc(ss_ready, 1)


_INS = ["x_prompt", "x_sample", "cache_a_k", "cache_a_v", "cache_b_k", "cache_b_v", "c", "c_ctx", "ada_w",
        "ada_b", "norm_g", "attn_w_in", "attn_w_out", "a_sink", "b_rpb", "conv_w_in", "conv_dw",
        "conv_dw_b", "conv_ln_g", "conv_ln_b", "conv_w_out", "final_g"]
_OUTS = [(1, CTX, D), (1, LAT, D), (1, 1, CTX, A_KV, P), (1, 1, CTX, A_KV, P), (1, 1, CTX, B_HEADS, P),
         (1, 1, CTX, B_HEADS, P)]


def constants():
    eye = np.zeros((P, LAT), np.float32)
    eye[:, 0:P] = np.eye(P, dtype=np.float32)
    columns = np.arange(P)
    eye[columns, P + columns // GRID_W * GRID_W + GRID_W - 1 - columns % GRID_W] = 1.0
    turn = np.zeros((P, LAT), np.float32)
    q4 = P // 4
    for half in range(2):
        for i in range(q4):
            x1, x2 = 2 * half * q4 + i, (2 * half + 1) * q4 + i
            turn[x2, x1] = -1.0
            turn[x1, x2] = 1.0
    inv = np.float32(10000.0) ** (-np.arange(q4, dtype=np.float32) / np.float32(q4))
    t = np.arange(LAT)
    row = (t // GRID_W).astype(np.float32)[None] * inv[:, None]
    col = (t % GRID_W).astype(np.float32)[None] * inv[:, None]
    ang = np.concatenate([row, row, col, col], axis=0)
    rot = np.stack([eye, turn, np.cos(ang), np.sin(ang)]).astype(np.float32)
    mask = np.zeros((2, P, 2, T), np.float32)
    i, j = np.arange(P)[:, None], np.arange(P)[None, :]
    mask[0, :, 0, P:2 * P] = np.where(j <= i, 0.0, NEG)
    mask[0, :, 1, 0:P] = np.where(j >= i, 0.0, NEG)
    first = np.clip(columns % GRID_W - NB_KW // 2, 0, GRID_W - NB_KW)[:, None]
    key = np.arange(LAT)[None, :] % GRID_W
    mask[1, :, :, 0:LAT] = np.where((key >= first) & (key < first + NB_KW), 0.0, NEG)[:, None]
    return rot, mask


def kernel(**inputs):
    import concourse.bacc as _bacc
    from concourse.bass_utils import run_bass_kernel_spmd as _run

    nc = _bacc.Bacc("TRN2", target_bir_lowering=False, num_devices=1, dynamic_dma_scratch_size=64)
    arrays, args = {}, []
    given = {name: inputs[name] for name in _INS}
    given["const_rot"], given["const_mask"] = constants()
    for name, a in given.items():
        a = np.ascontiguousarray(a)
        arrays[f"in_{name}_dram"] = a
        args.append(nc.dram_tensor(f"in_{name}_dram", a.shape, mybir.dt.from_np(a.dtype),
                                   kind="ExternalInput").ap())
    for i, shape in enumerate(_OUTS):
        args.append(nc.dram_tensor(f"out_{i}_dram", shape, F32, kind="ExternalOutput").ap())
    hybrid_trunk(nc, *args)
    r = _run(nc, [arrays], core_ids=[0])
    return tuple(r.results[0][f"out_{i}_dram"] for i in range(len(_OUTS)))
```

```python
from contextlib import ExitStack

import numpy as np

import concourse.bass as bass
from concourse import mybir

F32 = mybir.dt.float32
F32R = mybir.dt.float32r
ALU = mybir.AluOpType
ACT = mybir.ActivationFunctionType
AX = mybir.AxisListType

P = 128
D = 2048
KT = D // P
CTX, LAT = 128, 256
T = CTX + LAT
A_HEADS, A_KV, B_HEADS = 8, 2, 8
A_W, KV_W, B_W = A_HEADS * P, A_KV * P, B_HEADS * P
COL_QA, COL_KA, COL_VA = 0, A_W, A_W + KV_W
COL_QB = A_W + 2 * KV_W
COL_KB, COL_VB, COL_Z = COL_QB + B_W, COL_QB + 2 * B_W, COL_QB + 3 * B_W
GRID_W, NB_KW, RPB_H, RPB_W = 64, 16, 15, 31
ROWS = LAT // GRID_W
TAPS = 31
HALO = TAPS // 2
PAD = HALO + CTX + HALO + LAT + HALO
SPAN = PAD - 2 * HALO
POOL_TAPS = 14
PRODS = 14
CENTRE = [(0, 1, 2), (3, 4, 5), (6, 7, 8), (9, 10, 11), (12, 13), (14, 15)]
EPS = 1e-6
SCALE = float(P) ** -0.5
NEG = -3.0e38
W2 = 256
BK = 4
RAW, SPLIT = 4, 2
ADA_PAIRS = 3 * D // W2
PAIR_WOUT0, PAIR_GLU, PAIR_Z, PAIR_WOUT1 = 26, 34, 50, 58


def hybrid_trunk(nc, x_prompt, x_sample, cache_a_k, cache_a_v, cache_b_k, cache_b_v, c, c_ctx, ada_w,
                 ada_b, norm_g, attn_w_in, attn_w_out, a_sink, b_rpb, conv_w_in, conv_dw, conv_dw_b,
                 conv_ln_g, conv_ln_b, conv_w_out, final_g, const_rot, const_mask,
                 y_prompt, y_sample, new_a_k, new_a_v, new_b_k, new_b_v):
    ctx = ExitStack()
    with ctx:
        def sb(name, shape, dt=F32, where=ctx):
            return where.enter_context(nc.sbuf_tensor(name, shape, dt))

        def sem(name):
            return ctx.enter_context(nc.semaphore(name))

        X = sb("residual", [P, KT * T])
        H_hi = sb("h_hi", [P, KT, T], F32R)
        H_lo = sb("h_lo", [P, KT, T], F32R)
        raw = sb("w_raw", [P, RAW, BK, W2])
        w_hi = sb("w_hi", [P, SPLIT, BK, W2], F32R)
        w_lo = sb("w_lo", [P, SPLIT, BK, W2], F32R)
        ident = sb("ident", [P, P])
        ones = sb("ones", [P, P])
        pvec = sb("pvec", [P, 224])
        taps = sb("taps", [P, TAPS * KT])
        mod_in = sb("mod_in", [P, 2 * 3 * KT, 2])
        mod = sb("mod", [P, 2 * 3 * KT, 2])
        gain = sb("gain", [P, KT, 2])
        ssum = sb("ssum", [P, T])
        rstd = sb("rstd", [P, T])
        small = sb("small", [P, 32])
        y_area = ExitStack()
        Y_hi = sb("y_hi", [P, KT * T], F32R, y_area)
        Y_lo = sb("y_lo", [P, KT * T], F32R, y_area)
        y_area.close()
        in_area = ExitStack()
        x_tok = sb("x_tok", [P, 3, D], F32, in_area)
        rows1 = sb("rows1", [P, P], F32, in_area)
        rows2 = sb("rows2", [P, P], F32, in_area)
        rows_dw = sb("rows_dw", [P, 4, P], F32, in_area)
        c_tanh = sb("c_tanh", [P, 32], F32, in_area)
        sq0 = sb("sq0", [P, 2, T], F32, in_area)
        in_area.close()
        glu_area = ExitStack()
        th_g = sb("tanh_g", [P, 2, T], F32, glu_area)
        u_pad = sb("u_pad", [P, 2, PAD], F32, glu_area)
        conv_v = sb("conv_v", [P, 2, SPAN], F32, glu_area)
        conv_p = sb("conv_p", [P, 2, SPAN], F32, glu_area)
        tap_prod = sb("tap_products", [P, PRODS, SPAN], F32, glu_area)
        glu_area.close()
        y_hold = sb("y_area", [P, 2 * KT * T])
        att = ExitStack()
        ada_raw = sb("ada_raw", [P, RAW, BK, W2], F32, att)
        cc = sb("cond", [P, KT, 32], F32, att)
        ada_row = sb("ada_row", [P, W2], F32, att)
        rot = sb("rot", [P, P], F32, att)
        cos = sb("cos", [P, LAT], F32, att)
        sin = sb("sin", [P, LAT], F32, att)
        sink = sb("sink", [P, A_HEADS + B_HEADS], F32, att)
        zero = sb("zero", [P, P], F32, att)
        q = sb("q", [P, 2, T], F32, att)
        k = sb("k", [P, 2, T], F32, att)
        v = sb("v", [P, 3, 2 * P], F32, att)
        ck_rows = sb("ck_rows", [P, 2 * P], F32, att)
        ck = sb("ck", [P, 2 * P], F32, att)
        cv = sb("cv", [P, 2 * P], F32, att)
        k_out = sb("k_out", [P, 2 * P], F32, att)
        flip = sb("flip", [P, P], F32, att)
        mask = sb("mask", [P, 2, T], F32, att)
        rpb = sb("rpb", [P, 2, 2, LAT], F32, att)
        s = sb("scores", [P, 2 * T + CTX], F32, att)
        pT = sb("probs_t", [P, 3 * LAT + CTX], F32, att)
        zs = sb("z_silu", [P, 2, T], F32, att)
        yf = sb("y_full", [P, T], F32, att)
        st = sb("softmax_stats", [P, 6, 4], F32, att)
        att.close()
        cnv = ExitStack()
        C = sb("conv_out", [P, KT * T], F32, cnv)
        SZ = sb("silu_z", [P, KT * T], F32, cnv)
        zt = sb("tanh_z", [P, 2, T], F32, cnv)
        lsum = sb("conv_sum", [P, T], F32, cnv)
        cnv.close()
        fin = ExitStack()
        out_tok = sb("out_tok", [P, 3, D], F32, fin)
        fin_g = sb("x_gained", [P, 2, T], F32, fin)
        fin.close()
        l_hold = sb("layer_area", [P, 2 * KT * T + 1248])
        h_t = sb("h_t", [P, 2, T])
        h_f = sb("h_f", [P, 2, T])

        acc = ctx.enter_context(nc.psum_tensor("acc", [P, 4, 512], F32))
        p_ada = ctx.enter_context(nc.psum_tensor("p_ada", [P, 512], F32))
        p_s = ctx.enter_context(nc.psum_tensor("p_s", [P, 2, 512], F32))
        p_m = ctx.enter_context(nc.psum_tensor("p_m", [P, 512], F32))

        PV_ADA_B, PV_C, PV_CCTX = 0, 96, 112
        PV_NORM, PV_FINAL, PV_DWB, PV_LNG, PV_LNB = 128, 160, 176, 192, 208

        const_in = sem("const_in"); x_in = sem("x_in")
        raw_in = [sem(f"raw_in{i}") for i in range(RAW)]
        ada_in = [sem(f"ada_in{i}") for i in range(RAW)]
        hi_ready = sem("hi_ready"); lo_ready = sem("lo_ready")
        w_used = sem("w_used")
        acc_free = [sem("acc_even_free"), sem("acc_odd_free")]
        ada_used = sem("ada_used"); ada_out = sem("ada_out")
        m_ready = sem("m_ready"); m_free = sem("m_free")
        par_t = sem("params_turned"); par_ready = sem("params_ready"); c_th = sem("cond_tanh")
        cc_ready = sem("cond_ready"); zeroed = sem("zeroed")
        xt_ready = sem("x_turned"); x_done = sem("x_stored"); xsq_ready = sem("x_squared")
        xsq_added = sem("x_squares_added")
        ss_ready = sem("squares_summed"); rt_ready = sem("root_ready"); rs_ready = sem("rstd_ready")
        t_ready = sem("normed"); hf_ready = sem("h_full"); hh_ready = sem("h_hi_ready")
        h_ready = sem("h_ready")
        rope_ready = sem("roped"); s_ready = sem("scores_ready"); negm_ready = sem("negmax_ready")
        exp_done = sem("exp_done"); rcp_ready = sem("rcp_ready"); probs_ready = sem("probs_ready")
        pt_ready = sem("probs_turned"); pt_out = sem("probs_t_stored")
        z_tanh = sem("z_tanh"); yh_ready = sem("y_hi_ready"); y_ready = sem("y_ready")
        ck_in = sem("ck_in"); cv_in = sem("cv_in"); rpb_in = sem("rpb_in")
        ko_sent = sem("k_out_sent"); v_sent = sem("v_sent")
        th_ready = sem("tanh_g_ready"); u_ready = sem("u_ready"); pc_ready = sem("pool_taps_ready")
        prod_ready = sem("tap_products_ready"); prod_added = sem("tap_products_added")
        c_ready = sem("conv_ready"); pc_summed = sem("conv_summed")
        ln_sum = sem("ln_summed"); cen_ready = sem("centred"); sq_ready = sem("squared")
        cn_ready = sem("ln_normed"); v_ready = sem("ln_affine"); y2_full = sem("y2_full")
        y2h_ready = sem("y2_hi"); y2_done = sem("y2_ready"); lsq_ready = sem("ln_squares")
        sq_summed = sem("ln_squares_summed")
        xs_ready = sem("x_updated"); fg_ready = sem("final_gained"); ft_ready = sem("final_turned")
        ft_out = sem("final_stored"); fs_ready = sem("final_scaled"); y_sent = sem("y_sent")

        w_in0 = attn_w_in[0].rearrange("(k p) n -> p k n", p=P)
        w_out0 = attn_w_out[0].rearrange("(k p) n -> p k n", p=P)
        w_in1 = conv_w_in[0].rearrange("(k p) n -> p k n", p=P)
        w_out1 = conv_w_out[0].rearrange("(k p) n -> p k n", p=P)
        w_ada = [ada_w[i].rearrange("(k p) n -> p k n", p=P) for i in range(2)]

        M_NORM0 = 2
        M_FIRST = 16 + 1
        M_A = M_FIRST + 3
        M_B = M_A + 3 * 7
        M_BLOOP = M_B + 9
        M_LAST = M_BLOOP + 3 * 8
        M_NORM1 = M_LAST + 6
        M_LN = M_NORM1 + 1
        M_FIN = M_LN + 2

        def m_of_ada(a):
            return a if a < M_NORM0 else a + 1

        def at(e, sm, n):
            if not isinstance(n, int) or n > 0:
                e.wait_ge(sm, n)

        def evacuated(e, par, half):
            e.wait_ge(acc_free[par], half + 1)

        block = ctx.enter_context(nc.Block())

        @block.sync
        def _(sp):
            consts = [(ident[:], const_rot[0, :, 0:P]), (rot[:], const_rot[1, :, 0:P]),
                      (flip[:], const_rot[0, :, P:]),
                      (cos[:], const_rot[2]), (sin[:], const_rot[3]),
                      (rows1[0:96], ada_b.rearrange("l (r f) -> (l r) f", f=P)),
                      (rows1[96:112], c.rearrange("b (r f) -> (b r) f", f=P)),
                      (rows1[112:128], c_ctx.rearrange("(r f) -> r f", f=P)),
                      (rows2[0:32], norm_g.rearrange("l (r f) -> (l r) f", f=P)),
                      (rows2[32:48], final_g.rearrange("(r f) -> r f", f=P)),
                      (rows2[48:64], conv_dw_b.rearrange("l (r f) -> (l r) f", f=P)),
                      (rows2[64:80], conv_ln_g.rearrange("l (r f) -> (l r) f", f=P)),
                      (rows2[80:96], conv_ln_b.rearrange("l (r f) -> (l r) f", f=P)),
                      (rows_dw[0:124], conv_dw[0].rearrange("k (r f) -> (k r) f", f=P)
                       .rearrange("(a b) f -> b a f", b=124)),
                      (sink[:, 0:A_HEADS], a_sink.broadcast_to([P, A_HEADS])),
                      (mask[:], const_mask[0])]
            assert len(consts) == 16
            for dst, src in consts:
                sp.dma_start(dst, src).then_inc(const_in, 16)
            sp.dma_start(x_tok[:, 0], x_prompt[0]).then_inc(x_in, 16)
            for j in range(2):
                sp.dma_start(x_tok[:, 1 + j], x_sample[0, j * P:(j + 1) * P]).then_inc(x_in, 16)

            def ada(a, src, col, first=False):
                for s_ in range(BK):
                    ada_block(a, s_, src, col, first)

            def ada_block(a, s_, src, col, first=False):
                if not first:
                    sp.wait_ge(ada_used, 4 * a + s_ - 3)
                sp.dma_start(ada_raw[:, s_], src[:, BK * s_:BK * s_ + BK, bass.ds(col, W2)])\
                    .then_inc(ada_in[s_], 16)

            def w_block(m, s_, src, col, first=False):
                if not first:
                    sp.wait_ge(lo_ready, 4 * m + s_ - 3)
                sp.dma_start(raw[:, s_], src[:, BK * s_:BK * s_ + BK, bass.ds(col, W2)])\
                    .then_inc(raw_in[s_], 16)

            def first_block(b, first=False):
                if not first:
                    sp.wait_ge(lo_ready, b - 3)
                kt, col = BK * (b // 2), (COL_KA, COL_VA)[b % 2]
                sp.dma_start(raw[:, b % RAW], w_in0[:, kt:kt + BK, col:col + W2]).then_inc(raw_in[b % RAW], 16)

            ada(0, w_ada[0], 0, first=True)
            for b in range(4):
                first_block(b, first=True)
            ada(1, w_ada[0], D)
            for t0, t1, blocks in ((1, 2, (4, 5)), (2, 6, (6, 7)), (6, 8, ())):
                with sp.Fori(t0, t1) as t:
                    ada(2 * t, w_ada[0], t * W2)
                    ada(2 * t + 1, w_ada[0], D + t * W2)
                for b in blocks:
                    first_block(b)

            def pairs(m, cols, src, ada_of=lambda t: [], small_of=lambda t: None):
                for t in range(4 * len(cols)):
                    w_block(m + t // 4, t % 4, src, cols[t // 4])
                    for a in ada_of(t):
                        ada_block(*a)
                    small_of(t)

            sp.dma_start(ck_rows[:], cache_a_k[0, 0].rearrange("s h d -> s (h d)")).then_inc(ck_in, 16)
            sp.dma_start(cv[:], cache_a_v[0, 0].rearrange("s h d -> s (h d)")).then_inc(cv_in, 16)
            g0 = 2 * D
            pairs(2, [COL_QA], w_in0, lambda t: [(16, t, w_ada[0], g0)])

            def kv_out(m_free_n, half, k_to, v_to):
                sp.wait_ge(m_free, m_free_n)
                sp.dma_start(k_to, k_out[:]).then_inc(ko_sent, 16)
                sp.wait_ge(acc_free[1], half + 1)
                sp.dma_start(v_to, v[:, 0]).then_inc(v_sent, 16)

            kv_out(M_FIRST + 2, 0, new_a_k[0, 0].rearrange("s h d -> s (h d)"),
                   new_a_v[0, 0].rearrange("s h d -> s (h d)"))

            def a_step(n):
                pairs(3 + 2 * n, [COL_Z + W2 * n, COL_QA + W2 * (n + 1)], w_in0,
                      lambda t: [(17 + 4 * n + t // 2, 2 * (t % 2) + j, w_ada[1], (4 * n + t // 2) * W2)
                                 for j in range(2)])

            with sp.Fori(0, 3) as n:
                a_step(n)

            def heads(x, i):
                return x[0, 0, :, bass.ds(2 * i, 2)].rearrange("s h d -> s (h d)")

            rpb_flat = b_rpb.rearrange("l h r c -> (l h r c)")

            def small_loads(i):
                def at_tick(t):
                    if t == 8:
                        sp.wait_ge(m_free, M_FIRST + 3 if isinstance(i, int) else M_BLOOP + 8 * (i - 2) + 7)
                        sp.dma_start(ck_rows[:], heads(cache_b_k, i)).then_inc(ck_in, 16)
                    if t == 12:
                        sp.wait_ge(s_ready, 2 * (i + 3) + 2)
                        for j in range(2):
                            for qt in range(2):
                                for half in range(2):
                                    r = 2 * qt + half
                                    off = ((2 * i + j) * RPB_H + 7 - r) * RPB_W + NB_KW - GRID_W
                                    first = rpb_flat[bass.ds(off, 1)]
                                    src = bass.AP(first.tensor, first.offset,
                                                  [[1, GRID_W], [RPB_W, ROWS], [1, GRID_W]])
                                    dst = rpb[64 * half:64 * half + 64, j, qt]\
                                        .rearrange("p (r c) -> p r c", c=GRID_W)
                                    sp.dma_start(dst, src).then_inc(rpb_in, 16)
                        if isinstance(i, int) and i == 0:
                            sp.wait_ge(negm_ready, 2 * 4)
                            sp.dma_start(mask[:], const_mask[1]).then_inc(const_in, 16)
                    if t == 13:
                        sp.wait_ge(y_ready, 2 * (i + 3) + 2)
                        sp.dma_start(cv[:], heads(cache_b_v, i)).then_inc(cv_in, 16)
                return at_tick

            def b_loads(i, src, first_col):
                pairs(9 + 4 * i, [COL_Z + W2 * (i + 3), COL_KB + W2 * i, COL_VB + W2 * i,
                                  COL_QB + W2 * i], w_in0,
                      lambda t: [(29 + 4 * i + t // 4, t % 4, src, first_col + (t // 4) * W2)],
                      small_loads(i))
                kv_out(M_B + 7 if isinstance(i, int) else M_BLOOP + 8 * (i - 1) + 6, 5 + 2 * i,
                       heads(new_b_k, i), heads(new_b_v, i))

            b_loads(0, w_ada[0], g0 + W2)
            with sp.Fori(1, 4) as i:
                b_loads(i, w_ada[1], (8 + 4 * i) * W2)
            pairs(25, [COL_Z + 7 * W2], w_in0,
                  lambda t: [(45, t, w_ada[0], g0 + 5 * W2)])
            pairs(PAIR_WOUT0, [0], w_out0,
                  lambda t: [(46 + t // 2, 2 * (t % 2) + j, w_ada[0], g0 + (6 + t // 2) * W2)
                             for j in range(2)])
            with sp.Fori(1, 8) as j:
                pairs(PAIR_WOUT0 + j, [j * W2], w_out0)
            with sp.Fori(1, 9) as j:
                pairs(PAIR_GLU - 2 + 2 * j, [W2 * j + (D - W2), W2 * j - W2], w_in1)
            with sp.Fori(0, 8) as j:
                pairs(PAIR_Z + j, [2 * D + j * W2], w_in1)
            with sp.Fori(0, 8) as j:
                pairs(PAIR_WOUT1 + j, [j * W2], w_out1)
            outs = [y_prompt[0], y_sample[0, 0:P], y_sample[0, P:2 * P]]
            for i in range(3):
                sp.wait_ge(fs_ready, i + 1)
                sp.dma_start(outs[i], out_tok[:, i]).then_inc(y_sent, 16)
            sp.wait_ge(y_sent, 48)
            sp.wait_ge(ko_sent, 16 * 5)
            sp.wait_ge(v_sent, 16 * 5)

        @block.tensor
        def _(pe):
            def m_use(n):
                at(pe, m_free, n)

            def mm3(out, wh, wl, xh, xl, start, stop):
                pe.matmul(out, wh, xh, start=start, stop=False)
                pe.matmul(out, wh, xl, start=False, stop=False)
                return pe.matmul(out, wl, xh, start=False, stop=stop)

            def w_block(m, half, par, s_, kind="h", x_wait=None, number=None, tiles=range(BK)):
                if s_ == 0 and 0 in tiles:
                    at(pe, acc_free[par], half)
                b = number if number is not None else 4 * m + s_
                pe.wait_ge(lo_ready, b + 1)
                b = (s_ if number is None else number) % SPLIT
                for kk in tiles:
                    kt = BK * s_ + kk
                    if x_wait is not None:
                        pe.wait_ge(x_wait[0], x_wait[1] + kt + 1)
                    if kind == "v":
                        for t in range(3):
                            out = acc[:, 2 * par + t // 2, (t % 2) * W2:(t % 2) * W2 + W2]
                            xh, xl = (z[:, kt, t * P:(t + 1) * P] for z in (H_hi, H_lo))
                            pe.matmul(out, xh, w_hi[:, b, kk], start=(kt == 0 and t != 1), stop=False,
                                      skip_group_check=True)
                            pe.matmul(out, xh, w_lo[:, b, kk], start=False, stop=False,
                                      skip_group_check=True)
                            last = pe.matmul(out, xl, w_hi[:, b, kk], start=False, stop=(kt == KT - 1),
                                             skip_group_check=True)
                        continue
                    if kind == "h":
                        xh, xl = H_hi[:, kt], H_lo[:, kt]
                    else:
                        xh, xl = Y_hi[:, kt * T:(kt + 1) * T], Y_lo[:, kt * T:(kt + 1) * T]
                    for j in range(2):
                        cols = slice(j * P, (j + 1) * P)
                        last = mm3(acc[:, 2 * par + j, 0:T], w_hi[:, b, kk, cols], w_lo[:, b, kk, cols],
                                   xh, xl, kt == 0, kt == KT - 1)
                if BK - 1 in tiles:
                    last.then_inc(w_used, 1)

            def ada_block(a, s_):
                pe.wait_ge(ada_in[s_], 16 * (a + 1))
                if s_ == 0:
                    at(pe, ada_out, a)
                for g in range(4):
                    last = pe.matmul(p_ada[32 * g:32 * g + 32, 0:W2], cc[:, BK * s_ + g],
                                     ada_raw[:, s_, g], start=(s_ == 0), stop=(s_ == 3),
                                     tile_position=(0, 32 * g))
                last.then_inc(ada_used, 1)

            def ada_turn(a, use):
                pe.wait_ge(ada_out, a + 1)
                m_use(use)
                for j in range(2):
                    last = pe.transpose(p_m[:, j * P:(j + 1) * P], ada_row[:, j * P:(j + 1) * P], ident[:])
                last.then_inc(m_ready, 1)

            pe.wait_ge(const_in, 256)
            pe.transpose(p_s[:, 0, 0:P], rows1[:], ident[:])
            pe.transpose(p_s[:, 0, P:P + 96], rows2[0:96], ident[0:96, 0:96])
            for i in range(4):
                last = pe.transpose(p_s[:, 1, 124 * i:124 * i + 124], rows_dw[0:124, i],
                                    ident[0:124, 0:124])
            last.then_inc(par_t, 1)
            pe.wait_ge(x_in, 48)
            for f in range(KT):
                at(pe, x_done, f - 3)
                for t in range(3):
                    last = pe.transpose(acc[:, f % 4, t * P:(t + 1) * P],
                                        x_tok[:, t, f * P:(f + 1) * P], ident[:])
                last.then_inc(xt_ready, 1)
            pe.wait_ge(cc_ready, 1)

            def norm_mean(n, use):
                pe.wait_ge(ss_ready, n + 1)
                m_use(use)
                pe.matmul(p_m[:, 0:T], ones[:], ssum[:], start=True, stop=True).then_inc(m_ready, 1)

            def first_block(b, tiles=range(BK)):
                w_block(b % 2, 0, b % 2, b // 2, "hv"[b % 2], (h_ready, 0), b, tiles)

            for s_ in range(4):
                for a in range(4 * s_, 4 * s_ + 4):
                    for i in range(BK):
                        ada_block(a, i)
                        unit = (4 * (a % 4) + i) // 2
                        if s_ > 0 and i % 2 == 1:
                            first_block(2 * s_ - 2 + unit // 4, [unit % 4])
                    ada_turn(a, m_of_ada(a))
                    if a == 1:
                        norm_mean(0, M_NORM0)
            first_block(6)
            first_block(7)

            def rotate(x, use):
                m_use(use)
                pe.matmul(p_m[:].rearrange("p (a b) -> p a b", a=2), rot[:], x[:, :, CTX:T],
                          start=True, stop=True).then_inc(m_ready, 1)

            def scores(n, j, kv, is_a=True):
                at(pe, pt_out, 2 * n + j)
                pe.matmul(p_s[:, 0, T:T + CTX], q[:, j, 0:CTX], k[:, kv, 0:CTX], start=True, stop=True)
                for t in range(2):
                    lhs = q[:, j, CTX + t * P:CTX + (t + 1) * P]
                    pe.matmul(p_s[:, t, 0:LAT], lhs, k[:, kv, CTX:T], start=True, stop=is_a)
                    if not is_a:
                        pe.matmul(p_s[:, t, 0:LAT], flip[:], rpb[:, j, t], start=False, stop=True)
                    last = pe.matmul(p_s[:, t, LAT:LAT + P], lhs, ck[:, kv * P:(kv + 1) * P],
                                     start=True, stop=True)
                last.then_inc(s_ready, 1)

            def turn_probs(n, j):
                pe.wait_ge(probs_ready, 2 * n + j + 1)
                for t in range(2):
                    for kt in range(3):
                        pe.transpose(p_s[:, kt // 2, (kt % 2) * LAT + t * P:(kt % 2) * LAT + (t + 1) * P],
                                     s[:, t * T + kt * P:t * T + (kt + 1) * P], ident[:])
                pe.transpose(p_s[:, 1, LAT:LAT + P], s[:, 2 * T:2 * T + CTX], ident[:])\
                    .then_inc(pt_ready, 1)

            def attend(n, j, kv, use):
                pe.wait_ge(pt_out, 2 * n + j + 1)
                m_use(use)
                vs = slice(kv * P, (kv + 1) * P)
                pe.matmul(p_m[:, 0:CTX], v[:, 0, vs], pT[:, 3 * LAT:3 * LAT + CTX], start=True, stop=True)
                pe.matmul(p_m[:, CTX:T], v[:, 1, vs], pT[:, 0:LAT], start=True, stop=False)
                pe.matmul(p_m[:, CTX:T], v[:, 2, vs], pT[:, LAT:2 * LAT], start=False, stop=False)
                pe.matmul(p_m[:, CTX:T], cv[:, vs], pT[:, 2 * LAT:3 * LAT], start=False, stop=True)\
                    .then_inc(m_ready, 1)

            def turn_k(use):
                m_use(use)
                for j in range(2):
                    last = pe.transpose(p_m[:, j * P:(j + 1) * P], k[:, j, 0:CTX], ident[:])
                last.then_inc(m_ready, 1)

            def turn_ck(i, use):
                pe.wait_ge(ck_in, 16 * (i + 1))
                m_use(use)
                for j in range(2):
                    last = pe.transpose(p_m[:, j * P:(j + 1) * P], ck_rows[:, j * P:(j + 1) * P], ident[:])
                last.then_inc(m_ready, 1)

            for t in range(4):
                w_block(2, 1, 0, t)
                ada_block(16, t)
                if t == 0:
                    evacuated(pe, 0, 0)
                    rotate(k, M_FIRST)
                if t == 1:
                    turn_k(M_FIRST + 1)
                if t == 2:
                    turn_ck(0, M_FIRST + 2)

            def a_step(n, kv):
                use = M_A + 7 * n
                for t in range(8):
                    i, s_ = t // 4, t % 4
                    m = 3 + 2 * n + i
                    w_block(m, 1 + n + i, 1 - i, s_)
                    for j in range(2):
                        ada_block(17 + 4 * n + t // 2, 2 * (t % 2) + j)
                    if t == 0:
                        evacuated(pe, 0, 1 + n)
                        rotate(q, use)
                    if t == 1:
                        pe.wait_ge(rope_ready, n + 2)
                        scores(n, 0, kv)
                        ada_turn(16 + 4 * n, use + 1)
                    if t == 2:
                        ada_turn(17 + 4 * n, use + 2)
                    if t == 3:
                        turn_probs(n, 0)
                    if t == 4:
                        pe.wait_ge(cv_in, 16)
                        attend(n, 0, kv, use + 3)
                        scores(n, 1, kv)
                    if t == 5:
                        ada_turn(18 + 4 * n, use + 4)
                    if t == 6:
                        turn_probs(n, 1)
                        ada_turn(19 + 4 * n, use + 5)
                    if t == 7:
                        attend(n, 1, kv, use + 6)

            a_step(0, 0)
            a_step(1, 0)
            a_step(2, 1)

            def b_step(n, is_a, last=False):
                i = n - 3
                use = (M_B if is_a else M_BLOOP + 8 * (n - 4)) + (1 if is_a else 0)
                ab = 29 + 4 * i
                kvs = (1, 1) if is_a else (0, 1)
                for t in range(12 if last else 16):
                    pi, s_ = t // 4, t % 4
                    m, half, par = 9 + 4 * i + pi, 4 + 2 * i + (pi + 1) // 2, 1 - pi % 2
                    if last and pi > 0:
                        w_block(m, half, par, s_, "y", (y_ready, 0) if pi == 1 else None)
                    else:
                        w_block(m, half, par, s_, "v" if pi == 2 else "h")
                    if not last or pi == 0:
                        ada_block(ab + pi, s_)
                    elif pi == 1:
                        for j in range(2):
                            ada_block(ab + 1 + s_ // 2, 2 * (s_ % 2) + j)
                    if t == 0 and is_a:
                        evacuated(pe, 0, 1 + n)
                        rotate(q, M_B)
                    if t == 1:
                        if is_a:
                            pe.wait_ge(rope_ready, n + 2)
                        else:
                            evacuated(pe, 0, 4 + 2 * i)
                            pe.wait_ge(rpb_in, 128 * i)
                        scores(n, 0, kvs[0], is_a)
                        ada_turn(ab - 1, use)
                    if t == 3:
                        turn_probs(n, 0)
                    if t == 4:
                        if not is_a:
                            pe.wait_ge(cv_in, 16 * (i + 1))
                        attend(n, 0, kvs[0], use + 1)
                        scores(n, 1, kvs[1], is_a)
                    if t == 5:
                        ada_turn(ab, use + 2)
                    if t == 6:
                        turn_probs(n, 1)
                        if last:
                            attend(n, 1, kvs[1], use + 3)
                            ada_turn(ab + 1, use + 4)
                    if last:
                        if t == 8:
                            ada_turn(ab + 2, use + 5)
                        continue
                    if t == 7:
                        attend(n, 1, kvs[1], use + 3)
                    if t == 9:
                        ada_turn(ab + 1, use + 4)
                    if t == 10:
                        evacuated(pe, 0, 5 + 2 * i)
                        turn_k(use + 5)
                    if t == 11:
                        turn_ck(i + 1, use + 6)
                    if t == 13:
                        ada_turn(ab + 2, use + 7)

            b_step(3, True)
            with pe.Fori(4, 7) as n:
                b_step(n, False)
            b_step(7, False, last=True)

            with pe.Fori(1, 4) as p:
                for t in range(8):
                    i, s_ = t // 4, t % 4
                    w_block(PAIR_WOUT0 + 2 * p + i, PAIR_WOUT0 // 2 + p, i, s_, "y")

            norm_mean(1, M_NORM1)

            def two_pairs(p, x_wait=None):
                for t in range(8):
                    i, s_ = t // 4, t % 4
                    w_block(PAIR_GLU + 2 * p + i, PAIR_GLU // 2 + p, i, s_, "h", x_wait if i == 0 else None)
                    if isinstance(p, int) and p == 9 and t == 1:
                        pe.wait_ge(ln_sum, 1)
                        m_use(M_LN)
                        pe.matmul(p_m[:, 0:T], ones[:], lsum[:], start=True, stop=True).then_inc(m_ready, 1)
                    if isinstance(p, int) and p == 10 and t == 1:
                        norm_mean(2, M_LN + 1)

            two_pairs(0, (h_ready, KT))
            with pe.Fori(1, 9) as p:
                two_pairs(p)
            two_pairs(9)
            two_pairs(10)
            two_pairs(11)

            def turn_final(f, b):
                pe.wait_ge(fg_ready, f + 1)
                at(pe, ft_out, f - 1 if isinstance(f, int) else f - 1)
                for t in range(3):
                    last = pe.transpose(p_s[:, b, t * P:(t + 1) * P], fin_g[:, b, t * P:(t + 1) * P],
                                        ident[:])
                last.then_inc(ft_ready, 1)

            def out_pairs(p, first=False):
                for t in range(8):
                    i, s_ = t // 4, t % 4
                    w_block(PAIR_WOUT1 + 2 * p + i, PAIR_WOUT1 // 2 + p, i, s_, "y",
                            (y2_done, 0) if first and i == 0 else None)
                    if t in (1, 2) and not first:
                        turn_final(4 * p - 2 + t - 1, t - 1)
                    if t in (5, 6):
                        turn_final(4 * p + t - 5, t - 5)

            out_pairs(0, first=True)
            with pe.Fori(1, 4) as p:
                out_pairs(p)
            turn_final(14, 0)
            turn_final(15, 1)
            pe.wait_ge(ss_ready, 4)
            m_use(M_FIN)
            for t in range(3):
                last = pe.matmul(p_m[:, 2 * t:2 * t + 2], ssum[:, t * P:(t + 1) * P], ones[:, 0:2],
                                 start=True, stop=True)
            last.then_inc(m_ready, 1)

        @block.scalar
        def _(act):
            def split(mb, k_):
                m, s_ = mb + k_ // 4, k_ % 4
                act.wait_ge(raw_in[s_], 16 * (m + 1))
                at(act, w_used, 4 * m + s_ - 1)
                act.activation(w_hi[:, s_ % SPLIT], raw[:, s_], ACT.Copy).then_inc(hi_ready, 1)

            def root(n, use, x):
                act.wait_ge(m_free, use + 1)
                act.activation(x, x, ACT.Sqrt).then_inc(rt_ready, 1)

            def h_two(layer, i):
                for j in range(2):
                    act.wait_ge(hf_ready, layer * KT + 2 * i + j + 1)
                    act.activation(H_hi[:].rearrange("p k t -> p (k t)")[:, bass.ds((2 * i + j) * T, T)],
                                   h_f[:, j], ACT.Copy).then_inc(hh_ready, 1)

            act.wait_ge(par_ready, 1)
            act.activation(c_tanh[:], pvec[:, PV_C:PV_C + 32], ACT.Tanh, scale=0.5).then_inc(c_th, 1)
            for f in range(KT):
                act.wait_ge(x_done, f + 1)
                at(act, xsq_added, f - 1)
                act.activation(sq0[:, f % 2], X[:, f * T:(f + 1) * T], ACT.Square).then_inc(xsq_ready, 1)
                if f in (6, 8):
                    split(0, (f - 6) // 2)
            root(0, M_NORM0, rstd[:])
            for t in range(8):
                h_two(0, t)
                if t > 1:
                    split(0, t)

            def take(par, mb_done, out, scale=1.0, blocks=4):
                act.wait_ge(w_used, 4 * mb_done + blocks)
                act.activation(out, acc[:, 2 * par:2 * par + 2, 0:T], ACT.Copy, scale=scale)\
                    .then_inc(acc_free[par], 1)

            def take_v(mb_done, n_sent):
                act.wait_ge(w_used, 4 * mb_done + 4)
                at(act, v_sent, n_sent)
                act.activation(v[:, 0:2].rearrange("p a b -> p (a b)"), acc[:, 2], ACT.Copy)
                act.activation(v[:, 2], acc[:, 3, 0:W2], ACT.Copy).then_inc(acc_free[1], 1)

            def exps(n, j):
                act.wait_ge(negm_ready, 2 * n + j + 1)
                for r in range(3):
                    cols = slice(r * T, r * T + (T if r < 2 else CTX))
                    act.activation(s[:, cols], s[:, cols], ACT.Exp, bias=st[:, 1, r:r + 1],
                                   accum_out=st[:, 2, r:r + 1])
                act.activation(st[:, 3, 0:3], st[:, 1, 0:3], ACT.Exp, bias=sink[:, bass.ds(2 * n + j, 1)])\
                    .then_inc(exp_done, 1)

            def store_pt(n, j):
                act.wait_ge(pt_ready, 2 * n + j + 1)
                act.activation(pT[:, 0:512], p_s[:, 0], ACT.Copy)
                act.activation(pT[:, 512:3 * LAT + CTX], p_s[:, 1, 0:T], ACT.Copy).then_inc(pt_out, 1)

            def y_hi(n, j, use):
                act.wait_ge(m_free, use + 1)
                act.activation(Y_hi[:, bass.ds((2 * n + j) * T, T)], yf[:], ACT.Copy).then_inc(yh_ready, 1)

            def z_gate(n, mb_done, par):
                act.wait_ge(w_used, 4 * mb_done + 4)
                act.activation(zs[:], acc[:, 2 * par:2 * par + 2, 0:T], ACT.Tanh, scale=0.5)\
                    .then_inc(z_tanh, 1)

            for k_ in range(8, 14):
                split(0, k_)
                if k_ == 8:
                    take(0, 0, k[:], blocks=7)
                if k_ == 9:
                    take_v(1, 0)
                if k_ == 13:
                    take(0, 2, q[:], SCALE)

            def a_step(n):
                mb, use = 3 + 2 * n, M_A + 7 * n
                for k_ in range(2, 10):
                    split(mb, k_)
                    if k_ == 3:
                        exps(n, 0)
                    if k_ == 5:
                        z_gate(n, mb, 1)
                        store_pt(n, 0)
                    if k_ == 6:
                        y_hi(n, 0, use + 3)
                        exps(n, 1)
                    if k_ == 8:
                        store_pt(n, 1)
                    if k_ == 9:
                        y_hi(n, 1, use + 6)
                        take(0, mb + 1, q[:], SCALE)

            with act.Fori(0, 3) as n:
                a_step(n)

            def b_step(n, is_a, last=False):
                i = n - 3
                mb, use = 9 + 4 * i, (M_B + 1 if is_a else M_BLOOP + 8 * (n - 4))
                for k_ in range(2, 14 if last else 18):
                    split(mb, k_)
                    if k_ == 3:
                        exps(n, 0)
                    if k_ == 5:
                        z_gate(n, mb, 1)
                        store_pt(n, 0)
                    if k_ == 6:
                        y_hi(n, 0, use + 1)
                        exps(n, 1)
                    if k_ == 8:
                        store_pt(n, 1)
                        if last:
                            y_hi(n, 1, use + 3)
                    if last:
                        if k_ in (9, 13):
                            squares((k_ - 9) // 4, (PAIR_WOUT0 + (k_ - 9) // 4) // 2, (k_ - 9) // 4)
                        continue
                    if k_ == 9:
                        y_hi(n, 1, use + 3)
                        take(0, mb + 1, k[:])
                    if k_ == 13:
                        take_v(mb + 2, 16 * (i + 1))
                    if k_ == 17:
                        take(0, mb + 3, q[:], SCALE)

            def squares(pr, half, par):
                act.wait_ge(acc_free[par], half + 1)
                act.activation(h_f[:].rearrange("p a b -> p (a b)"), X[:, bass.ds(2 * pr * T, 2 * T)],
                               ACT.Square).then_inc(sq_ready, 1)

            b_step(3, True)
            with act.Fori(4, 7) as n:
                b_step(n, False)
            b_step(7, False, last=True)
            with act.Fori(1, 4) as p:
                for k_ in range(2, 10):
                    split(PAIR_WOUT0 + 2 * p, k_)
                    if k_ in (5, 9):
                        i = (k_ - 5) // 4
                        squares(2 * p + i, PAIR_WOUT0 // 2 + p, i)

            root(1, M_NORM1, rstd[:])
            with act.Fori(0, 4) as i:
                h_two(1, i)
            split(PAIR_GLU, 2)
            with act.Fori(4, 6) as i:
                h_two(1, i)
            split(PAIR_GLU, 3)
            with act.Fori(6, 8) as i:
                h_two(1, i)

            def tanh_g(p):
                act.wait_ge(w_used, 4 * (PAIR_GLU + 2 * p) + 4)
                at(act, acc_free[1], PAIR_GLU // 2 + p)
                act.activation(th_g[:], acc[:, 0:2, 0:T], ACT.Tanh, scale=0.5).then_inc(acc_free[0], 1)

            def tanh_z(j, par):
                act.wait_ge(w_used, 4 * (PAIR_Z + j) + 4)
                at(act, acc_free[1 - par], (PAIR_Z + j + par) // 2)
                act.activation(zt[:], acc[:, 2 * par:2 * par + 2, 0:T], ACT.Tanh, scale=0.5)\
                    .then_inc(z_tanh, 1)

            def tap_products(p, part):
                for i in range(POOL_TAPS * part // 4, POOL_TAPS * (part + 1) // 4):
                    j, tap = i % 2, TAPS - POOL_TAPS + i // 2
                    if i == 0:
                        act.wait_ge(acc_free[1], PAIR_GLU // 2 + p + 1)
                    at(act, prod_added, 2 * POOL_TAPS * p + i + 1 - PRODS)
                    act.activation(tap_prod[:, i % PRODS], u_pad[:, j, tap:tap + SPAN], ACT.Copy,
                                   scale=taps[:, bass.ds(tap * KT + 2 * p + j, 1)]).then_inc(prod_ready, 1)

            for k_ in range(4, 10):
                split(PAIR_GLU, k_)
                if k_ == 5:
                    tanh_g(0)

            def glu_step(p):
                for k_ in range(2, 10):
                    split(PAIR_GLU + 2 * p, k_)
                    tap_products(p - 1, k_ - 2)
                    if k_ == 5:
                        tanh_g(p)

            glu_step(1)
            with act.Fori(2, 8) as p:
                glu_step(p)

            def centred_squares(tiles):
                for f in tiles:
                    act.wait_ge(cen_ready, f + 1)
                    if f >= PRODS:
                        act.wait_ge(sq_summed, f + 1 - PRODS)
                    act.activation(tap_prod[:, f % PRODS, 0:T], C[:, f * T:(f + 1) * T], ACT.Square)\
                        .then_inc(lsq_ready, 1)

            def ln_gate(f):
                tile = C[:, f * T:(f + 1) * T]
                act.wait_ge(cn_ready, f + 1)
                act.activation(tile, tile, ACT.Identity, scale=pvec[:, PV_LNG + f:PV_LNG + f + 1],
                               bias=pvec[:, PV_LNB + f:PV_LNB + f + 1])
                act.drain()
                at(act, y2_full, f - 1)
                act.activation(h_t[:, f % 2], tile, ACT.Tanh, scale=0.5).then_inc(v_ready, 1)

            def y2_hi(f):
                act.wait_ge(y2_full, f + 1)
                act.activation(Y_hi[:, f * T:(f + 1) * T], h_f[:, f % 2], ACT.Copy).then_inc(y2h_ready, 1)

            def y2_tile(f):
                if f > 0:
                    y2_hi(f - 1)
                if f + 1 < KT:
                    ln_gate(f + 1)

            for p in range(8, 12):
                for k_ in range(2, 10):
                    split(PAIR_GLU + 2 * p, k_)
                    if p == 8:
                        tap_products(7, k_ - 2)
                    if p == 9 and k_ >= 5:
                        centred_squares(CENTRE[k_ - 5])
                    if k_ in (5, 9):
                        tanh_z(2 * (p - 8) + (k_ - 5) // 4, (k_ - 5) // 4)
                    if p == 9 and k_ == 9:
                        centred_squares(CENTRE[5])
                    if p == 10 and k_ == 3:
                        root(2, M_LN + 1, rstd[:])
                        ln_gate(0)
                    if p == 10 and k_ >= 4:
                        y2_tile(k_ - 4)
                    if p == 11:
                        y2_tile(k_ + 4)

            def final_pair(pr, half, par):
                squares(pr, half, par)
                for j in range(2):
                    f = 2 * pr + j
                    at(act, ft_ready, f - 1)
                    act.activation(fin_g[:, j], X[:, bass.ds(f * T, T)], ACT.Copy,
                                   scale=pvec[:, bass.ds(PV_FINAL + f, 1)]).then_inc(fg_ready, 1)

            def out_step(p, first=False, last=False):
                for k_ in range(2, 10):
                    if not (last and k_ > 7):
                        split(PAIR_WOUT1 + 2 * p, k_)
                    if first and k_ < 4:
                        y2_tile(12 + k_)
                    if first and k_ == 3:
                        y2_hi(15)
                    if k_ in (5, 9):
                        i = (k_ - 5) // 4
                        final_pair(2 * p + i, PAIR_WOUT1 // 2 + p, i)

            out_step(0, first=True)
            with act.Fori(1, 3) as p:
                out_step(p)
            out_step(3, last=True)
            root(3, M_FIN, small[:, 4:10])

        @block.vector
        def _(dve):
            def split(mb, k_):
                m, s_ = mb + k_ // 4, k_ % 4
                dve.wait_ge(hi_ready, 4 * m + s_ + 1)
                dve.tensor_tensor(w_lo[:, s_ % SPLIT], raw[:, s_], w_hi[:, s_ % SPLIT].bitcast(F32),
                                  ALU.subtract).then_inc(lo_ready, 1)

            def over2(x, n):
                return x.unsqueeze(1).broadcast_to([P, 2, n])

            def ada_store(a):
                dve.wait_ge(ada_used, 4 * a + 4)
                dve.tensor_copy(ada_row[:], p_ada[:, 0:W2]).then_inc(ada_out, 1)

            def ada_sum(a, use):
                dve.wait_ge(m_ready, use + 1)
                dve.tensor_reduce(mod_in[:].rearrange("p f c -> p (f c)")[:, bass.ds(4 * a, 4)]
                                  .rearrange("p (f c) -> p f c", c=2),
                                  p_m[:, 0:2 * P].rearrange("p (f g c) -> p f c g", f=2, g=4)[:, :, 0:2, :],
                                  AX.X, ALU.add).then_inc(m_free, 1)

            def mod_done(pair, a, n):
                for c_ in range(2):
                    dve.tensor_tensor(mod[:, 2 * pair:2 * (pair + n), c_], mod_in[:, 2 * a:2 * (a + n), c_],
                                      pvec[:, PV_ADA_B + 2 * pair:PV_ADA_B + 2 * (pair + n)], ALU.add)

            def norm_rstd(n, use, out, src):
                dve.wait_ge(m_ready, use + 1)
                dve.tensor_scalar(out, src, EPS, None, ALU.add).then_inc(m_free, 1)
                dve.wait_ge(rt_ready, n + 1)
                dve.reciprocal(out, out).then_inc(rs_ready, 1)

            gain_f = gain[:].rearrange("p k c -> p (k c)")
            mod_f = mod[:].rearrange("p k c -> p (k c)")

            def gains(f, n, src, layer):
                dve.scalar_tensor_tensor(
                    out=gain[:, bass.ds(f, n)], in0=src, scalar=1.0,
                    in1=pvec[:, bass.ds(PV_NORM + layer * KT + f, n)].unsqueeze(2).broadcast_to([P, n, 2]),
                    op0=ALU.add, op1=ALU.mult)

            def h_two(layer, i):
                base = 3 * KT * layer
                dve.drain()
                for j in range(2):
                    f = 2 * i + j
                    dve.wait_ge(t_ready, layer * KT + f + 1)
                    for c_, cols in enumerate((slice(0, CTX), slice(CTX, T))):
                        last = dve.tensor_scalar(h_f[:, j, cols], h_t[:, j, cols],
                                                 gain_f[:, bass.ds(2 * f + c_, 1)],
                                                 mod_f[:, bass.ds(2 * (base + f) + c_, 1)],
                                                 ALU.mult, ALU.add)
                    last.then_inc(hf_ready, 1)
                for j in range(2):
                    f = 2 * i + j
                    dve.wait_ge(hh_ready, layer * KT + f + 1)
                    at_ = bass.ds(f * T, T)
                    dve.tensor_tensor(H_lo[:].rearrange("p k t -> p (k t)")[:, at_], h_f[:, j],
                                      H_hi[:].rearrange("p k t -> p (k t)")[:, at_].bitcast(F32),
                                      ALU.subtract).then_inc(h_ready, 1)

            dve.memset(cc[:], 0.0)
            dve.memset(ones[:], 1.0 / D)
            dve.memset(zero[:], 0.0)
            dve.memset(sink[:, A_HEADS:], NEG)
            dve.wait_ge(par_t, 1)
            dve.tensor_copy(pvec[:], p_s[:, 0, 0:224])
            dve.tensor_scalar(taps[:], p_s[:, 1, 0:TAPS * KT], 0.5, None, ALU.mult)
            dve.drain().then_inc(par_ready, 1)
            dve.wait_ge(c_th, 1)
            dve.scalar_tensor_tensor(out=c_tanh[:], in0=c_tanh[:], scalar=1.0, in1=pvec[:, PV_C:PV_C + 32],
                                     op0=ALU.add, op1=ALU.mult)
            dve.drain()
            for col, src in ((0, 16), (1, 0)):
                last = dve.tensor_scalar(cc[:, :, col:col + 1], c_tanh[:, src:src + 16].unsqueeze(2), 0.5,
                                         None, ALU.mult)
            last.then_inc(cc_ready, 1)
            for f in range(KT):
                dve.wait_ge(xt_ready, f + 1)
                dve.tensor_copy(X[:, f * T:(f + 1) * T], acc[:, f % 4, 0:T]).then_inc(x_done, 1)
            for s_ in range(4):
                for i in range(2):
                    t = 2 * s_ + i
                    for a in (2 * t, 2 * t + 1):
                        ada_store(a)
                        ada_sum(a, m_of_ada(a))
                        if t == 0:
                            split(0, a)
                    if t == 0:
                        norm_rstd(0, M_NORM0, rstd[:], p_m[:, 0:T])
                    dve.drain()
                    for kind in range(2):
                        f = kind * KT + 2 * t
                        dve.tensor_tensor(mod[:, f:f + 2], mod_in[:, 4 * t + 2 * kind:4 * t + 2 * kind + 2],
                                          pvec[:, PV_ADA_B + f:PV_ADA_B + f + 2].unsqueeze(2)
                                          .broadcast_to([P, 2, 2]), ALU.add)
                    dve.drain()
                    gains(2 * t, 2, mod[:, KT + 2 * t:KT + 2 * t + 2], 0)
                    h_two(0, t)
                    if s_ > 0:
                        split(0, 2 * s_ + i)

            def rope(x, use):
                dve.wait_ge(m_ready, use + 1)
                lat, tmp = x[:, :, CTX:T], h_t[:, :, 0:LAT]
                dve.tensor_tensor(tmp, p_m[:].rearrange("p (a b) -> p a b", a=2), over2(sin[:], LAT),
                                  ALU.mult).then_inc(m_free, 1)
                dve.tensor_tensor(lat, lat, over2(cos[:], LAT), ALU.mult)
                dve.drain()
                dve.tensor_tensor(lat, lat, tmp, ALU.add).then_inc(rope_ready, 1)

            def maxima(n, j, is_a=True):
                dve.wait_ge(s_ready, 2 * n + j + 1)
                dve.memset(st[:, 0, 3:4], NEG)
                if not is_a:
                    dve.wait_ge(const_in, 16 * 17)
                for t in range(2):
                    dve.tensor_tensor_reduce(out=s[:, t * T:(t + 1) * T], in0=p_s[:, t, 0:T],
                                             in1=mask[:, t], scale=1.0, scalar=NEG, op0=ALU.add,
                                             op1=ALU.max, accum_out=st[:, 0, t:t + 1])
                dve.tensor_tensor_reduce(out=s[:, 2 * T:], in0=p_s[:, 0, T:T + CTX], in1=zero[:], scale=1.0,
                                         scalar=NEG, op0=ALU.add, op1=ALU.max, accum_out=st[:, 0, 2:3])
                dve.drain()
                dve.tensor_scalar(st[:, 1, 0:3], st[:, 0, 0:3], sink[:, bass.ds(2 * n + j, 1)], -1.0,
                                  ALU.max, ALU.mult).then_inc(negm_ready, 1)

            def denominators(n, j):
                dve.wait_ge(exp_done, 2 * n + j + 1)
                dve.tensor_tensor(st[:, 4, 0:3], st[:, 2, 0:3], st[:, 3, 0:3], ALU.add)
                dve.drain()
                dve.reciprocal(st[:, 5, 0:3], st[:, 4, 0:3]).then_inc(rcp_ready, 1)

            def z_gate(n, par):
                dve.wait_ge(z_tanh, n + 1)
                dve.scalar_tensor_tensor(out=zs[:], in0=zs[:], scalar=1.0,
                                         in1=acc[:, 2 * par:2 * par + 2, 0:T], op0=ALU.add, op1=ALU.mult)\
                    .then_inc(acc_free[par], 1)

            def y_mul(n, j, use):
                dve.wait_ge(m_ready, use + 1)
                dve.scalar_tensor_tensor(out=yf[:], in0=p_m[:, 0:T], scalar=0.5, in1=zs[:, j],
                                         op0=ALU.mult, op1=ALU.mult).then_inc(m_free, 1)

            def y_lo(n, j):
                dve.wait_ge(yh_ready, 2 * n + j + 1)
                at_ = bass.ds((2 * n + j) * T, T)
                dve.tensor_tensor(Y_lo[:, at_], yf[:], Y_hi[:, at_].bitcast(F32), ALU.subtract)\
                    .then_inc(y_ready, 1)

            def k_store(use):
                dve.wait_ge(m_ready, use + 1)
                dve.tensor_copy(k_out[:], p_m[:, 0:2 * P]).then_inc(m_free, 1)

            def ck_store(use):
                dve.wait_ge(m_ready, use + 1)
                dve.tensor_copy(ck[:], p_m[:, 0:2 * P]).then_inc(m_free, 1)

            for k_ in range(8, 14):
                split(0, k_)
                if k_ == 10:
                    rope(k, M_FIRST)
                if k_ == 11:
                    k_store(M_FIRST + 1)
                if k_ == 12:
                    ck_store(M_FIRST + 2)
                if k_ == 13:
                    ada_store(16)

            def a_step(n):
                mb, use = 3 + 2 * n, M_A + 7 * n
                for k_ in range(2, 10):
                    split(mb, k_)
                    if k_ == 2:
                        rope(q, use)
                    if k_ == 3:
                        ada_sum(16 + 4 * n, use + 1)
                        ada_store(17 + 4 * n)
                        maxima(n, 0)
                    if k_ == 4:
                        denominators(n, 0)
                        ada_sum(17 + 4 * n, use + 2)
                    if k_ == 5:
                        z_gate(n, 1)
                        ada_store(18 + 4 * n)
                    if k_ == 6:
                        dve.drain()
                        y_mul(n, 0, use + 3)
                        maxima(n, 1)
                    if k_ == 7:
                        y_lo(n, 0)
                        denominators(n, 1)
                        ada_sum(18 + 4 * n, use + 4)
                        ada_store(19 + 4 * n)
                    if k_ == 8:
                        ada_sum(19 + 4 * n, use + 5)
                    if k_ == 9:
                        dve.drain()
                        y_mul(n, 1, use + 6)
                        y_lo(n, 1)
                        ada_store(20 + 4 * n)

            with dve.Fori(0, 3) as n:
                a_step(n)

            def b_step(n, is_a, last=False):
                i = n - 3
                mb, ab = 9 + 4 * i, 29 + 4 * i
                use = M_B + 1 if is_a else M_BLOOP + 8 * (n - 4)
                for k_ in range(2, 14 if last else 18):
                    split(mb, k_)
                    if k_ == 2 and is_a:
                        rope(q, M_B)
                    if k_ == 3:
                        ada_sum(ab - 1, use)
                        maxima(n, 0, is_a)
                    if k_ == 4:
                        denominators(n, 0)
                    if k_ == 5:
                        z_gate(n, 1)
                        ada_store(ab)
                    if k_ == 6:
                        dve.drain()
                        y_mul(n, 0, use + 1)
                        maxima(n, 1, is_a)
                    if k_ == 7:
                        y_lo(n, 0)
                        denominators(n, 1)
                        ada_sum(ab, use + 2)
                    if last:
                        if k_ == 7:
                            dve.memset(ssum[:], 0.0)
                            dve.drain()
                            mod_done(ADA_PAIRS * 2 // 3, 16, 1)
                            mod_done(ADA_PAIRS * 2 // 3 + 1, 29, 4)
                            mod_done(ADA_PAIRS * 2 // 3 + 5, 45, 1)
                            mod_done(ADA_PAIRS, 17, 12)
                            mod_done(ADA_PAIRS + 12, 33, 12)
                            dve.drain()
                            ada_store(ab + 1)
                        if k_ == 8:
                            y_mul(n, 1, use + 3)
                            y_lo(n, 1)
                            ada_sum(ab + 1, use + 4)
                        if k_ == 9:
                            ada_store(ab + 2)
                        if k_ == 10:
                            ada_sum(ab + 2, use + 5)
                            dve.drain()
                            mod_done(ADA_PAIRS * 2 // 3 + 6, 46, 2)
                            dve.drain()
                        if k_ in (9, 13):
                            update(0, (k_ - 9) // 4, PAIR_WOUT0 + (k_ - 9) // 4, (k_ - 9) // 4, 0)
                        continue
                    if k_ == 9:
                        dve.drain()
                        y_mul(n, 1, use + 3)
                        y_lo(n, 1)
                        ada_store(ab + 1)
                    if k_ == 11:
                        ada_sum(ab + 1, use + 4)
                    if k_ == 12:
                        dve.wait_ge(ko_sent, 16 * (i + 1))
                        k_store(use + 5)
                    if k_ == 13:
                        ck_store(use + 6)
                        ada_store(ab + 2)
                    if k_ == 15:
                        ada_sum(ab + 2, use + 7)
                    if k_ == 17:
                        ada_store(ab + 3)

            mod_flat = mod[:].rearrange("p k c -> p (k c)")

            def update(layer, pr, m, par, sq0_):
                dve.wait_ge(w_used, 4 * m + 4)
                for j in range(2):
                    for c_, (lo, w) in enumerate(((0, CTX), (CTX, LAT))):
                        x_ = X[:, bass.ds((2 * pr + j) * T + lo, w)]
                        last = dve.scalar_tensor_tensor(
                            out=x_, in0=acc[:, 2 * par + j, lo:lo + w],
                            scalar=mod_flat[:, bass.ds(2 * ((3 * layer + 2) * KT + 2 * pr + j) + c_, 1)],
                            in1=x_, op0=ALU.mult, op1=ALU.add)
                last.then_inc(acc_free[par], 1)
                dve.wait_ge(sq_ready, sq0_ + pr + 1)
                for j in range(2):
                    dve.tensor_tensor(ssum[:], ssum[:], h_f[:, j], ALU.add)
                    dve.drain()

            b_step(3, True)
            with dve.Fori(4, 7) as n:
                b_step(n, False)
            b_step(7, False, last=True)
            with dve.Fori(1, 4) as p:
                for k_ in range(2, 10):
                    split(PAIR_WOUT0 + 2 * p, k_)
                    if k_ in (5, 9):
                        i = (k_ - 5) // 4
                        update(0, 2 * p + i, PAIR_WOUT0 + 2 * p + i, i, 0)
            dve.drain().then_inc(ss_ready, 1)

            norm_rstd(1, M_NORM1, rstd[:], p_m[:, 0:T])
            dve.memset(u_pad[:], 0.0)
            gains(0, KT, mod[:, 3 * KT + KT:3 * KT + 2 * KT], 1)
            with dve.Fori(0, 4) as i:
                h_two(1, i)
            split(PAIR_GLU, 2)
            with dve.Fori(4, 6) as i:
                h_two(1, i)
            split(PAIR_GLU, 3)
            with dve.Fori(6, 8) as i:
                h_two(1, i)

            def glu(p):
                dve.wait_ge(w_used, 4 * (PAIR_GLU + 2 * p) + 8)
                dve.wait_ge(acc_free[0], PAIR_GLU // 2 + p + 1)
                for j in range(2):
                    for lo, to, w in ((0, HALO, CTX), (CTX, 2 * HALO + CTX, LAT)):
                        last = dve.scalar_tensor_tensor(out=u_pad[:, j, to:to + w],
                                                        in0=th_g[:, j, lo:lo + w], scalar=1.0,
                                                        in1=acc[:, 2 + j, lo:lo + w], op0=ALU.add,
                                                        op1=ALU.mult)
                last.then_inc(acc_free[1], 1)

            def tap_steps(p):
                for tap in range(TAPS - POOL_TAPS):
                    dve.drain()
                    for j in range(2):
                        f = 2 * p + j
                        w_ = taps[:, bass.ds(tap * KT + f, 1)]
                        if tap == 0:
                            dve.tensor_scalar(conv_v[:, j], u_pad[:, j, 0:SPAN], w_,
                                              pvec[:, bass.ds(PV_DWB + f, 1)], ALU.mult, ALU.add)
                        else:
                            dve.scalar_tensor_tensor(out=conv_v[:, j], in0=u_pad[:, j, tap:tap + SPAN],
                                                     scalar=w_, in1=conv_v[:, j], op0=ALU.mult, op1=ALU.add)
                        yield
                dve.drain()
                for j in range(2):
                    f = 2 * p + j
                    dve.wait_ge(pc_ready, p + 1)
                    for lo, frm, w in ((0, 0, CTX), (CTX, CTX + HALO, LAT)):
                        last = dve.tensor_tensor(C[:, bass.ds(f * T + lo, w)], conv_v[:, j, frm:frm + w],
                                                 conv_p[:, j, frm:frm + w], ALU.add)
                    last.then_inc(c_ready, 1)
                    yield

            def z_silu(j, par):
                dve.wait_ge(z_tanh, 8 + j + 1)
                dve.scalar_tensor_tensor(out=SZ[:, 2 * j * T:(2 * j + 2) * T].rearrange("p (a b) -> p a b", a=2),
                                         in0=zt[:], scalar=1.0, in1=acc[:, 2 * par:2 * par + 2, 0:T],
                                         op0=ALU.add, op1=ALU.mult).then_inc(acc_free[par], 1)

            for k_ in range(4, 10):
                split(PAIR_GLU, k_)
            glu(0)

            def conv_step(p, last=False):
                steps = tap_steps(p - 1)
                n = 2 * (TAPS - POOL_TAPS + 1)
                for k_ in range(2, 10):
                    split(PAIR_GLU + 2 * p, k_)
                    for _ in range(n * (k_ - 1) // 8 - n * (k_ - 2) // 8):
                        next(steps)
                    if last and k_ in (5, 9):
                        z_silu((k_ - 5) // 4, (k_ - 5) // 4)
                if not last:
                    glu(p)

            with dve.Fori(1, 8) as p:
                conv_step(p)
            dve.memset(ssum[:], 0.0)
            conv_step(8, last=True)

            def y2_lo(f):
                dve.wait_ge(y2h_ready, f + 1)
                dve.tensor_tensor(Y_lo[:, f * T:(f + 1) * T], h_f[:, f % 2],
                                  Y_hi[:, f * T:(f + 1) * T].bitcast(F32), ALU.subtract).then_inc(y2_done, 1)

            def y2_tile(f):
                tile = C[:, f * T:(f + 1) * T]
                dve.wait_ge(v_ready, f + 1)
                dve.scalar_tensor_tensor(out=tile, in0=h_t[:, f % 2], scalar=1.0, in1=tile, op0=ALU.add,
                                         op1=ALU.mult)
                dve.drain()
                dve.scalar_tensor_tensor(out=h_f[:, f % 2], in0=tile, scalar=0.25, in1=SZ[:, f * T:(f + 1) * T],
                                         op0=ALU.mult, op1=ALU.mult).then_inc(y2_full, 1)
                if f > 0:
                    y2_lo(f - 1)

            for p in range(9, 12):
                for k_ in range(2, 10):
                    split(PAIR_GLU + 2 * p, k_)
                    if p == 9 and k_ == 3:
                        dve.wait_ge(m_ready, M_LN + 1)
                        dve.tensor_copy(rstd[:], p_m[:, 0:T]).then_inc(m_free, 1)
                        dve.drain()
                    if p == 9 and k_ >= 4:
                        for f in CENTRE[k_ - 4]:
                            tile = C[:, f * T:(f + 1) * T]
                            dve.tensor_tensor(tile, tile, rstd[:], ALU.subtract).then_inc(cen_ready, 1)
                    if k_ in (5, 9):
                        z_silu(2 * (p - 8) + (k_ - 5) // 4, (k_ - 5) // 4)
                    if p == 10 and k_ == 3:
                        dve.drain()
                        norm_rstd(2, M_LN + 1, rstd[:], p_m[:, 0:T])
                    if p == 10 and k_ >= 4:
                        y2_tile(k_ - 4)
                    if p == 11:
                        y2_tile(k_ + 4)

            def final_store(f, b):
                dve.wait_ge(ft_ready, f + 1)
                dve.tensor_copy(out_tok[:, :, bass.ds(f * P, P)],
                                p_s[:, b, 0:T].rearrange("p (a b) -> p a b", a=3)).then_inc(ft_out, 1)

            def out_step(p, first=False, last=False):
                for k_ in range(2, 10):
                    if not (last and k_ > 7):
                        split(PAIR_WOUT1 + 2 * p, k_)
                    if first and k_ < 4:
                        y2_tile(12 + k_)
                    if first and k_ == 3:
                        y2_lo(15)
                    if first and k_ == 4:
                        dve.memset(ssum[:], 0.0)
                        dve.drain()
                    if k_ in (3, 4) and not first:
                        final_store(4 * p - 2 + k_ - 3, k_ - 3)
                    if k_ in (7, 8):
                        final_store(4 * p + k_ - 7, k_ - 7)
                    if k_ in (5, 9):
                        i = (k_ - 5) // 4
                        update(1, 2 * p + i, PAIR_WOUT1 + 2 * p + i, i, 8)

            out_step(0, first=True)
            with dve.Fori(1, 3) as p:
                out_step(p)
            out_step(3, last=True)
            dve.drain().then_inc(ss_ready, 1)
            final_store(14, 0)
            final_store(15, 1)
            norm_rstd(3, M_FIN, small[:, 4:10], p_m[:, 0:6])
            dve.drain()
            for t in range(3):
                dve.tensor_scalar(out_tok[:, t], out_tok[:, t], small[:, 4 + 2 * t:5 + 2 * t], None,
                                  ALU.mult).then_inc(fs_ready, 1)

        @block.gpsimd
        def _(pool):
            def h_tiles(layer):
                pool.wait_ge(rs_ready, layer + 1)

                def two(i, wait=True):
                    for j in range(2):
                        f = 2 * i + j
                        if wait:
                            pool.wait_ge(hf_ready, layer * KT + f - 1)
                        pool.tensor_tensor(h_t[:, j], X[:, bass.ds(f * T, T)], rstd[:], ALU.mult)\
                            .then_inc(t_ready, 1)
                two(0, wait=False)
                with pool.Fori(1, 8) as i:
                    two(i)

            pool.memset(ssum[:], 0.0)
            pool.drain()
            for f in range(KT):
                pool.wait_ge(xsq_ready, f + 1)
                pool.tensor_tensor(ssum[:], ssum[:], sq0[:, f % 2], ALU.add).then_inc(xsq_added, 1)
                pool.drain()
            pool.drain().then_inc(ss_ready, 1)
            h_tiles(0)
            with pool.Fori(0, 8) as n:
                for j in range(2):
                    pool.wait_ge(rcp_ready, 2 * n + j + 1)
                    pool.tensor_tensor(s[:, 2 * T:], s[:, 2 * T:], st[:, 5, 2:3].broadcast_to([P, CTX]),
                                       ALU.mult)
                    for r in range(2):
                        cols = slice(r * T, (r + 1) * T)
                        last = pool.tensor_scalar(s[:, cols], s[:, cols], st[:, 5, r:r + 1], None, ALU.mult)
                    last.then_inc(probs_ready, 1)

            h_tiles(1)
            pool.memset(lsum[:], 0.0)
            pool.drain()

            def conv_step(p):
                for tap in range(1, POOL_TAPS):
                    if tap > 1:
                        pool.drain()
                    for j in range(2):
                        i = 2 * tap + j
                        pool.wait_ge(prod_ready, 2 * POOL_TAPS * p + i + 1)
                        first = tap_prod[:, j] if tap == 1 else conv_p[:, j]
                        last = pool.tensor_tensor(conv_p[:, j], first, tap_prod[:, i % PRODS], ALU.add)
                        last.then_inc(prod_added, 3 if i == 3 else 1)
                pool.drain().then_inc(pc_ready, 1)
                for j in range(2):
                    f = 2 * p + j
                    pool.wait_ge(c_ready, f + 1)
                    pool.tensor_tensor(lsum[:], lsum[:], C[:, bass.ds(f * T, T)], ALU.add)
                    pool.drain()

            with pool.Fori(0, 8) as p:
                conv_step(p)
            pool.drain().then_inc(ln_sum, 1)
            for f in range(KT):
                pool.wait_ge(lsq_ready, f + 1)
                pool.tensor_tensor(ssum[:], ssum[:], tap_prod[:, f % PRODS, 0:T], ALU.add)\
                    .then_inc(sq_summed, 1)
                pool.drain()
            pool.drain().then_inc(ss_ready, 1)
            pool.wait_ge(rs_ready, 3)
            for f in range(KT):
                tile = C[:, f * T:(f + 1) * T]
                pool.tensor_tensor(tile, tile, rstd[:], ALU.mult).then_inc(cn_ready, 1)


_INS = ["x_prompt", "x_sample", "cache_a_k", "cache_a_v", "cache_b_k", "cache_b_v", "c", "c_ctx", "ada_w",
        "ada_b", "norm_g", "attn_w_in", "attn_w_out", "a_sink", "b_rpb", "conv_w_in", "conv_dw",
        "conv_dw_b", "conv_ln_g", "conv_ln_b", "conv_w_out", "final_g"]
_OUTS = [(1, CTX, D), (1, LAT, D), (1, 1, CTX, A_KV, P), (1, 1, CTX, A_KV, P), (1, 1, CTX, B_HEADS, P),
         (1, 1, CTX, B_HEADS, P)]


def constants():
    eye = np.zeros((P, LAT), np.float32)
    eye[:, 0:P] = np.eye(P, dtype=np.float32)
    columns = np.arange(P)
    eye[columns, P + columns // GRID_W * GRID_W + GRID_W - 1 - columns % GRID_W] = 1.0
    turn = np.zeros((P, LAT), np.float32)
    q4 = P // 4
    for half in range(2):
        for i in range(q4):
            x1, x2 = 2 * half * q4 + i, (2 * half + 1) * q4 + i
            turn[x2, x1] = -1.0
            turn[x1, x2] = 1.0
    inv = np.float32(10000.0) ** (-np.arange(q4, dtype=np.float32) / np.float32(q4))
    t = np.arange(LAT)
    row = (t // GRID_W).astype(np.float32)[None] * inv[:, None]
    col = (t % GRID_W).astype(np.float32)[None] * inv[:, None]
    ang = np.concatenate([row, row, col, col], axis=0)
    rot = np.stack([eye, turn, np.cos(ang), np.sin(ang)]).astype(np.float32)
    mask = np.zeros((2, P, 2, T), np.float32)
    i, j = np.arange(P)[:, None], np.arange(P)[None, :]
    mask[0, :, 0, P:2 * P] = np.where(j <= i, 0.0, NEG)
    mask[0, :, 1, 0:P] = np.where(j >= i, 0.0, NEG)
    first = np.clip(columns % GRID_W - NB_KW // 2, 0, GRID_W - NB_KW)[:, None]
    key = np.arange(LAT)[None, :] % GRID_W
    mask[1, :, :, 0:LAT] = np.where((key >= first) & (key < first + NB_KW), 0.0, NEG)[:, None]
    return rot, mask


def kernel(**inputs):
    import concourse.bacc as _bacc
    from concourse.bass_utils import run_bass_kernel_spmd as _run

    nc = _bacc.Bacc("TRN2", target_bir_lowering=False, num_devices=1, dynamic_dma_scratch_size=64)
    arrays, args = {}, []
    given = {name: inputs[name] for name in _INS}
    given["const_rot"], given["const_mask"] = constants()
    for name, a in given.items():
        a = np.ascontiguousarray(a)
        arrays[f"in_{name}_dram"] = a
        args.append(nc.dram_tensor(f"in_{name}_dram", a.shape, mybir.dt.from_np(a.dtype),
                                   kind="ExternalInput").ap())
    for i, shape in enumerate(_OUTS):
        args.append(nc.dram_tensor(f"out_{i}_dram", shape, F32, kind="ExternalOutput").ap())
    hybrid_trunk(nc, *args)
    r = _run(nc, [arrays], core_ids=[0])
    return tuple(r.results[0][f"out_{i}_dram"] for i in range(len(_OUTS)))
```

```python
from contextlib import ExitStack

import numpy as np

import concourse.bass as bass
from concourse import mybir

F32 = mybir.dt.float32
F32R = mybir.dt.float32r
ALU = mybir.AluOpType
ACT = mybir.ActivationFunctionType
AX = mybir.AxisListType

P = 128
D = 2048
KT = D // P
CTX, LAT = 128, 256
T = CTX + LAT
A_HEADS, A_KV, B_HEADS = 8, 2, 8
A_W, KV_W, B_W = A_HEADS * P, A_KV * P, B_HEADS * P
COL_QA, COL_KA, COL_VA = 0, A_W, A_W + KV_W
COL_QB = A_W + 2 * KV_W
COL_KB, COL_VB, COL_Z = COL_QB + B_W, COL_QB + 2 * B_W, COL_QB + 3 * B_W
GRID_W, NB_KW, RPB_H, RPB_W = 64, 16, 15, 31
ROWS = LAT // GRID_W
TAPS = 31
HALO = TAPS // 2
PAD = HALO + CTX + HALO + LAT + HALO
SPAN = PAD - 2 * HALO
POOL_TAPS = 15
PRODS = 15
CENTRE = [(0, 1, 2), (3, 4, 5), (6, 7, 8), (9, 10, 11), (12, 13), (14, 15)]
H_SPLITS = (None, None, 2, 3, None, 4, 5, None)
EPS = 1e-6
SCALE = float(P) ** -0.5
NEG = -3.0e38
W2 = 256
BK = 4
RAW, SPLIT = 4, 2
ADA_PAIRS = 3 * D // W2
PAIR_WOUT0, PAIR_GLU, PAIR_Z, PAIR_WOUT1 = 26, 34, 50, 58


def hybrid_trunk(nc, x_prompt, x_sample, cache_a_k, cache_a_v, cache_b_k, cache_b_v, c, c_ctx, ada_w,
                 ada_b, norm_g, attn_w_in, attn_w_out, a_sink, b_rpb, conv_w_in, conv_dw, conv_dw_b,
                 conv_ln_g, conv_ln_b, conv_w_out, final_g, const_rot, const_mask,
                 y_prompt, y_sample, new_a_k, new_a_v, new_b_k, new_b_v):
    ctx = ExitStack()
    with ctx:
        def sb(name, shape, dt=F32, where=ctx):
            return where.enter_context(nc.sbuf_tensor(name, shape, dt))

        def sem(name):
            return ctx.enter_context(nc.semaphore(name))

        X = sb("residual", [P, KT * T])
        H_hi = sb("h_hi", [P, KT, T], F32R)
        H_lo = sb("h_lo", [P, KT, T], F32R)
        raw = sb("w_raw", [P, RAW, BK, W2])
        w_hi = sb("w_hi", [P, SPLIT, BK, W2], F32R)
        w_lo = sb("w_lo", [P, SPLIT, BK, W2], F32R)
        ident = sb("ident", [P, P])
        ones = sb("ones", [P, P])
        pvec = sb("pvec", [P, 224])
        taps = sb("taps", [P, TAPS * KT])
        mod_in = sb("mod_in", [P, 2 * 3 * KT, 2])
        mod = sb("mod", [P, 2 * 3 * KT, 2])
        gain = sb("gain", [P, KT, 2])
        ssum = sb("ssum", [P, T])
        rstd = sb("rstd", [P, T])
        small = sb("small", [P, 32])
        y_area = ExitStack()
        Y_hi = sb("y_hi", [P, KT * T], F32R, y_area)
        Y_lo = sb("y_lo", [P, KT * T], F32R, y_area)
        y_area.close()
        in_area = ExitStack()
        x_tok = sb("x_tok", [P, 3, D], F32, in_area)
        rows1 = sb("rows1", [P, P], F32, in_area)
        rows2 = sb("rows2", [P, P], F32, in_area)
        rows_dw = sb("rows_dw", [P, 4, P], F32, in_area)
        c_tanh = sb("c_tanh", [P, 32], F32, in_area)
        sq0 = sb("sq0", [P, 2, T], F32, in_area)
        in_area.close()
        glu_area = ExitStack()
        th_g = sb("tanh_g", [P, 2, T], F32, glu_area)
        u_pad = sb("u_pad", [P, 4, PAD], F32, glu_area)
        conv_v = sb("conv_v", [P, 4, SPAN], F32, glu_area)
        conv_p = sb("conv_p", [P, 4, SPAN], F32, glu_area)
        tap_prod = sb("tap_products", [P, PRODS, SPAN], F32, glu_area)
        glu_area.close()
        sb("y_area", [P, 2 * KT * T])
        att = ExitStack()
        ada_raw = sb("ada_raw", [P, RAW, BK, W2], F32, att)
        cc = sb("cond", [P, KT, 32], F32, att)
        ada_row = sb("ada_row", [P, W2], F32, att)
        rot = sb("rot", [P, P], F32, att)
        cos = sb("cos", [P, LAT], F32, att)
        sin = sb("sin", [P, LAT], F32, att)
        sink = sb("sink", [P, A_HEADS + B_HEADS], F32, att)
        zero = sb("zero", [P, P], F32, att)
        q = sb("q", [P, 2, T], F32, att)
        k = sb("k", [P, 2, T], F32, att)
        v = sb("v", [P, 3, 2 * P], F32, att)
        ck_rows = sb("ck_rows", [P, 2 * P], F32, att)
        ck = sb("ck", [P, 2 * P], F32, att)
        cv = sb("cv", [P, 2 * P], F32, att)
        k_out = sb("k_out", [P, 2 * P], F32, att)
        flip = sb("flip", [P, P], F32, att)
        mask = sb("mask", [P, 2, T], F32, att)
        rpb = sb("rpb", [P, 2, 2, LAT], F32, att)
        s = sb("scores", [P, 2 * T + CTX], F32, att)
        pT = sb("probs_t", [P, 3 * LAT + CTX], F32, att)
        zs = sb("z_silu", [P, 2, T], F32, att)
        yf = sb("y_full", [P, T], F32, att)
        st = sb("softmax_stats", [P, 6, 4], F32, att)
        att.close()
        cnv = ExitStack()
        C = sb("conv_out", [P, KT * T], F32, cnv)
        SZ = sb("silu_z", [P, KT * T], F32, cnv)
        zt = sb("tanh_z", [P, 2, T], F32, cnv)
        lsum = sb("conv_sum", [P, T], F32, cnv)
        cnv.close()
        fin = ExitStack()
        out_tok = sb("out_tok", [P, 3, D], F32, fin)
        fin_g = sb("x_gained", [P, 2, T], F32, fin)
        fin.close()
        sb("layer_area", [P, 2 * KT * T + 1248])
        h_t = sb("h_t", [P, 2, T])
        h_f = sb("h_f", [P, 2, T])

        acc = ctx.enter_context(nc.psum_tensor("acc", [P, 4, 512], F32))
        p_ada = ctx.enter_context(nc.psum_tensor("p_ada", [P, 512], F32))
        p_s = ctx.enter_context(nc.psum_tensor("p_s", [P, 2, 512], F32))
        p_m = ctx.enter_context(nc.psum_tensor("p_m", [P, 512], F32))

        PV_ADA_B, PV_C, PV_CCTX = 0, 96, 112
        PV_NORM, PV_FINAL, PV_DWB, PV_LNG, PV_LNB = 128, 160, 176, 192, 208

        const_in = sem("const_in"); x_in = sem("x_in")
        raw_in = [sem(f"raw_in{i}") for i in range(RAW)]
        ada_in = [sem(f"ada_in{i}") for i in range(RAW)]
        hi_ready = sem("hi_ready"); lo_ready = sem("lo_ready")
        w_used = sem("w_used")
        acc_free = [sem("acc_even_free"), sem("acc_odd_free")]
        ada_used = sem("ada_used"); ada_out = sem("ada_out")
        m_ready = sem("m_ready"); m_free = sem("m_free")
        par_t = sem("params_turned"); par_ready = sem("params_ready"); c_th = sem("cond_tanh")
        cc_ready = sem("cond_ready")
        xt_ready = sem("x_turned"); x_done = sem("x_stored"); xsq_ready = sem("x_squared")
        xsq_added = sem("x_squares_added")
        ss_ready = sem("squares_summed"); rt_ready = sem("root_ready"); rs_ready = sem("rstd_ready")
        t_ready = sem("normed"); hf_ready = sem("h_full"); hh_ready = sem("h_hi_ready")
        h_ready = sem("h_ready")
        rope_ready = sem("roped"); s_ready = sem("scores_ready"); negm_ready = sem("negmax_ready")
        exp_done = sem("exp_done"); rcp_ready = sem("rcp_ready"); probs_ready = sem("probs_ready")
        pt_ready = sem("probs_turned"); pt_out = sem("probs_t_stored")
        z_tanh = sem("z_tanh"); yh_ready = sem("y_hi_ready"); y_ready = sem("y_ready")
        ck_in = sem("ck_in"); cv_in = sem("cv_in"); rpb_in = sem("rpb_in")
        ko_sent = sem("k_out_sent"); v_sent = sem("v_sent")
        pc_ready = sem("pool_taps_ready")
        prod_ready = sem("tap_products_ready"); prod_added = sem("tap_products_added")
        tap_done = sem("tap_done")
        c_ready = sem("conv_ready")
        ln_sum = sem("ln_summed"); cen_ready = sem("centred"); sq_ready = sem("squared")
        cn_ready = sem("ln_normed"); v_ready = sem("ln_affine"); y2_full = sem("y2_full")
        y2h_ready = sem("y2_hi"); y2_done = sem("y2_ready"); lsq_ready = sem("ln_squares")
        sq_summed = sem("ln_squares_summed")
        fg_ready = sem("final_gained"); ft_ready = sem("final_turned")
        ft_out = sem("final_stored"); fs_ready = sem("final_scaled"); y_sent = sem("y_sent")

        w_in0 = attn_w_in[0].rearrange("(k p) n -> p k n", p=P)
        w_out0 = attn_w_out[0].rearrange("(k p) n -> p k n", p=P)
        w_in1 = conv_w_in[0].rearrange("(k p) n -> p k n", p=P)
        w_out1 = conv_w_out[0].rearrange("(k p) n -> p k n", p=P)
        w_ada = [ada_w[i].rearrange("(k p) n -> p k n", p=P) for i in range(2)]

        M_NORM0 = 2
        M_FIRST = 16 + 1
        M_A = M_FIRST + 3
        M_B = M_A + 3 * 7
        M_BLOOP = M_B + 9
        M_LAST = M_BLOOP + 3 * 8
        M_NORM1 = M_LAST + 4
        M_LN = M_NORM1 + 3
        M_FIN = M_LN + 2

        def m_of_ada(a):
            return a if a < M_NORM0 else a + 1

        def at(e, sm, n):
            if not isinstance(n, int) or n > 0:
                e.wait_ge(sm, n)

        def evacuated(e, par, half):
            e.wait_ge(acc_free[par], half + 1)

        block = ctx.enter_context(nc.Block())

        @block.sync
        def _(sp):
            sp.dma_start(x_tok[:, 0], x_prompt[0]).then_inc(x_in, 16)
            for j in range(2):
                sp.dma_start(x_tok[:, 1 + j], x_sample[0, j * P:(j + 1) * P]).then_inc(x_in, 16)
            consts = [(ident[:], const_rot[0, :, 0:P]), (rot[:], const_rot[1, :, 0:P]),
                      (flip[:], const_rot[0, :, P:]),
                      (cos[:], const_rot[2]), (sin[:], const_rot[3]),
                      (rows1[0:96], ada_b.rearrange("l (r f) -> (l r) f", f=P)),
                      (rows1[96:112], c.rearrange("b (r f) -> (b r) f", f=P)),
                      (rows1[112:128], c_ctx.rearrange("(r f) -> r f", f=P)),
                      (rows2[0:32], norm_g.rearrange("l (r f) -> (l r) f", f=P)),
                      (rows2[32:48], final_g.rearrange("(r f) -> r f", f=P)),
                      (rows2[48:64], conv_dw_b.rearrange("l (r f) -> (l r) f", f=P)),
                      (rows2[64:80], conv_ln_g.rearrange("l (r f) -> (l r) f", f=P)),
                      (rows2[80:96], conv_ln_b.rearrange("l (r f) -> (l r) f", f=P)),
                      (rows_dw[0:124], conv_dw[0].rearrange("k (r f) -> (k r) f", f=P)
                       .rearrange("(a b) f -> b a f", b=124)),
                      (sink[:, 0:A_HEADS], a_sink.broadcast_to([P, A_HEADS])),
                      (mask[:], const_mask[0])]
            assert len(consts) == 16
            for dst, src in consts:
                sp.dma_start(dst, src).then_inc(const_in, 16)

            def ada(a, src, col, first=False):
                for s_ in range(BK):
                    ada_block(a, s_, src, col, first)

            def ada_block(a, s_, src, col, first=False):
                if not first:
                    sp.wait_ge(ada_used, 4 * a + s_ - 3)
                sp.dma_start(ada_raw[:, s_], src[:, BK * s_:BK * s_ + BK, bass.ds(col, W2)])\
                    .then_inc(ada_in[s_], 16)

            def w_block(m, s_, src, col, first=False):
                if not first:
                    sp.wait_ge(lo_ready, 4 * m + s_ - 3)
                sp.dma_start(raw[:, s_], src[:, BK * s_:BK * s_ + BK, bass.ds(col, W2)])\
                    .then_inc(raw_in[s_], 16)

            def paired_block(m, b, src, cols, first=False):
                if not first:
                    sp.wait_ge(lo_ready, 4 * m + b - 3)
                kt, col = BK * (b // 2), cols[b % 2]
                sp.dma_start(raw[:, b % RAW], src[:, kt:kt + BK, col:col + W2]).then_inc(raw_in[b % RAW], 16)

            ada(0, w_ada[0], 0, first=True)
            for b in range(4):
                paired_block(0, b, w_in0, (COL_KA, COL_VA), first=True)
            ada(1, w_ada[0], D)
            for t0, t1, blocks in ((1, 2, (4, 5)), (2, 6, (6, 7)), (6, 8, ())):
                with sp.Fori(t0, t1) as t:
                    ada(2 * t, w_ada[0], t * W2)
                    ada(2 * t + 1, w_ada[0], D + t * W2)
                for b in blocks:
                    paired_block(0, b, w_in0, (COL_KA, COL_VA))

            def pairs(m, cols, src, ada_of=lambda t: [], small_of=lambda t: None):
                for t in range(4 * len(cols)):
                    w_block(m + t // 4, t % 4, src, cols[t // 4])
                    for a in ada_of(t):
                        ada_block(*a)
                    small_of(t)

            sp.dma_start(ck_rows[:], cache_a_k[0, 0].rearrange("s h d -> s (h d)")).then_inc(ck_in, 16)
            sp.dma_start(cv[:], cache_a_v[0, 0].rearrange("s h d -> s (h d)")).then_inc(cv_in, 16)
            g0 = 2 * D
            pairs(2, [COL_QA], w_in0, lambda t: [(16, t, w_ada[0], g0)])

            def kv_out(m_free_n, half, k_to, v_to):
                sp.wait_ge(m_free, m_free_n)
                sp.dma_start(k_to, k_out[:]).then_inc(ko_sent, 16)
                sp.wait_ge(acc_free[1], half + 1)
                sp.dma_start(v_to, v[:, 0]).then_inc(v_sent, 16)

            kv_out(M_FIRST + 2, 0, new_a_k[0, 0].rearrange("s h d -> s (h d)"),
                   new_a_v[0, 0].rearrange("s h d -> s (h d)"))

            def a_step(n):
                pairs(3 + 2 * n, [COL_Z + W2 * n, COL_QA + W2 * (n + 1)], w_in0,
                      lambda t: [(17 + 4 * n + t // 2, 2 * (t % 2) + j, w_ada[1], (4 * n + t // 2) * W2)
                                 for j in range(2)])

            with sp.Fori(0, 3) as n:
                a_step(n)

            def heads(x, i):
                return x[0, 0, :, bass.ds(2 * i, 2)].rearrange("s h d -> s (h d)")

            def is_first(i):
                return isinstance(i, int) and i == 0

            rpb_flat = b_rpb.rearrange("l h r c -> (l h r c)")

            def small_loads(i):
                def at_tick(t):
                    if t == 8:
                        sp.wait_ge(m_free, M_FIRST + 3 if is_first(i) else M_BLOOP + 8 * (i - 2) + 7)
                        sp.dma_start(ck_rows[:], heads(cache_b_k, i)).then_inc(ck_in, 16)
                    if t == 12:
                        sp.wait_ge(s_ready, 2 * (i + 3) + 2)
                        for j in range(2):
                            for qt in range(2):
                                for half in range(2):
                                    r = 2 * qt + half
                                    off = ((2 * i + j) * RPB_H + 7 - r) * RPB_W + NB_KW - GRID_W
                                    first = rpb_flat[bass.ds(off, 1)]
                                    src = bass.AP(first.tensor, first.offset,
                                                  [[1, GRID_W], [RPB_W, ROWS], [1, GRID_W]])
                                    dst = rpb[64 * half:64 * half + 64, j, qt]\
                                        .rearrange("p (r c) -> p r c", c=GRID_W)
                                    sp.dma_start(dst, src).then_inc(rpb_in, 16)
                        if is_first(i):
                            sp.wait_ge(negm_ready, 2 * 4)
                            sp.dma_start(mask[:], const_mask[1]).then_inc(const_in, 16)
                    if t == 13:
                        sp.wait_ge(y_ready, 2 * (i + 3) + 2)
                        sp.dma_start(cv[:], heads(cache_b_v, i)).then_inc(cv_in, 16)
                return at_tick

            def b_loads(i, ada_src):
                pairs(9 + 4 * i, [COL_Z + W2 * (i + 3), COL_KB + W2 * i, COL_VB + W2 * i,
                                  COL_QB + W2 * i], w_in0,
                      lambda t: [(29 + 4 * i + t // 4, t % 4, *ada_src(t // 4))],
                      small_loads(i))
                kv_out(M_B + 7 if is_first(i) else M_BLOOP + 8 * (i - 1) + 6, 5 + 2 * i,
                       heads(new_b_k, i), heads(new_b_v, i))

            b_loads(0, lambda q: (w_ada[0], g0 + W2 * (1 + q)))
            b_loads(1, lambda q: (w_ada[0], g0 + W2 * (5 + q)) if q < 3 else (w_ada[1], 12 * W2))
            with sp.Fori(2, 4) as i:
                b_loads(i, lambda q: (w_ada[1], (4 * i + 5) * W2 + q * W2))
            pairs(25, [COL_Z + 7 * W2], w_in0, lambda t: [(45, t, w_ada[1], 21 * W2)])
            for b in range(8):
                paired_block(PAIR_WOUT0, b, w_out0, (0, W2))
            for t in range(4):
                ada_block(46, t, w_ada[1], 22 * W2)
            with sp.Fori(2, 8) as j:
                pairs(PAIR_WOUT0 + j, [j * W2], w_out0)
            for b in range(8):
                paired_block(PAIR_GLU, b, w_in1, (D, 0))
                if b == 3:
                    for t in range(4):
                        ada_block(47, t, w_ada[1], 23 * W2)
            with sp.Fori(2, 9) as j:
                pairs(PAIR_GLU - 2 + 2 * j, [W2 * j + (D - W2), W2 * j - W2], w_in1)
            with sp.Fori(0, 8) as j:
                pairs(PAIR_Z + j, [2 * D + j * W2], w_in1)
            with sp.Fori(0, 8) as j:
                pairs(PAIR_WOUT1 + j, [j * W2], w_out1)
            outs = [y_prompt[0], y_sample[0, 0:P], y_sample[0, P:2 * P]]
            for i in range(6):
                half = slice(D // 2 * (i % 2), D // 2 * (i % 2 + 1))
                sp.wait_ge(fs_ready, i + 1)
                sp.dma_start(outs[i // 2][:, half], out_tok[:, i // 2, half]).then_inc(y_sent, 16)
            sp.wait_ge(y_sent, 6 * 16)
            sp.wait_ge(ko_sent, 16 * 5)
            sp.wait_ge(v_sent, 16 * 5)

        @block.tensor
        def _(pe):
            def m_use(n):
                at(pe, m_free, n)

            def mm3(out, wh, wl, xh, xl, start, stop):
                pe.matmul(out, wh, xh, start=start, stop=False)
                pe.matmul(out, wh, xl, start=False, stop=False)
                return pe.matmul(out, wl, xh, start=False, stop=stop)

            def w_block(m, half, par, s_, kind="h", x_wait=None, number=None, tiles=range(BK)):
                if s_ == 0 and 0 in tiles:
                    at(pe, acc_free[par], half)
                b = number if number is not None else 4 * m + s_
                pe.wait_ge(lo_ready, b + 1)
                b = (s_ if number is None else number) % SPLIT
                for kk in tiles:
                    kt = BK * s_ + kk
                    if x_wait is not None:
                        pe.wait_ge(x_wait[0], x_wait[1] + kt + 1)
                    if kind == "v":
                        for t in range(3):
                            out = acc[:, 2 * par + t // 2, (t % 2) * W2:(t % 2) * W2 + W2]
                            xh, xl = (z[:, kt, t * P:(t + 1) * P] for z in (H_hi, H_lo))
                            pe.matmul(out, xh, w_hi[:, b, kk], start=(kt == 0 and t != 1), stop=False,
                                      skip_group_check=True)
                            pe.matmul(out, xh, w_lo[:, b, kk], start=False, stop=False,
                                      skip_group_check=True)
                            last = pe.matmul(out, xl, w_hi[:, b, kk], start=False, stop=(kt == KT - 1),
                                             skip_group_check=True)
                        continue
                    if kind == "h":
                        xh, xl = H_hi[:, kt], H_lo[:, kt]
                    else:
                        xh, xl = Y_hi[:, kt * T:(kt + 1) * T], Y_lo[:, kt * T:(kt + 1) * T]
                    for j in range(2):
                        cols = slice(j * P, (j + 1) * P)
                        last = mm3(acc[:, 2 * par + j, 0:T], w_hi[:, b, kk, cols], w_lo[:, b, kk, cols],
                                   xh, xl, kt == 0, kt == KT - 1)
                if BK - 1 in tiles:
                    last.then_inc(w_used, 1)

            def ada_block(a, s_):
                pe.wait_ge(ada_in[s_], 16 * (a + 1))
                if s_ == 0:
                    at(pe, ada_out, a)
                for g in range(4):
                    last = pe.matmul(p_ada[32 * g:32 * g + 32, 0:W2], cc[:, BK * s_ + g],
                                     ada_raw[:, s_, g], start=(s_ == 0), stop=(s_ == 3),
                                     tile_position=(0, 32 * g))
                last.then_inc(ada_used, 1)

            def ada_turn(a, use):
                pe.wait_ge(ada_out, a + 1)
                m_use(use)
                for j in range(2):
                    last = pe.transpose(p_m[:, j * P:(j + 1) * P], ada_row[:, j * P:(j + 1) * P], ident[:])
                last.then_inc(m_ready, 1)

            pe.wait_ge(const_in, 256)
            pe.transpose(p_s[:, 0, 0:P], rows1[:], ident[:])
            pe.transpose(p_s[:, 0, P:P + 96], rows2[0:96], ident[0:96, 0:96])
            for i in range(4):
                last = pe.transpose(p_s[:, 1, 124 * i:124 * i + 124], rows_dw[0:124, i],
                                    ident[0:124, 0:124])
            last.then_inc(par_t, 1)
            pe.wait_ge(x_in, 48)
            for f in range(KT):
                at(pe, x_done, f - 3)
                for t in range(3):
                    last = pe.transpose(acc[:, f % 4, t * P:(t + 1) * P],
                                        x_tok[:, t, f * P:(f + 1) * P], ident[:])
                last.then_inc(xt_ready, 1)
            pe.wait_ge(cc_ready, 1)

            def norm_mean(n, use):
                pe.wait_ge(ss_ready, n + 1)
                m_use(use)
                pe.matmul(p_m[:, 0:T], ones[:], ssum[:], start=True, stop=True).then_inc(m_ready, 1)

            def first_block(b, tiles=range(BK)):
                w_block(b % 2, 0, b % 2, b // 2, "hv"[b % 2], (h_ready, 0), b, tiles)

            for s_ in range(4):
                for a in range(4 * s_, 4 * s_ + 4):
                    for i in range(BK):
                        ada_block(a, i)
                        unit = (4 * (a % 4) + i) // 2
                        if s_ > 0 and i % 2 == 1:
                            first_block(2 * s_ - 2 + unit // 4, [unit % 4])
                    ada_turn(a, m_of_ada(a))
                    if a == 1:
                        norm_mean(0, M_NORM0)
            first_block(6)
            first_block(7)

            def rotate(x, use):
                m_use(use)
                pe.matmul(p_m[:].rearrange("p (a b) -> p a b", a=2), rot[:], x[:, :, CTX:T],
                          start=True, stop=True).then_inc(m_ready, 1)

            def scores(n, j, kv, is_a=True):
                at(pe, pt_out, 2 * n + j)
                pe.matmul(p_s[:, 0, T:T + CTX], q[:, j, 0:CTX], k[:, kv, 0:CTX], start=True, stop=True)
                for t in range(2):
                    lhs = q[:, j, CTX + t * P:CTX + (t + 1) * P]
                    pe.matmul(p_s[:, t, 0:LAT], lhs, k[:, kv, CTX:T], start=True, stop=is_a)
                    if not is_a:
                        pe.matmul(p_s[:, t, 0:LAT], flip[:], rpb[:, j, t], start=False, stop=True)
                    last = pe.matmul(p_s[:, t, LAT:LAT + P], lhs, ck[:, kv * P:(kv + 1) * P],
                                     start=True, stop=True)
                last.then_inc(s_ready, 1)

            def turn_probs(n, j):
                pe.wait_ge(probs_ready, 2 * n + j + 1)
                for t in range(2):
                    for kt in range(3):
                        pe.transpose(p_s[:, kt // 2, (kt % 2) * LAT + t * P:(kt % 2) * LAT + (t + 1) * P],
                                     s[:, t * T + kt * P:t * T + (kt + 1) * P], ident[:])
                pe.transpose(p_s[:, 1, LAT:LAT + P], s[:, 2 * T:2 * T + CTX], ident[:])\
                    .then_inc(pt_ready, 1)

            def attend(n, j, kv, use):
                pe.wait_ge(pt_out, 2 * n + j + 1)
                m_use(use)
                vs = slice(kv * P, (kv + 1) * P)
                pe.matmul(p_m[:, 0:CTX], v[:, 0, vs], pT[:, 3 * LAT:3 * LAT + CTX], start=True, stop=True)
                pe.matmul(p_m[:, CTX:T], v[:, 1, vs], pT[:, 0:LAT], start=True, stop=False)
                pe.matmul(p_m[:, CTX:T], v[:, 2, vs], pT[:, LAT:2 * LAT], start=False, stop=False)
                pe.matmul(p_m[:, CTX:T], cv[:, vs], pT[:, 2 * LAT:3 * LAT], start=False, stop=True)\
                    .then_inc(m_ready, 1)

            def turn_k(use):
                m_use(use)
                for j in range(2):
                    last = pe.transpose(p_m[:, j * P:(j + 1) * P], k[:, j, 0:CTX], ident[:])
                last.then_inc(m_ready, 1)

            def turn_ck(i, use):
                pe.wait_ge(ck_in, 16 * (i + 1))
                m_use(use)
                for j in range(2):
                    last = pe.transpose(p_m[:, j * P:(j + 1) * P], ck_rows[:, j * P:(j + 1) * P], ident[:])
                last.then_inc(m_ready, 1)

            for t in range(4):
                w_block(2, 1, 0, t)
                ada_block(16, t)
                if t == 0:
                    evacuated(pe, 0, 0)
                    rotate(k, M_FIRST)
                if t == 1:
                    turn_k(M_FIRST + 1)
                if t == 2:
                    turn_ck(0, M_FIRST + 2)

            def a_step(n, kv):
                use = M_A + 7 * n
                for t in range(8):
                    i, s_ = t // 4, t % 4
                    m = 3 + 2 * n + i
                    w_block(m, 1 + n + i, 1 - i, s_)
                    for j in range(2):
                        ada_block(17 + 4 * n + t // 2, 2 * (t % 2) + j)
                    if t == 0:
                        evacuated(pe, 0, 1 + n)
                        rotate(q, use)
                    if t == 1:
                        pe.wait_ge(rope_ready, n + 2)
                        scores(n, 0, kv)
                        ada_turn(16 + 4 * n, use + 1)
                    if t == 2:
                        ada_turn(17 + 4 * n, use + 2)
                    if t == 3:
                        turn_probs(n, 0)
                    if t == 4:
                        pe.wait_ge(cv_in, 16)
                        attend(n, 0, kv, use + 3)
                        scores(n, 1, kv)
                    if t == 5:
                        ada_turn(18 + 4 * n, use + 4)
                    if t == 6:
                        turn_probs(n, 1)
                        ada_turn(19 + 4 * n, use + 5)
                    if t == 7:
                        attend(n, 1, kv, use + 6)

            a_step(0, 0)
            a_step(1, 0)
            a_step(2, 1)

            def b_step(n, is_a, last=False):
                i = n - 3
                use = (M_B if is_a else M_BLOOP + 8 * (n - 4)) + (1 if is_a else 0)
                ab = 29 + 4 * i
                kvs = (1, 1) if is_a else (0, 1)
                for t in range(12 if last else 16):
                    pi, s_ = t // 4, t % 4
                    m, half, par = 9 + 4 * i + pi, 4 + 2 * i + (pi + 1) // 2, 1 - pi % 2
                    if last and pi > 0:
                        b = t - 4
                        w_block(PAIR_WOUT0 + b % 2, PAIR_WOUT0 // 2, b % 2, b // 2, "y", (y_ready, 0),
                                4 * PAIR_WOUT0 + b)
                    else:
                        w_block(m, half, par, s_, "v" if pi == 2 else "h")
                    if not last or pi == 0:
                        ada_block(ab + pi, s_)
                    if t == 0 and is_a:
                        evacuated(pe, 0, 1 + n)
                        rotate(q, M_B)
                    if t == 1:
                        if is_a:
                            pe.wait_ge(rope_ready, n + 2)
                        else:
                            evacuated(pe, 0, 4 + 2 * i)
                            pe.wait_ge(rpb_in, 128 * i)
                        scores(n, 0, kvs[0], is_a)
                        ada_turn(ab - 1, use)
                    if t == 4:
                        turn_probs(n, 0)
                    if t == 5:
                        if not is_a:
                            pe.wait_ge(cv_in, 16 * (i + 1))
                        attend(n, 0, kvs[0], use + 1)
                        scores(n, 1, kvs[1], is_a)
                    if t == 6:
                        ada_turn(ab, use + 2)
                    if t == 8:
                        turn_probs(n, 1)
                    if t == 9:
                        attend(n, 1, kvs[1], use + 3)
                    if last:
                        continue
                    if t == 10:
                        ada_turn(ab + 1, use + 4)
                    if t == 11:
                        evacuated(pe, 0, 5 + 2 * i)
                        turn_k(use + 5)
                    if t == 12:
                        turn_ck(i + 1, use + 6)
                    if t == 14:
                        ada_turn(ab + 2, use + 7)

            b_step(3, True)
            with pe.Fori(4, 7) as n:
                b_step(n, False)
            b_step(7, False, last=True)

            with pe.Fori(1, 4) as p:
                for t in range(8):
                    i, s_ = t // 4, t % 4
                    w_block(PAIR_WOUT0 + 2 * p + i, PAIR_WOUT0 // 2 + p, i, s_, "y")

            def edge_pair(a):
                for s_ in range(BK):
                    ada_block(a, s_)

            edge_pair(46)
            norm_mean(1, M_NORM1)
            ada_turn(46, M_NORM1 + 1)
            edge_pair(47)

            def two_pairs(p):
                for t in range(8):
                    i, s_ = t // 4, t % 4
                    w_block(PAIR_GLU + 2 * p + i, PAIR_GLU // 2 + p, i, s_)
                    if isinstance(p, int) and p == 9 and t == 2:
                        pe.wait_ge(ln_sum, 1)
                        m_use(M_LN)
                        pe.matmul(p_m[:, 0:T], ones[:], lsum[:], start=True, stop=True).then_inc(m_ready, 1)
                    if isinstance(p, int) and p == 10 and t == 1:
                        norm_mean(2, M_LN + 1)

            for b in range(8):
                w_block(PAIR_GLU + b % 2, PAIR_GLU // 2, b % 2, b // 2, "h", (h_ready, KT),
                        4 * PAIR_GLU + b)
                if b == 0:
                    ada_turn(47, M_NORM1 + 2)
            with pe.Fori(1, 9) as p:
                two_pairs(p)
            two_pairs(9)
            two_pairs(10)
            two_pairs(11)

            def turn_final(f, b):
                pe.wait_ge(fg_ready, f + 1)
                at(pe, ft_out, f - 1)
                for t in range(3):
                    last = pe.transpose(p_s[:, b, t * P:(t + 1) * P], fin_g[:, b, t * P:(t + 1) * P],
                                        ident[:])
                last.then_inc(ft_ready, 1)

            def out_pairs(p, first=False):
                for t in range(8):
                    i, s_ = t // 4, t % 4
                    w_block(PAIR_WOUT1 + 2 * p + i, PAIR_WOUT1 // 2 + p, i, s_, "y",
                            (y2_done, 0) if first and i == 0 else None)
                    if t in (1, 2) and not first:
                        turn_final(4 * p - 2 + t - 1, t - 1)
                    if t in (5, 6):
                        turn_final(4 * p + t - 5, t - 5)

            out_pairs(0, first=True)
            with pe.Fori(1, 4) as p:
                out_pairs(p)
            pe.wait_ge(ss_ready, 4)
            m_use(M_FIN)
            for t in range(3):
                last = pe.matmul(p_m[:, 2 * t:2 * t + 2], ssum[:, t * P:(t + 1) * P], ones[:, 0:2],
                                 start=True, stop=True)
            last.then_inc(m_ready, 1)
            turn_final(14, 0)
            turn_final(15, 1)

        @block.scalar
        def _(act):
            def split(mb, k_):
                m, s_ = mb + k_ // 4, k_ % 4
                act.wait_ge(raw_in[s_], 16 * (m + 1))
                at(act, w_used, 4 * m + s_ - 1)
                act.activation(w_hi[:, s_ % SPLIT], raw[:, s_], ACT.Copy).then_inc(hi_ready, 1)

            def root(n, use, x):
                act.wait_ge(m_free, use + 1)
                act.activation(x, x, ACT.Sqrt).then_inc(rt_ready, 1)

            def h_two(layer, i):
                for j in range(2):
                    act.wait_ge(hf_ready, layer * KT + 2 * i + j + 1)
                    act.activation(H_hi[:].rearrange("p k t -> p (k t)")[:, bass.ds((2 * i + j) * T, T)],
                                   h_f[:, j], ACT.Copy).then_inc(hh_ready, 1)

            act.wait_ge(par_ready, 1)
            act.activation(c_tanh[:], pvec[:, PV_C:PV_C + 32], ACT.Tanh, scale=0.5).then_inc(c_th, 1)
            for f in range(KT):
                act.wait_ge(x_done, f + 1)
                at(act, xsq_added, f - 1)
                act.activation(sq0[:, f % 2], X[:, f * T:(f + 1) * T], ACT.Square).then_inc(xsq_ready, 1)
                if f in (6, 8):
                    split(0, (f - 6) // 2)
            root(0, M_NORM0, rstd[:])
            for t in range(8):
                h_two(0, t)
                if t > 1:
                    split(0, t)

            def take(par, mb_done, out, scale=1.0, blocks=4):
                act.wait_ge(w_used, 4 * mb_done + blocks)
                act.activation(out, acc[:, 2 * par:2 * par + 2, 0:T], ACT.Copy, scale=scale)\
                    .then_inc(acc_free[par], 1)

            def take_v(mb_done, n_sent):
                act.wait_ge(w_used, 4 * mb_done + 4)
                at(act, v_sent, n_sent)
                act.activation(v[:, 0:2].rearrange("p a b -> p (a b)"), acc[:, 2], ACT.Copy)
                act.activation(v[:, 2], acc[:, 3, 0:W2], ACT.Copy).then_inc(acc_free[1], 1)

            def exps(n, j):
                act.wait_ge(negm_ready, 2 * n + j + 1)
                for r in range(3):
                    cols = slice(r * T, r * T + (T if r < 2 else CTX))
                    act.activation(s[:, cols], s[:, cols], ACT.Exp, bias=st[:, 1, r:r + 1],
                                   accum_out=st[:, 2, r:r + 1])
                act.activation(st[:, 3, 0:3], st[:, 1, 0:3], ACT.Exp, bias=sink[:, bass.ds(2 * n + j, 1)])\
                    .then_inc(exp_done, 1)

            def store_pt(n, j):
                act.wait_ge(pt_ready, 2 * n + j + 1)
                act.activation(pT[:, 0:512], p_s[:, 0], ACT.Copy)
                act.activation(pT[:, 512:3 * LAT + CTX], p_s[:, 1, 0:T], ACT.Copy).then_inc(pt_out, 1)

            def y_hi(n, j, use):
                act.wait_ge(m_free, use + 1)
                act.activation(Y_hi[:, bass.ds((2 * n + j) * T, T)], yf[:], ACT.Copy).then_inc(yh_ready, 1)

            def z_gate(n, mb_done, par):
                act.wait_ge(w_used, 4 * mb_done + 4)
                act.activation(zs[:], acc[:, 2 * par:2 * par + 2, 0:T], ACT.Tanh, scale=0.5)\
                    .then_inc(z_tanh, 1)

            for k_ in range(8, 14):
                split(0, k_)
                if k_ == 8:
                    take(0, 0, k[:], blocks=7)
                if k_ == 9:
                    take_v(1, 0)
                if k_ == 13:
                    take(0, 2, q[:], SCALE)

            def a_step(n):
                mb, use = 3 + 2 * n, M_A + 7 * n
                for k_ in range(2, 10):
                    split(mb, k_)
                    if k_ == 3:
                        exps(n, 0)
                    if k_ == 5:
                        z_gate(n, mb, 1)
                        store_pt(n, 0)
                    if k_ == 6:
                        y_hi(n, 0, use + 3)
                        exps(n, 1)
                    if k_ == 8:
                        store_pt(n, 1)
                    if k_ == 9:
                        y_hi(n, 1, use + 6)
                        take(0, mb + 1, q[:], SCALE)

            with act.Fori(0, 3) as n:
                a_step(n)

            def b_step(n, is_a, last=False):
                i = n - 3
                mb, use = 9 + 4 * i, (M_B + 1 if is_a else M_BLOOP + 8 * (n - 4))
                for k_ in range(2, 14 if last else 18):
                    split(mb, k_)
                    if k_ == 3:
                        exps(n, 0)
                    if k_ == 5:
                        z_gate(n, mb, 1)
                    if k_ == 6:
                        store_pt(n, 0)
                    if k_ == 7:
                        y_hi(n, 0, use + 1)
                        exps(n, 1)
                    if k_ == 10:
                        store_pt(n, 1)
                    if k_ == 11:
                        y_hi(n, 1, use + 3)
                    if last:
                        if k_ in (12, 13):
                            squares(k_ - 12, PAIR_WOUT0 // 2, k_ - 12)
                        continue
                    if k_ == 9:
                        take(0, mb + 1, k[:])
                    if k_ == 13:
                        take_v(mb + 2, 16 * (i + 1))
                    if k_ == 17:
                        take(0, mb + 3, q[:], SCALE)

            def squares(pr, half, par):
                act.wait_ge(acc_free[par], half + 1)
                act.activation(h_f[:].rearrange("p a b -> p (a b)"), X[:, bass.ds(2 * pr * T, 2 * T)],
                               ACT.Square).then_inc(sq_ready, 1)

            b_step(3, True)
            with act.Fori(4, 7) as n:
                b_step(n, False)
            b_step(7, False, last=True)
            with act.Fori(1, 4) as p:
                for k_ in range(2, 10):
                    split(PAIR_WOUT0 + 2 * p, k_)
                    if k_ in (5, 9):
                        i = (k_ - 5) // 4
                        squares(2 * p + i, PAIR_WOUT0 // 2 + p, i)

            root(1, M_NORM1, rstd[:])
            for i, k_ in enumerate(H_SPLITS):
                h_two(1, i)
                if k_ is not None:
                    split(PAIR_GLU, k_)

            def tanh_g(p, blocks=4):
                act.wait_ge(w_used, 4 * (PAIR_GLU + 2 * p) + blocks)
                at(act, acc_free[1], PAIR_GLU // 2 + p)
                act.activation(th_g[:], acc[:, 0:2, 0:T], ACT.Tanh, scale=0.5).then_inc(acc_free[0], 1)

            def tanh_z(j, par):
                act.wait_ge(w_used, 4 * (PAIR_Z + j) + 4)
                at(act, acc_free[1 - par], (PAIR_Z + j + par) // 2)
                act.activation(zt[:], acc[:, 2 * par:2 * par + 2, 0:T], ACT.Tanh, scale=0.5)\
                    .then_inc(z_tanh, 1)

            def tap_products(p, b, part):
                for i in range(POOL_TAPS * part // 4, POOL_TAPS * (part + 1) // 4):
                    j, tap = i % 2, TAPS - POOL_TAPS + i // 2
                    if i == 0:
                        act.wait_ge(acc_free[1], PAIR_GLU // 2 + p + 1)
                    at(act, prod_added, 2 * POOL_TAPS * p + i + 1 - PRODS)
                    act.activation(tap_prod[:, i % PRODS], u_pad[:, 2 * b + j, tap:tap + SPAN], ACT.Copy,
                                   scale=taps[:, bass.ds(tap * KT + 2 * p + j, 1)]).then_inc(prod_ready, 1)

            for k_ in range(6, 10):
                split(PAIR_GLU, k_)
                if k_ == 8:
                    tanh_g(0, blocks=7)

            def glu_step(p, b):
                for k_ in range(2, 10):
                    split(PAIR_GLU + 2 * p, k_)
                    tap_products(p - 1, 1 - b, k_ - 2)
                    if k_ == 5:
                        tanh_g(p)

            glu_step(1, 1)
            with act.Fori(1, 4) as i:
                for b in range(2):
                    glu_step(2 * i + b, b)

            def centred_squares(tiles):
                for f in tiles:
                    act.wait_ge(cen_ready, f + 1)
                    if f >= PRODS:
                        act.wait_ge(sq_summed, f + 1 - PRODS)
                    act.activation(tap_prod[:, f % PRODS, 0:T], C[:, f * T:(f + 1) * T], ACT.Square)\
                        .then_inc(lsq_ready, 1)

            def ln_gate(f):
                tile = C[:, f * T:(f + 1) * T]
                act.wait_ge(cn_ready, f + 1)
                act.activation(tile, tile, ACT.Identity, scale=pvec[:, PV_LNG + f:PV_LNG + f + 1],
                               bias=pvec[:, PV_LNB + f:PV_LNB + f + 1])
                act.drain()
                at(act, y2_full, f - 1)
                act.activation(h_t[:, f % 2], tile, ACT.Tanh, scale=0.5).then_inc(v_ready, 1)

            def y2_hi(f):
                act.wait_ge(y2_full, f + 1)
                act.activation(Y_hi[:, f * T:(f + 1) * T], h_f[:, f % 2], ACT.Copy).then_inc(y2h_ready, 1)

            def y2_tile(f):
                if f > 0:
                    y2_hi(f - 1)
                if f + 1 < KT:
                    ln_gate(f + 1)

            for p in range(8, 12):
                for k_ in range(2, 10):
                    split(PAIR_GLU + 2 * p, k_)
                    if p == 8:
                        tap_products(7, 1, k_ - 2)
                    if p == 9 and k_ >= 5:
                        centred_squares(CENTRE[k_ - 5])
                    if k_ in (5, 9):
                        tanh_z(2 * (p - 8) + (k_ - 5) // 4, (k_ - 5) // 4)
                    if p == 9 and k_ == 9:
                        centred_squares(CENTRE[5])
                    if p == 10 and k_ == 3:
                        root(2, M_LN + 1, rstd[:])
                    if p == 10 and k_ == 5:
                        ln_gate(0)
                    if p == 10 and k_ >= 5:
                        y2_tile(k_ - 5)
                    if p == 11:
                        y2_tile(k_ + 3)

            def final_pair(pr, half, par):
                squares(pr, half, par)
                for j in range(2):
                    f = 2 * pr + j
                    at(act, ft_ready, f - 1)
                    act.activation(fin_g[:, j], X[:, bass.ds(f * T, T)], ACT.Copy,
                                   scale=pvec[:, bass.ds(PV_FINAL + f, 1)]).then_inc(fg_ready, 1)

            def out_step(p, first=False, last=False):
                for k_ in range(2, 10):
                    if not (last and k_ > 7):
                        split(PAIR_WOUT1 + 2 * p, k_)
                    if first and k_ < 4:
                        y2_tile(11 + k_)
                    if first and k_ == 3:
                        y2_tile(15)
                        y2_hi(15)
                    if k_ in (5, 9):
                        i = (k_ - 5) // 4
                        final_pair(2 * p + i, PAIR_WOUT1 // 2 + p, i)

            out_step(0, first=True)
            with act.Fori(1, 3) as p:
                out_step(p)
            out_step(3, last=True)
            root(3, M_FIN, small[:, 4:10])

        @block.vector
        def _(dve):
            def split(mb, k_):
                m, s_ = mb + k_ // 4, k_ % 4
                dve.wait_ge(hi_ready, 4 * m + s_ + 1)
                dve.tensor_tensor(w_lo[:, s_ % SPLIT], raw[:, s_], w_hi[:, s_ % SPLIT].bitcast(F32),
                                  ALU.subtract).then_inc(lo_ready, 1)

            def over2(x, n):
                return x.unsqueeze(1).broadcast_to([P, 2, n])

            def ada_store(a):
                dve.wait_ge(ada_used, 4 * a + 4)
                dve.tensor_copy(ada_row[:], p_ada[:, 0:W2]).then_inc(ada_out, 1)

            def ada_sum(a, use):
                dve.wait_ge(m_ready, use + 1)
                dve.tensor_reduce(mod_in[:].rearrange("p f c -> p (f c)")[:, bass.ds(4 * a, 4)]
                                  .rearrange("p (f c) -> p f c", c=2),
                                  p_m[:, 0:2 * P].rearrange("p (f g c) -> p f c g", f=2, g=4)[:, :, 0:2, :],
                                  AX.X, ALU.add).then_inc(m_free, 1)

            def mod_done(pair, a, n):
                for c_ in range(2):
                    dve.tensor_tensor(mod[:, 2 * pair:2 * (pair + n), c_], mod_in[:, 2 * a:2 * (a + n), c_],
                                      pvec[:, PV_ADA_B + 2 * pair:PV_ADA_B + 2 * (pair + n)], ALU.add)

            def norm_eps(use, out, src):
                dve.wait_ge(m_ready, use + 1)
                dve.tensor_scalar(out, src, EPS, None, ALU.add).then_inc(m_free, 1)

            def norm_inverse(n, out):
                dve.wait_ge(rt_ready, n + 1)
                dve.reciprocal(out, out).then_inc(rs_ready, 1)

            def norm_rstd(n, use, out, src):
                norm_eps(use, out, src)
                norm_inverse(n, out)

            gain_f = gain[:].rearrange("p k c -> p (k c)")
            mod_f = mod[:].rearrange("p k c -> p (k c)")

            def gains(f, n, src, layer):
                dve.scalar_tensor_tensor(
                    out=gain[:, bass.ds(f, n)], in0=src, scalar=1.0,
                    in1=pvec[:, bass.ds(PV_NORM + layer * KT + f, n)].unsqueeze(2).broadcast_to([P, n, 2]),
                    op0=ALU.add, op1=ALU.mult)

            def h_two(layer, i):
                base = 3 * KT * layer
                dve.drain()
                for j in range(2):
                    f = 2 * i + j
                    dve.wait_ge(t_ready, layer * KT + f + 1)
                    for c_, cols in enumerate((slice(0, CTX), slice(CTX, T))):
                        last = dve.tensor_scalar(h_f[:, j, cols], h_t[:, j, cols],
                                                 gain_f[:, bass.ds(2 * f + c_, 1)],
                                                 mod_f[:, bass.ds(2 * (base + f) + c_, 1)],
                                                 ALU.mult, ALU.add)
                    last.then_inc(hf_ready, 1)
                for j in range(2):
                    f = 2 * i + j
                    dve.wait_ge(hh_ready, layer * KT + f + 1)
                    at_ = bass.ds(f * T, T)
                    dve.tensor_tensor(H_lo[:].rearrange("p k t -> p (k t)")[:, at_], h_f[:, j],
                                      H_hi[:].rearrange("p k t -> p (k t)")[:, at_].bitcast(F32),
                                      ALU.subtract).then_inc(h_ready, 1)

            dve.memset(cc[:], 0.0)
            dve.memset(ones[:], 1.0 / D)
            dve.memset(zero[:], 0.0)
            dve.memset(sink[:, A_HEADS:], NEG)
            dve.wait_ge(par_t, 1)
            dve.tensor_copy(pvec[:], p_s[:, 0, 0:224])
            dve.tensor_scalar(taps[:], p_s[:, 1, 0:TAPS * KT], 0.5, None, ALU.mult)
            dve.drain().then_inc(par_ready, 1)
            dve.wait_ge(c_th, 1)
            dve.scalar_tensor_tensor(out=c_tanh[:], in0=c_tanh[:], scalar=1.0, in1=pvec[:, PV_C:PV_C + 32],
                                     op0=ALU.add, op1=ALU.mult)
            dve.drain()
            for col, src in ((0, 16), (1, 0)):
                last = dve.tensor_scalar(cc[:, :, col:col + 1], c_tanh[:, src:src + 16].unsqueeze(2), 0.5,
                                         None, ALU.mult)
            last.then_inc(cc_ready, 1)
            for f in range(KT):
                dve.wait_ge(xt_ready, f + 1)
                dve.tensor_copy(X[:, f * T:(f + 1) * T], acc[:, f % 4, 0:T]).then_inc(x_done, 1)
            for s_ in range(4):
                for i in range(2):
                    t = 2 * s_ + i
                    for a in (2 * t, 2 * t + 1):
                        ada_store(a)
                        ada_sum(a, m_of_ada(a))
                        if t == 0:
                            split(0, a)
                    if t == 0:
                        norm_rstd(0, M_NORM0, rstd[:], p_m[:, 0:T])
                    dve.drain()
                    for kind in range(2):
                        f = kind * KT + 2 * t
                        dve.tensor_tensor(mod[:, f:f + 2], mod_in[:, 4 * t + 2 * kind:4 * t + 2 * kind + 2],
                                          pvec[:, PV_ADA_B + f:PV_ADA_B + f + 2].unsqueeze(2)
                                          .broadcast_to([P, 2, 2]), ALU.add)
                    dve.drain()
                    gains(2 * t, 2, mod[:, KT + 2 * t:KT + 2 * t + 2], 0)
                    h_two(0, t)
                    if s_ > 0:
                        split(0, 2 * s_ + i)

            def rope(x, use):
                dve.wait_ge(m_ready, use + 1)
                lat, tmp = x[:, :, CTX:T], h_t[:, :, 0:LAT]
                dve.tensor_tensor(tmp, p_m[:].rearrange("p (a b) -> p a b", a=2), over2(sin[:], LAT),
                                  ALU.mult).then_inc(m_free, 1)
                dve.tensor_tensor(lat, lat, over2(cos[:], LAT), ALU.mult)
                dve.drain()
                dve.tensor_tensor(lat, lat, tmp, ALU.add).then_inc(rope_ready, 1)

            def maxima(n, j, is_a=True):
                dve.wait_ge(s_ready, 2 * n + j + 1)
                dve.memset(st[:, 0, 3:4], NEG)
                if not is_a:
                    dve.wait_ge(const_in, 16 * 17)
                for t in range(2):
                    dve.tensor_tensor_reduce(out=s[:, t * T:(t + 1) * T], in0=p_s[:, t, 0:T],
                                             in1=mask[:, t], scale=1.0, scalar=NEG, op0=ALU.add,
                                             op1=ALU.max, accum_out=st[:, 0, t:t + 1])
                dve.tensor_tensor_reduce(out=s[:, 2 * T:], in0=p_s[:, 0, T:T + CTX], in1=zero[:], scale=1.0,
                                         scalar=NEG, op0=ALU.add, op1=ALU.max, accum_out=st[:, 0, 2:3])
                dve.drain()
                dve.tensor_scalar(st[:, 1, 0:3], st[:, 0, 0:3], sink[:, bass.ds(2 * n + j, 1)], -1.0,
                                  ALU.max, ALU.mult).then_inc(negm_ready, 1)

            def denominators(n, j):
                dve.wait_ge(exp_done, 2 * n + j + 1)
                dve.tensor_tensor(st[:, 4, 0:3], st[:, 2, 0:3], st[:, 3, 0:3], ALU.add)
                dve.drain()
                dve.reciprocal(st[:, 5, 0:3], st[:, 4, 0:3]).then_inc(rcp_ready, 1)

            def z_gate(n, par):
                dve.wait_ge(z_tanh, n + 1)
                dve.scalar_tensor_tensor(out=zs[:], in0=zs[:], scalar=1.0,
                                         in1=acc[:, 2 * par:2 * par + 2, 0:T], op0=ALU.add, op1=ALU.mult)\
                    .then_inc(acc_free[par], 1)

            def y_mul(n, j, use):
                dve.wait_ge(m_ready, use + 1)
                dve.scalar_tensor_tensor(out=yf[:], in0=p_m[:, 0:T], scalar=0.5, in1=zs[:, j],
                                         op0=ALU.mult, op1=ALU.mult).then_inc(m_free, 1)

            def y_lo(n, j):
                dve.wait_ge(yh_ready, 2 * n + j + 1)
                at_ = bass.ds((2 * n + j) * T, T)
                dve.tensor_tensor(Y_lo[:, at_], yf[:], Y_hi[:, at_].bitcast(F32), ALU.subtract)\
                    .then_inc(y_ready, 1)

            def k_store(use):
                dve.wait_ge(m_ready, use + 1)
                dve.tensor_copy(k_out[:], p_m[:, 0:2 * P]).then_inc(m_free, 1)

            def ck_store(use):
                dve.wait_ge(m_ready, use + 1)
                dve.tensor_copy(ck[:], p_m[:, 0:2 * P]).then_inc(m_free, 1)

            for k_ in range(8, 14):
                split(0, k_)
                if k_ == 10:
                    rope(k, M_FIRST)
                if k_ == 11:
                    k_store(M_FIRST + 1)
                if k_ == 12:
                    ck_store(M_FIRST + 2)
                if k_ == 13:
                    ada_store(16)

            def a_step(n):
                mb, use = 3 + 2 * n, M_A + 7 * n
                for k_ in range(2, 10):
                    split(mb, k_)
                    if k_ == 2:
                        rope(q, use)
                    if k_ == 3:
                        ada_sum(16 + 4 * n, use + 1)
                        ada_store(17 + 4 * n)
                        maxima(n, 0)
                    if k_ == 4:
                        denominators(n, 0)
                        ada_sum(17 + 4 * n, use + 2)
                    if k_ == 5:
                        z_gate(n, 1)
                        ada_store(18 + 4 * n)
                    if k_ == 6:
                        dve.drain()
                        y_mul(n, 0, use + 3)
                        maxima(n, 1)
                    if k_ == 7:
                        y_lo(n, 0)
                        denominators(n, 1)
                        ada_sum(18 + 4 * n, use + 4)
                        ada_store(19 + 4 * n)
                    if k_ == 8:
                        ada_sum(19 + 4 * n, use + 5)
                    if k_ == 9:
                        dve.drain()
                        y_mul(n, 1, use + 6)
                        y_lo(n, 1)
                        ada_store(20 + 4 * n)

            with dve.Fori(0, 3) as n:
                a_step(n)

            def b_step(n, is_a, last=False):
                i = n - 3
                mb, ab = 9 + 4 * i, 29 + 4 * i
                use = M_B + 1 if is_a else M_BLOOP + 8 * (n - 4)
                for k_ in range(2, 14 if last else 18):
                    split(mb, k_)
                    if k_ == 2 and is_a:
                        rope(q, M_B)
                    if k_ == 3:
                        ada_sum(ab - 1, use)
                        maxima(n, 0, is_a)
                    if k_ == 4:
                        denominators(n, 0)
                    if k_ == 5:
                        z_gate(n, 1)
                        ada_store(ab)
                    if k_ == 7:
                        dve.drain()
                        y_mul(n, 0, use + 1)
                        maxima(n, 1, is_a)
                    if k_ == 8:
                        ada_sum(ab, use + 2)
                        y_lo(n, 0)
                        denominators(n, 1)
                    if last:
                        if k_ == 7:
                            dve.memset(ssum[:], 0.0)
                            dve.drain()
                            mod_done(ADA_PAIRS * 2 // 3, 16, 1)
                            mod_done(ADA_PAIRS * 2 // 3 + 1, 29, 7)
                            mod_done(ADA_PAIRS, 17, 12)
                            mod_done(ADA_PAIRS + 12, 36, 9)
                            dve.drain()
                            gains(0, KT, mod[:, 3 * KT + KT:3 * KT + 2 * KT], 1)
                            dve.drain()
                        if k_ == 11:
                            dve.drain()
                            y_mul(n, 1, use + 3)
                            y_lo(n, 1)
                        if k_ in (12, 13):
                            update(0, k_ - 12, PAIR_WOUT0, k_ - 12, 0, blocks=k_ - 5)
                        continue
                    if k_ == 9:
                        ada_store(ab + 1)
                    if k_ == 11:
                        dve.drain()
                        y_mul(n, 1, use + 3)
                    if k_ == 12:
                        y_lo(n, 1)
                        ada_sum(ab + 1, use + 4)
                    if k_ == 13:
                        dve.wait_ge(ko_sent, 16 * (i + 1))
                        k_store(use + 5)
                        ada_store(ab + 2)
                    if k_ == 14:
                        ck_store(use + 6)
                    if k_ == 16:
                        ada_sum(ab + 2, use + 7)
                    if k_ == 17:
                        ada_store(ab + 3)

            mod_flat = mod[:].rearrange("p k c -> p (k c)")

            def update(layer, pr, m, par, sq0_, blocks=4):
                dve.wait_ge(w_used, 4 * m + blocks)
                for j in range(2):
                    for c_, (lo, w) in enumerate(((0, CTX), (CTX, LAT))):
                        x_ = X[:, bass.ds((2 * pr + j) * T + lo, w)]
                        last = dve.scalar_tensor_tensor(
                            out=x_, in0=acc[:, 2 * par + j, lo:lo + w],
                            scalar=mod_flat[:, bass.ds(2 * ((3 * layer + 2) * KT + 2 * pr + j) + c_, 1)],
                            in1=x_, op0=ALU.mult, op1=ALU.add)
                last.then_inc(acc_free[par], 1)
                dve.wait_ge(sq_ready, sq0_ + pr + 1)
                for j in range(2):
                    dve.tensor_tensor(ssum[:], ssum[:], h_f[:, j], ALU.add)
                    dve.drain()

            b_step(3, True)
            with dve.Fori(4, 7) as n:
                b_step(n, False)
            b_step(7, False, last=True)
            with dve.Fori(1, 4) as p:
                for k_ in range(2, 10):
                    split(PAIR_WOUT0 + 2 * p, k_)
                    if k_ in (5, 9):
                        i = (k_ - 5) // 4
                        update(0, 2 * p + i, PAIR_WOUT0 + 2 * p + i, i, 0)
            dve.drain().then_inc(ss_ready, 1)

            norm_eps(M_NORM1, rstd[:], p_m[:, 0:T])
            ada_store(46)
            norm_inverse(1, rstd[:])
            ada_sum(46, M_NORM1 + 1)
            for i, k_ in enumerate(H_SPLITS):
                h_two(1, i)
                if i == 0:
                    ada_store(47)
                if k_ is not None:
                    split(PAIR_GLU, k_)
            ada_sum(47, M_NORM1 + 2)
            dve.drain()

            def glu(p, b):
                dve.wait_ge(w_used, 4 * (PAIR_GLU + 2 * p) + 8)
                dve.wait_ge(acc_free[0], PAIR_GLU // 2 + p + 1)
                for j in range(2):
                    for lo, to, w in ((0, HALO, CTX), (CTX, 2 * HALO + CTX, LAT)):
                        last = dve.scalar_tensor_tensor(out=u_pad[:, 2 * b + j, to:to + w],
                                                        in0=th_g[:, j, lo:lo + w], scalar=1.0,
                                                        in1=acc[:, 2 + j, lo:lo + w], op0=ALU.add,
                                                        op1=ALU.mult)
                last.then_inc(acc_free[1], 1)

            def tap_steps(p, b):
                dve.drain()
                done = 2 * (TAPS - POOL_TAPS) * p
                for tap in range(TAPS - POOL_TAPS):
                    for j in range(2):
                        if tap > 0:
                            dve.wait_ge(tap_done, done + 2 * tap + j - 1)
                        w_ = taps[:, bass.ds(tap * KT + 2 * p + j, 1)]
                        u_, out = u_pad[:, 2 * b + j, tap:tap + SPAN], conv_v[:, 2 * b + j]
                        if tap == 0:
                            dve.tensor_scalar(out, u_, w_, pvec[:, bass.ds(PV_DWB + 2 * p + j, 1)],
                                              ALU.mult, ALU.add).then_inc(tap_done, 1)
                        else:
                            dve.scalar_tensor_tensor(out=out, in0=u_, scalar=w_, in1=out, op0=ALU.mult,
                                                     op1=ALU.add).then_inc(tap_done, 1)
                        yield

            def conv_sum(p, b):
                dve.drain()
                dve.wait_ge(pc_ready, p + 1)
                for j in range(2):
                    for lo, frm, w in ((0, 0, CTX), (CTX, CTX + HALO, LAT)):
                        last = dve.tensor_tensor(C[:, bass.ds((2 * p + j) * T + lo, w)],
                                                 conv_v[:, 2 * b + j, frm:frm + w],
                                                 conv_p[:, 2 * b + j, frm:frm + w], ALU.add)
                    last.then_inc(c_ready, 1)

            def z_silu(j, par):
                dve.wait_ge(z_tanh, 8 + j + 1)
                dve.scalar_tensor_tensor(out=SZ[:, 2 * j * T:(2 * j + 2) * T].rearrange("p (a b) -> p a b", a=2),
                                         in0=zt[:], scalar=1.0, in1=acc[:, 2 * par:2 * par + 2, 0:T],
                                         op0=ALU.add, op1=ALU.mult).then_inc(acc_free[par], 1)

            for k_ in range(6, 10):
                split(PAIR_GLU, k_)
                if k_ == 6:
                    mod_done(ADA_PAIRS + 21, 45, 3)
                    dve.memset(u_pad[:], 0.0)
            dve.drain()
            glu(0, 0)

            def conv_step(p, b, first=False, last=False):
                steps = tap_steps(p - 1, 1 - b)
                n = 2 * (TAPS - POOL_TAPS)
                for k_ in range(2, 10):
                    split(PAIR_GLU + 2 * p, k_)
                    for _ in range(n * (k_ - 1) // 8 - n * (k_ - 2) // 8):
                        next(steps)
                    if k_ == 4 and not first:
                        conv_sum(p - 2, b)
                    if last and k_ in (5, 9):
                        z_silu((k_ - 5) // 4, (k_ - 5) // 4)
                if last:
                    conv_sum(p - 1, 1 - b)
                else:
                    glu(p, b)

            conv_step(1, 1, first=True)
            with dve.Fori(1, 4) as i:
                for b in range(2):
                    conv_step(2 * i + b, b)
            dve.memset(ssum[:], 0.0)
            conv_step(8, 0, last=True)

            def y2_lo(f):
                dve.wait_ge(y2h_ready, f + 1)
                dve.tensor_tensor(Y_lo[:, f * T:(f + 1) * T], h_f[:, f % 2],
                                  Y_hi[:, f * T:(f + 1) * T].bitcast(F32), ALU.subtract).then_inc(y2_done, 1)

            def y2_tile(f):
                tile = C[:, f * T:(f + 1) * T]
                dve.wait_ge(v_ready, f + 1)
                dve.scalar_tensor_tensor(out=tile, in0=h_t[:, f % 2], scalar=1.0, in1=tile, op0=ALU.add,
                                         op1=ALU.mult)
                dve.drain()
                dve.scalar_tensor_tensor(out=h_f[:, f % 2], in0=tile, scalar=0.25, in1=SZ[:, f * T:(f + 1) * T],
                                         op0=ALU.mult, op1=ALU.mult).then_inc(y2_full, 1)
                if f > 0:
                    y2_lo(f - 1)

            for p in range(9, 12):
                for k_ in range(2, 10):
                    split(PAIR_GLU + 2 * p, k_)
                    if p == 9 and k_ == 4:
                        dve.wait_ge(m_ready, M_LN + 1)
                        dve.tensor_copy(rstd[:], p_m[:, 0:T]).then_inc(m_free, 1)
                        dve.drain()
                    if p == 9 and k_ >= 4:
                        for f in CENTRE[k_ - 4]:
                            tile = C[:, f * T:(f + 1) * T]
                            dve.tensor_tensor(tile, tile, rstd[:], ALU.subtract).then_inc(cen_ready, 1)
                    if k_ in (5, 9):
                        z_silu(2 * (p - 8) + (k_ - 5) // 4, (k_ - 5) // 4)
                    if p == 10 and k_ == 3:
                        dve.drain()
                        norm_eps(M_LN + 1, rstd[:], p_m[:, 0:T])
                    if p == 10 and k_ == 4:
                        norm_inverse(2, rstd[:])
                    if p == 10 and k_ >= 5:
                        y2_tile(k_ - 5)
                    if p == 11:
                        y2_tile(k_ + 3)

            def final_store(f, b):
                dve.wait_ge(ft_ready, f + 1)
                dve.tensor_copy(out_tok[:, :, bass.ds(f * P, P)],
                                p_s[:, b, 0:T].rearrange("p (a b) -> p a b", a=3)).then_inc(ft_out, 1)

            def out_step(p, first=False, last=False):
                for k_ in range(2, 10):
                    if not (last and k_ > 7):
                        split(PAIR_WOUT1 + 2 * p, k_)
                    if first and k_ < 4:
                        y2_tile(11 + k_)
                    if first and k_ == 3:
                        y2_tile(15)
                        y2_lo(15)
                    if first and k_ == 4:
                        dve.memset(ssum[:], 0.0)
                        dve.drain()
                    if k_ in (3, 4) and not first:
                        final_store(4 * p - 2 + k_ - 3, k_ - 3)
                    if k_ in (7, 8):
                        final_store(4 * p + k_ - 7, k_ - 7)
                    if k_ in (5, 9):
                        i = (k_ - 5) // 4
                        update(1, 2 * p + i, PAIR_WOUT1 + 2 * p + i, i, 8)

            out_step(0, first=True)
            with dve.Fori(1, 3) as p:
                out_step(p)
            out_step(3, last=True)
            dve.drain().then_inc(ss_ready, 1)
            norm_eps(M_FIN, small[:, 4:10], p_m[:, 0:6])
            final_store(14, 0)
            final_store(15, 1)
            norm_inverse(3, small[:, 4:10])
            dve.drain()
            for i in range(6):
                part = out_tok[:, i // 2, D // 2 * (i % 2):D // 2 * (i % 2 + 1)]
                dve.tensor_scalar(part, part, small[:, 4 + 2 * (i // 2):5 + 2 * (i // 2)], None,
                                  ALU.mult).then_inc(fs_ready, 1)

        @block.gpsimd
        def _(pool):
            def h_tiles(layer):
                pool.wait_ge(rs_ready, layer + 1)

                def two(i, wait=True):
                    for j in range(2):
                        f = 2 * i + j
                        if wait:
                            pool.wait_ge(hf_ready, layer * KT + f - 1)
                        pool.tensor_tensor(h_t[:, j], X[:, bass.ds(f * T, T)], rstd[:], ALU.mult)\
                            .then_inc(t_ready, 1)
                two(0, wait=False)
                with pool.Fori(1, 8) as i:
                    two(i)

            pool.memset(ssum[:], 0.0)
            pool.drain()
            for f in range(KT):
                pool.wait_ge(xsq_ready, f + 1)
                pool.tensor_tensor(ssum[:], ssum[:], sq0[:, f % 2], ALU.add).then_inc(xsq_added, 1)
                pool.drain()
            pool.drain().then_inc(ss_ready, 1)
            h_tiles(0)
            with pool.Fori(0, 8) as n:
                for j in range(2):
                    pool.wait_ge(rcp_ready, 2 * n + j + 1)
                    pool.tensor_tensor(s[:, 2 * T:], s[:, 2 * T:], st[:, 5, 2:3].broadcast_to([P, CTX]),
                                       ALU.mult)
                    for r in range(2):
                        cols = slice(r * T, (r + 1) * T)
                        last = pool.tensor_scalar(s[:, cols], s[:, cols], st[:, 5, r:r + 1], None, ALU.mult)
                    last.then_inc(probs_ready, 1)

            h_tiles(1)
            pool.memset(lsum[:], 0.0)
            pool.drain()

            def taps_added(p, b):
                for tap in range(1, POOL_TAPS):
                    for j in range(2):
                        i = 2 * tap + j
                        if tap > 1:
                            pool.wait_ge(prod_added, 2 * POOL_TAPS * p + (1 if i == 4 else i - 1))
                        pool.wait_ge(prod_ready, 2 * POOL_TAPS * p + i + 1)
                        out = conv_p[:, 2 * b + j]
                        last = pool.tensor_tensor(out, tap_prod[:, j] if tap == 1 else out,
                                                  tap_prod[:, i % PRODS], ALU.add)
                        last.then_inc(prod_added, 3 if i == 3 else 1)
                pool.drain().then_inc(pc_ready, 1)

            def features_added(p):
                for j in range(2):
                    f = 2 * p + j
                    pool.wait_ge(c_ready, f + 1)
                    pool.tensor_tensor(lsum[:], lsum[:], C[:, bass.ds(f * T, T)], ALU.add)
                    pool.drain()

            taps_added(0, 0)
            taps_added(1, 1)
            features_added(0)
            with pool.Fori(1, 4) as i:
                for b in range(2):
                    taps_added(2 * i + b, b)
                    features_added(2 * i + b - 1)
            features_added(7)
            pool.drain().then_inc(ln_sum, 1)
            for f in range(KT):
                pool.wait_ge(lsq_ready, f + 1)
                pool.tensor_tensor(ssum[:], ssum[:], tap_prod[:, f % PRODS, 0:T], ALU.add)\
                    .then_inc(sq_summed, 1)
                pool.drain()
            pool.drain().then_inc(ss_ready, 1)
            pool.wait_ge(rs_ready, 3)
            for f in range(KT):
                tile = C[:, f * T:(f + 1) * T]
                pool.tensor_tensor(tile, tile, rstd[:], ALU.mult).then_inc(cn_ready, 1)


_INS = ["x_prompt", "x_sample", "cache_a_k", "cache_a_v", "cache_b_k", "cache_b_v", "c", "c_ctx", "ada_w",
        "ada_b", "norm_g", "attn_w_in", "attn_w_out", "a_sink", "b_rpb", "conv_w_in", "conv_dw",
        "conv_dw_b", "conv_ln_g", "conv_ln_b", "conv_w_out", "final_g"]
_OUTS = [(1, CTX, D), (1, LAT, D), (1, 1, CTX, A_KV, P), (1, 1, CTX, A_KV, P), (1, 1, CTX, B_HEADS, P),
         (1, 1, CTX, B_HEADS, P)]


def constants():
    eye = np.zeros((P, LAT), np.float32)
    eye[:, 0:P] = np.eye(P, dtype=np.float32)
    columns = np.arange(P)
    eye[columns, P + columns // GRID_W * GRID_W + GRID_W - 1 - columns % GRID_W] = 1.0
    turn = np.zeros((P, LAT), np.float32)
    q4 = P // 4
    for half in range(2):
        for i in range(q4):
            x1, x2 = 2 * half * q4 + i, (2 * half + 1) * q4 + i
            turn[x2, x1] = -1.0
            turn[x1, x2] = 1.0
    inv = np.float32(10000.0) ** (-np.arange(q4, dtype=np.float32) / np.float32(q4))
    t = np.arange(LAT)
    row = (t // GRID_W).astype(np.float32)[None] * inv[:, None]
    col = (t % GRID_W).astype(np.float32)[None] * inv[:, None]
    ang = np.concatenate([row, row, col, col], axis=0)
    rot = np.stack([eye, turn, np.cos(ang), np.sin(ang)]).astype(np.float32)
    mask = np.zeros((2, P, 2, T), np.float32)
    i, j = np.arange(P)[:, None], np.arange(P)[None, :]
    mask[0, :, 0, P:2 * P] = np.where(j <= i, 0.0, NEG)
    mask[0, :, 1, 0:P] = np.where(j >= i, 0.0, NEG)
    first = np.clip(columns % GRID_W - NB_KW // 2, 0, GRID_W - NB_KW)[:, None]
    key = np.arange(LAT)[None, :] % GRID_W
    mask[1, :, :, 0:LAT] = np.where((key >= first) & (key < first + NB_KW), 0.0, NEG)[:, None]
    return rot, mask


def kernel(**inputs):
    import concourse.bacc as _bacc
    from concourse.bass_utils import run_bass_kernel_spmd as _run

    nc = _bacc.Bacc("TRN2", target_bir_lowering=False, num_devices=1, dynamic_dma_scratch_size=64)
    arrays, args = {}, []
    given = {name: inputs[name] for name in _INS}
    given["const_rot"], given["const_mask"] = constants()
    for name, a in given.items():
        a = np.ascontiguousarray(a)
        arrays[f"in_{name}_dram"] = a
        args.append(nc.dram_tensor(f"in_{name}_dram", a.shape, mybir.dt.from_np(a.dtype),
                                   kind="ExternalInput").ap())
    for i, shape in enumerate(_OUTS):
        args.append(nc.dram_tensor(f"out_{i}_dram", shape, F32, kind="ExternalOutput").ap())
    hybrid_trunk(nc, *args)
    r = _run(nc, [arrays], core_ids=[0])
    return tuple(r.results[0][f"out_{i}_dram"] for i in range(len(_OUTS)))
```
